# Optimizing a Trainium2 kernel written in Bass

```python
import jax
import jax.numpy as jnp
from jax import lax
import numpy as np

D_MODEL = 2048
BATCH = 1
SEQ = 512
DEPTH = 1
DEC_BATCH = 8
DEC_SEQ = 8
PAST_LEN = 4096
PAGE_SIZE = 128

CONV_CH = D_MODEL // 2
CONV_WIDTH = 31
GLA_HEADS = 4
GLA_DK = D_MODEL // 2 // GLA_HEADS
GLA_DV = D_MODEL // GLA_HEADS
GLA_KEY = GLA_HEADS * GLA_DK
GLA_VAL = GLA_HEADS * GLA_DV
GATE_RANK = 16
GATE_TEMP = 16.0
GLA_CHUNK = 64
PEER_HEADS = 8
PEER_NKEYS = 128
PEER_EXPERTS = PEER_NKEYS * PEER_NKEYS
PEER_QDIM = 256
PEER_TOPK = 16
PEER_BLOCK = 256
EPS = 1e-6

PROJ_SPLITS = (2 * CONV_CH, GLA_KEY, GLA_KEY, GLA_VAL, GLA_VAL, GATE_RANK, D_MODEL, D_MODEL)
PROJ_COLS = sum(PROJ_SPLITS)

kernel_name = 'conv_gla_gated_peer_step'

def _split_cols(z):
    idx = [int(i) for i in np.cumsum(PROJ_SPLITS)[:-1]]
    return jnp.split(z, idx, axis=-1)

def _rmsnorm(x, g):
    xf = x.astype(jnp.float32)
    y = xf * lax.rsqrt(jnp.mean(xf * xf, axis=-1, keepdims=True) + EPS)
    return (y * g.astype(jnp.float32)).astype(x.dtype)

def _layernorm(x, g, b):
    xf = x.astype(jnp.float32)
    mu = jnp.mean(xf, axis=-1, keepdims=True)
    var = jnp.mean(jnp.square(xf - mu), axis=-1, keepdims=True)
    y = (xf - mu) * lax.rsqrt(var + EPS)
    return (y * g.astype(jnp.float32) + b.astype(jnp.float32)).astype(x.dtype)

def _conv_branch(zc, conv_state, w_dw, b_dw, ln_g, ln_b, w_conv_out):
    a, gate = jnp.split(zc, 2, axis=-1)
    u = a * jax.nn.sigmoid(gate)
    ext = jnp.concatenate([conv_state.astype(u.dtype), u], axis=1)
    c = lax.conv_general_dilated(ext, w_dw[:, None, :].astype(u.dtype), window_strides=(1,), padding='VALID', dimension_numbers=('NWC', 'WIO', 'NWC'), feature_group_count=CONV_CH) + b_dw
    c = jax.nn.silu(_layernorm(c, ln_g, ln_b))
    return c @ w_conv_out, ext[:, ext.shape[1] - (CONV_WIDTH - 1):, :]

def _gla_recurrence(q, k, v, lg, s0):
    bsz, seq = q.shape[0], q.shape[1]
    blk = min(GLA_CHUNK, seq)
    n_blk = -(-seq // blk)
    seq_p = n_blk * blk

    def to_blocks(t):
        t = jnp.pad(t.astype(jnp.float32), ((0, 0), (0, seq_p - seq), (0, 0), (0, 0)))
        return t.reshape(bsz, n_blk, blk, t.shape[2], t.shape[3]).transpose(1, 0, 3, 2, 4)

    causal = jnp.tril(jnp.ones((blk, blk), dtype=bool))[:, :, None]

    def step(s, inp):
        qc, kc, vc, lc = inp
        b = jnp.cumsum(lc, axis=2)
        o_inter = jnp.einsum('bhtd,bhde->bhte', qc * jnp.exp(b), s)
        diff = b[:, :, :, None, :] - b[:, :, None, :, :]
        decay = jnp.exp(jnp.where(causal, diff, -jnp.inf))
        att = jnp.einsum('bhtd,bhsd,bhtsd->bhts', qc, kc, decay)
        o = o_inter + jnp.einsum('bhts,bhse->bhte', att, vc)
        b_last = b[:, :, -1:, :]
        s_new = jnp.exp(b_last[:, :, 0, :])[..., None] * s + jnp.einsum('bhsd,bhse->bhde', kc * jnp.exp(b_last - b), vc)
        return s_new, o

    s_fin, o = lax.scan(step, s0.astype(jnp.float32), (to_blocks(q), to_blocks(k), to_blocks(v), to_blocks(lg)))
    o = o.transpose(1, 0, 3, 2, 4).reshape(bsz, seq_p, GLA_HEADS, GLA_DV)[:, :seq]
    return o, s_fin

def _peer(h, wq, k1, k2, u_tab, v_tab):
    bsz, seq, dm = h.shape
    t = bsz * seq
    hf = h.reshape(t, dm)
    q = (hf @ wq).astype(jnp.float32).reshape(t, PEER_HEADS, 2, PEER_QDIM // 2)
    s1 = jnp.einsum('thd,nd->thn', q[:, :, 0], k1.astype(jnp.float32))
    s2 = jnp.einsum('thd,nd->thn', q[:, :, 1], k2.astype(jnp.float32))
    v1, i1 = lax.top_k(s1, PEER_TOPK)
    v2, i2 = lax.top_k(s2, PEER_TOPK)
    cand = (v1[..., :, None] + v2[..., None, :]).reshape(t, PEER_HEADS, PEER_TOPK * PEER_TOPK)
    cs, ci = lax.top_k(cand, PEER_TOPK)
    e = jnp.take_along_axis(i1, ci // PEER_TOPK, axis=-1) * PEER_NKEYS + jnp.take_along_axis(i2, ci % PEER_TOPK, axis=-1)
    g = jax.nn.softmax(cs, axis=-1)
    e = e.reshape(t, PEER_HEADS * PEER_TOPK)
    g = g.reshape(t, PEER_HEADS * PEER_TOPK).astype(h.dtype)
    blk = min(PEER_BLOCK, t)
    n_blk = -(-t // blk)
    pad = n_blk * blk - t
    hp = jnp.pad(hf, ((0, pad), (0, 0))).reshape(n_blk, blk, dm)
    ep = jnp.pad(e, ((0, pad), (0, 0))).reshape(n_blk, blk, PEER_HEADS * PEER_TOPK)
    gp = jnp.pad(g, ((0, pad), (0, 0))).reshape(n_blk, blk, PEER_HEADS * PEER_TOPK)

    def block(args):
        hb, eb, gb = args
        act = jax.nn.gelu(jnp.einsum('tkd,td->tk', u_tab[eb], hb))
        return jnp.einsum('tk,tkd->td', gb * act, v_tab[eb])

    out = lax.map(block, (hp, ep, gp)).reshape(n_blk * blk, dm)[:t]
    return out.reshape(bsz, seq, dm)

def _layer(x, conv_state, gla_state, norm1_g, w_in, w_a2, b_a, w_dw, b_dw, conv_ln_g, conv_ln_b, w_conv_out, gla_norm_g, w_gla_o, w_mix_out, norm2_g, peer_wq, peer_k1, peer_k2, peer_u, peer_v):
    bsz, seq = x.shape[0], x.shape[1]
    h = _rmsnorm(x, norm1_g)
    zc, zq, zk, zv, zr, za, zga, zgb = _split_cols(h @ w_in)
    a_out, conv_new = _conv_branch(zc, conv_state, w_dw, b_dw, conv_ln_g, conv_ln_b, w_conv_out)
    q = zq.reshape(bsz, seq, GLA_HEADS, GLA_DK) * (GLA_DK ** -0.5)
    k = zk.reshape(bsz, seq, GLA_HEADS, GLA_DK)
    v = zv.reshape(bsz, seq, GLA_HEADS, GLA_DV)
    lg = (jax.nn.log_sigmoid((za @ w_a2 + b_a).astype(jnp.float32)) / GATE_TEMP).reshape(bsz, seq, GLA_HEADS, GLA_DK)
    o, gla_new = _gla_recurrence(q, k, v, lg, gla_state)
    o = o * lax.rsqrt(jnp.mean(o * o, axis=-1, keepdims=True) + EPS)
    o = (o.reshape(bsz, seq, GLA_VAL) * gla_norm_g.astype(jnp.float32)).astype(x.dtype) * jax.nn.silu(zr)
    b_out = o @ w_gla_o
    merged = jax.nn.sigmoid(zga) * a_out + jax.nn.sigmoid(zgb) * b_out
    x = x + merged @ w_mix_out
    x = x + _peer(_rmsnorm(x, norm2_g), peer_wq, peer_k1, peer_k2, peer_u, peer_v)
    return x, conv_new, gla_new

def setup_inputs(seed: int = 0) -> dict:
    key = jax.random.key(seed)
    ks = jax.random.split(key, 23)

    def nrm(k, shape, scale):
        return jax.random.normal(k, shape, jnp.float32) * scale

    return {
        'x_prompt': nrm(ks[0], (BATCH, SEQ, D_MODEL), 1.0),
        'x_sample': nrm(ks[1], (DEC_BATCH, DEC_SEQ, D_MODEL), 1.0),
        'state_conv': nrm(ks[2], (DEPTH, DEC_BATCH, CONV_WIDTH - 1, CONV_CH), 0.5),
        'state_gla': nrm(ks[3], (DEPTH, DEC_BATCH, GLA_HEADS, GLA_DK, GLA_DV), 0.1),
        'norm1_g': 1.0 + nrm(ks[4], (DEPTH, D_MODEL), 0.02),
        'w_in': nrm(ks[5], (DEPTH, D_MODEL, PROJ_COLS), D_MODEL ** -0.5),
        'w_a2': nrm(ks[6], (DEPTH, GATE_RANK, GLA_KEY), GATE_RANK ** -0.5),
        'b_a': nrm(ks[7], (DEPTH, GLA_KEY), 0.01),
        'w_dw': nrm(ks[8], (DEPTH, CONV_WIDTH, CONV_CH), CONV_WIDTH ** -0.5),
        'b_dw': nrm(ks[9], (DEPTH, CONV_CH), 0.01),
        'conv_ln_g': 1.0 + nrm(ks[10], (DEPTH, CONV_CH), 0.02),
        'conv_ln_b': nrm(ks[11], (DEPTH, CONV_CH), 0.01),
        'w_conv_out': nrm(ks[12], (DEPTH, CONV_CH, D_MODEL), CONV_CH ** -0.5),
        'gla_norm_g': 1.0 + nrm(ks[13], (DEPTH, GLA_VAL), 0.02),
        'w_gla_o': nrm(ks[14], (DEPTH, GLA_VAL, D_MODEL), GLA_VAL ** -0.5),
        'w_mix_out': nrm(ks[15], (DEPTH, D_MODEL, D_MODEL), D_MODEL ** -0.5),
        'norm2_g': 1.0 + nrm(ks[16], (DEPTH, D_MODEL), 0.02),
        'peer_wq': nrm(ks[17], (DEPTH, D_MODEL, PEER_HEADS * PEER_QDIM), D_MODEL ** -0.5),
        'peer_k1': nrm(ks[18], (DEPTH, PEER_NKEYS, PEER_QDIM // 2), (PEER_QDIM // 2) ** -0.5),
        'peer_k2': nrm(ks[19], (DEPTH, PEER_NKEYS, PEER_QDIM // 2), (PEER_QDIM // 2) ** -0.5),
        'peer_u': nrm(ks[20], (DEPTH, PEER_EXPERTS, D_MODEL), D_MODEL ** -0.5),
        'peer_v': nrm(ks[21], (DEPTH, PEER_EXPERTS, D_MODEL), 0.5),
        'final_g': 1.0 + nrm(ks[22], (D_MODEL,), 0.02),
    }

def reference(x_prompt, x_sample, state_conv, state_gla, norm1_g, w_in, w_a2, b_a, w_dw, b_dw, conv_ln_g, conv_ln_b, w_conv_out, gla_norm_g, w_gla_o, w_mix_out, norm2_g, peer_wq, peer_k1, peer_k2, peer_u, peer_v, final_g):
    xp = x_prompt
    xs = x_sample
    nb = x_prompt.shape[0]
    conv_p, gla_p, conv_s, gla_s = [], [], [], []
    for l in range(DEPTH):
        params = (norm1_g[l], w_in[l], w_a2[l], b_a[l], w_dw[l], b_dw[l], conv_ln_g[l], conv_ln_b[l], w_conv_out[l], gla_norm_g[l], w_gla_o[l], w_mix_out[l], norm2_g[l], peer_wq[l], peer_k1[l], peer_k2[l], peer_u[l], peer_v[l])
        zero_conv = jnp.zeros((nb, CONV_WIDTH - 1, CONV_CH), x_prompt.dtype)
        zero_gla = jnp.zeros((nb, GLA_HEADS, GLA_DK, GLA_DV), jnp.float32)
        xp, cp, sp = _layer(xp, zero_conv, zero_gla, *params)
        xs, cs, ss = _layer(xs, state_conv[l], state_gla[l], *params)
        conv_p.append(cp.astype(state_conv.dtype))
        gla_p.append(sp.astype(state_gla.dtype))
        conv_s.append(cs.astype(state_conv.dtype))
        gla_s.append(ss.astype(state_gla.dtype))
    y_prompt = _rmsnorm(xp, final_g)
    y_sample = _rmsnorm(xs, final_g)
    return (y_prompt, y_sample, jnp.stack(conv_p), jnp.stack(gla_p), jnp.stack(conv_s), jnp.stack(gla_s))


_drawn_inputs = setup_inputs


def setup_inputs(seed=0):
    import zlib

    import numpy as np

    out = dict(_drawn_inputs(seed))
    spreads = {}
    factors = {'b_a': 5.567, 'b_dw': 2.856, 'conv_ln_b': 3.7, 'gla_norm_g': 2.69, 'final_g': 2.821}
    for name, (base, spread) in spreads.items():
        noise = np.random.default_rng([zlib.crc32(name.encode()), seed]).standard_normal(out[name].shape)
        drawn = base * np.exp(spread * noise) if base else spread * noise
        out[name] = jnp.asarray(drawn.astype(out[name].dtype))
    for name, factor in factors.items():
        out[name] = (out[name] * factor).astype(out[name].dtype)
    return out
```

```python
from contextlib import ExitStack

import numpy as np
import concourse.bass as bass
from concourse import mybir

F32 = mybir.dt.float32
I32 = mybir.dt.int32
U32 = mybir.dt.uint32
ACT = mybir.ActivationFunctionType
ALU = mybir.AluOpType
AX = mybir.AxisListType

P = 128
D = 2048
SEQ, DEC_B, DEC_S = 512, 8, 8
NS = DEC_B * DEC_S
TOK = SEQ + NS
HALF = TOK // 2
KT = D // P
NT = SEQ // P
TT = NT + 1
CONV = 1024
CT = CONV // P
TAPS = 31
HIST = TAPS - 1
HEADS, DK, DV = 4, 256, 512
RANK = 16
PAIR = 256
EPS = 1e-6
PH, NKEY, TOPK, NEXP = 8, 128, 16, 16384
COL_A, COL_G, COL_Q, COL_K, COL_V, COL_R, COL_Z = 0, 1024, 2048, 3072, 4096, 6144, 8192
COL_GA, COL_GB = COL_Z + RANK, COL_Z + RANK + D
LEVELS = [64, 32, 16, 8, 4, 2, 1]
NL = len(LEVELS)
RING = 4
UNITS = 2 * NT + 1
ROWS = UNITS * 2 * TOPK
NEG = -3.0e38

USE_X = 0
USE_HIST = 5
USE_CONV = 6
USE_TAIL = 14
USE_MEAN1, USE_VAR0 = 15, 16
USE_ZA1 = 16
USE_HEAD, PER_HEAD = 17, 15
USE_GATE = USE_HEAD + HEADS * PER_HEAD
USE_MIX = USE_GATE + 32
USE_H2 = USE_MIX + 8
USE_WQ = USE_H2 + TT
N_HEAD, N_GATE, N_MIX, N_WQ = 8, 32, 64, 72


eng_passed = {}


def wait(eng, sem, value):
    eng.wait_ge(sem, value)
    if not isinstance(value, int):
        eng.sem_inc(eng_passed[eng.engine], 1)


class Chain:

    def __init__(self, eng, sem):
        self.eng, self.sem, self.base, self.n = eng, sem, 0, 0

    def mark(self, ins):
        self.n += 1
        ins.then_inc(self.sem, 1)

    def wait(self, back=0):
        wait(self.eng, self.sem, self.base + self.n - back)

    def __call__(self, ins):
        self.mark(ins)
        self.wait()

    def enter(self, i, per_trip):
        self.start, self.per, self.base, self.n = self.base + self.n, per_trip, self.base + self.n + i * per_trip, 0

    def leave(self, trips):
        assert self.n == self.per, self.n
        self.base, self.n = self.start + self.per * trips, 0


def trunk(nc, a, o):
    eng_passed.clear()
    ctx = ExitStack()
    with ctx:
        def sb(name, shape, dt=F32):
            return ctx.enter_context(nc.sbuf_tensor(name, shape, dt))

        def sem(name):
            return ctx.enter_context(nc.semaphore(name))

        normT = sb("normT", [P, KT, TOK])
        wring = sb("wring", [P, 2, KT, PAIR])
        regB = sb("regB", [P, TT * D])
        glaT = regB[:, 0:KT * TOK].rearrange("p (k t) -> p k t", k=KT)
        resid = regB[:, :].rearrange("p (t d) -> p t d", t=TT)
        ident = sb("ident", [P, P])
        ones = sb("ones", [P, P])
        tri = sb("tri", [P, P])
        tri8 = sb("tri8", [NS, NS])
        bmask = sb("bmask", [NS, DEC_B])
        g1 = sb("g1", [P, KT])
        gln = sb("gln", [P, CT])
        bln = sb("bln", [P, CT])
        bdw = sb("bdw", [P, CT])
        ggla = sb("ggla", [P, KT])
        small = sb("small", [P, 3 * TT])
        zaT = sb("zaT", [RANK + 1, TT * P])
        wa2 = sb("wa2", [RANK + 1, HEADS * DK])
        i12 = sb("i12", [P, 2, 16], U32)
        ci = sb("ci", [P, 16], U32)
        abi = sb("abi", [P, 2, 16], U32)
        idx = sb("idx", [P, 3, 16], I32)
        iota16 = sb("iota16", [P, 16])
        ARENA = nc.sbuf_bytes_remaining // 4 - 8
        arena = sb("arena", [P, ARENA])
        print("arena", ARENA)

        def layout(*parts):
            out, at = [], 0
            for shape in parts:
                n = int(np.prod(shape))
                v = arena[:, at:at + n]
                if len(shape) == 2:
                    v = v.rearrange("p (a b) -> p a b", a=shape[0])
                elif len(shape) == 3:
                    v = v.rearrange("p (a b c) -> p a b c", a=shape[0], b=shape[1])
                out.append(v)
                at += n
            assert at <= ARENA, (at, ARENA)
            return out

        (x_in,) = layout((TT, D))
        EXT = HIST + SEQ + DEC_B * (HIST + DEC_S)
        conv, hist, uext, gate_s, acc, sq_ln, mean_s, wdw, wcur, wza, tails = layout(
            (CT, TOK), (CT, HIST * 9), (2, EXT), (2, TOK), (2, TOK), (CT, TOK), (TOK,), (CT, TAPS), (2, TAPS),
            (KT, RANK), (3, CONV))
        (qT, kT, lg, bT, vt, qf, kf, earg, mask, att, state, sring, qe, kdec, kd, kdm, dec, rs, rms) = layout(
            (2, TOK), (2, TOK), (TT, DK), (2, TOK), (TT, DV), (NL, 2, P), (NL, 2, P), (2 * NL, 2, P // 2),
            (NL + 1, P), (P,), (2, DV), (4, 2, DV), (2, P), (2, P), (DK,), (2, DK), (2, DEC_B), (4, TOK), (TOK,))
        masked = earg.rearrange("p a b c -> p (a b c)")[:, 0:(NL + 1) * P].rearrange("p (l t) -> p l t", l=NL + 1)
        sq = vt.rearrange("p t e -> p (t e)")[:, 0:4 * TOK].rearrange("p (e t) -> p e t", e=4)
        merged, convg, gsigB, gsigA, part = layout((KT, TOK), (CT, TOK), (2, TOK), (2, TOK), (2, TOK))
        (h2, ring, qp, sc2, cand, cand2, oh, v12, i12f, cs, ab, esel, gexp, gsum, hidden, gelu_t, wexp, ktab, kkT) = layout(
            (TT, D), (RING, D), (2, 2, TOK), (2, NKEY), (TOPK, TOPK), (TOPK * TOPK,), (TOPK, TOPK), (2, TOPK),
            (2, TOPK), (TOPK + 1,), (2, TOPK), (2, TOPK), (3, TOPK), (3,), (TOPK,), (TOPK,), (TOPK,), (2, P), (2, P))

        ps = ctx.enter_context(nc.psum_tensor("ps", [P, 2, 2, 512], F32))
        pm = ctx.enter_context(nc.psum_tensor("pm", [P, 4, 512], F32))
        conv_dram = nc.dram_tensor("conv_spill", [P, CT * TOK], F32, kind="Internal").ap()

        def flat(s):
            return ps[:, s, :, :].rearrange("p b n -> p (b n)")

        def halves(s):
            return ps[:, s, :, 0:HALF]

        def th(ap):
            return ap.rearrange("p (b n) -> p b n", b=2)

        def head(h):
            return USE_HEAD + PER_HEAD * h

        def span(c):
            return slice(c * P, c * P + (P if c < NT else NS))

        def levels(c):
            return [(l, w) for l, w in enumerate(LEVELS) if c < NT or w < DEC_S]

        for e in (nc.sync, nc.gpsimd, nc.tensor, nc.scalar, nc.vector):
            eng_passed[e.engine] = sem(f"waits_passed_{len(eng_passed)}")
        w_loaded = [sem("w_loaded0"), sem("w_loaded1")]
        ps_ready = [sem("ps_ready0"), sem("ps_ready1")]
        ps_free = [sem("ps_free0"), sem("ps_free1")]
        const_loaded = sem("const_loaded")
        x_loaded = [sem(f"x_loaded{t}") for t in range(TT)]
        g1_loaded = sem("g1_loaded")
        hist_loaded = sem("hist_loaded")
        consts_made = sem("consts_made")
        act_step, dve_step, pool_step = sem("act_step"), sem("dve_step"), sem("pool_step")
        ss_ready, rms_ready, x_normed = sem("ss_ready"), sem("rms_ready"), sem("x_normed")
        normT_ready = sem("normT_ready")
        hist_zeroed, hist_ready, uext_hist, u_ready, tails_kept = sem("hist_zeroed"), sem("hist_ready"), sem("uext_hist"), sem("u_ready"), sem("tails_kept")
        gate_ready, gate_used = sem("gate_ready"), sem("gate_used")
        wcur_ready, conv_done, conv_kept = sem("wcur_ready"), sem("conv_done"), sem("conv_kept")
        tail_ready, tail_stored = sem("tail_ready"), sem("tail_stored")
        mean_ready, centered, sqln_ready, sd_ready, lned, affined, tanhed, silu_ready = (
            sem("mean_ready"), sem("centered"), sem("sqln_ready"), sem("sd_ready"), sem("lned"), sem("affined"),
            sem("tanhed"), sem("silu_ready"))
        spilled, reloaded = sem("spilled"), sem("reloaded")
        za_ready = sem("za_ready")
        wa2_loaded = sem("wa2_loaded")
        stores_done = sem("stores_done")
        za_ready2 = sem("za_ready2")
        masks_made = sem("masks_made")
        lgabs_ready, lg_ready, k_ready, q_ready, b_ready, v_ready = (
            sem("lgabs_ready"), sem("lg_ready"), sem("k_ready"), sem("q_ready"), sem("b_ready"), sem("v_ready"))
        earg_ready, exp_ready, kdarg_ready, decay_ready = (
            sem("earg_ready"), sem("exp_ready"), sem("kdarg_ready"), sem("decay_ready"))
        factors_ready, scores_ready, att_ready, o_ready, o_kept = (
            sem("factors_ready"), sem("scores_ready"), sem("att_ready"), sem("o_ready"), sem("o_kept"))
        kdT_ready, kd_ready, kdm_ready = sem("kdT_ready"), sem("kd_ready"), sem("kdm_ready")
        rtanh_ready, rsilu_ready = sem("rtanh_ready"), sem("rsilu_ready")
        state_ready, state_stored = sem("state_ready"), sem("state_stored")
        st_updated = sem("st_updated")
        st_loaded = [sem(f"st_loaded{k}") for k in range(4)]
        st_stored = [sem(f"st_stored{k}") for k in range(4)]
        gateB_ready, gateA_ready, mergedB_ready, part_ready, merged_ready = (
            sem("gateB_ready"), sem("gateA_ready"), sem("mergedB_ready"), sem("part_ready"), sem("merged_ready"))
        conv_back, resid_loaded, g2_loaded, resid_ready = (
            sem("conv_back"), sem("resid_loaded"), sem("g2_loaded"), sem("resid_ready"))
        ktab_loaded, kkT_ready, kk_ready = sem("ktab_loaded"), sem("kkT_ready"), sem("kk_ready")
        ss2_done, ms2_ready, rms2_ready, h2_ready, h2T_ready, h2_doubled = (
            sem("ss2_done"), sem("ms2_ready"), sem("rms2_ready"), sem("h2_ready"), sem("h2T_ready"), sem("h2_doubled"))
        qp_ready, keyscores_ready, routed, negmax_ready, softmax_ready, cs_free = (
            sem("qp_ready"), sem("keyscores_ready"), sem("routed"), sem("negmax_ready"), sem("softmax_ready"),
            sem("cs_free"))
        rows_used, gelu_arg, gelu_tanh, hidden_ready = (
            sem("rows_used"), sem("gelu_arg"), sem("gelu_tanh"), sem("hidden_ready"))
        rows_loaded = [sem(f"rows_loaded{k}") for k in range(RING)]
        fold_loaded, fg_loaded, peer_done, folded, ss3_done, ms3_ready, rms3_ready, y_ready, y_stored = (
            sem("fold_loaded"), sem("fg_loaded"), sem("peer_done"), sem("folded"), sem("ss3_done"), sem("ms3_ready"),
            sem("rms3_ready"), sem("y_ready"), sem("y_stored"))
        osq_ready, rms_done, gla_ready = sem("osq_ready"), sem("rms_done"), sem("gla_ready")

        block = ctx.enter_context(nc.Block())
        w_in = a["w_in"][0]

        @block.sync
        def _(sp):
            def load(slot, w, rows, col):
                k = rows // P
                sp.dma_start(wring[:, slot, 0:k, :],
                             w[:, bass.ds(col, PAIR)].rearrange("(k p) c -> p k c", p=P)).then_inc(w_loaded[slot], 16)

            for t in range(NT):
                sp.dma_start(x_in[:, t, :], a["x_prompt"][0, t * P:(t + 1) * P, :]).then_inc(x_loaded[t], 16)
            sp.dma_start(x_in[0:NS, NT, :], a["x_sample"].rearrange("b s d -> (b s) d")).then_inc(x_loaded[NT], 16)
            sp.dma_start(g1[:, :], a["norm1_g"].rearrange("o (k p) -> p (o k)", p=P),
                         allow_slow_non_contiguous=True).then_inc(g1_loaded, 16)
            load(0, w_in, D, COL_G)
            load(1, w_in, D, COL_A)
            with sp.Fori(1, CT // 2) as i:
                wait(sp, ps_ready[1], USE_CONV + 2 * i - 1)
                load(0, w_in, D, COL_G + i * PAIR)
                wait(sp, ps_ready[1], USE_CONV + 2 * i)
                load(1, w_in, D, COL_A + i * PAIR)

            wait(sp, ps_ready[1], USE_CONV + CT - 1)
            load(0, w_in, D, COL_K)
            wait(sp, ps_ready[1], USE_CONV + CT)
            load(1, w_in, D, COL_Q)
            sp.dma_start(wa2[0:RANK, :], a["w_a2"][0, :, :]).then_inc(wa2_loaded, 16)
            sp.dma_start(wa2[RANK:RANK + 1, :], a["b_a"]).then_inc(wa2_loaded, 16)
            for k in range(3):
                wait(sp, tail_ready, k + 1)
                if k == 0:
                    sp.dma_start(o[2][0, 0, :, :], tails[0:HIST, 0, :]).then_inc(tail_stored, 16)
                else:
                    sp.dma_start(o[4][0, 4 * (k - 1):4 * k, :, :].rearrange("b t c -> (b t) c"),
                                 tails[0:4 * HIST, k, :]).then_inc(tail_stored, 16)
            wait(sp, silu_ready, 1)
            sp.dma_start(conv_dram, conv[:, :, :].rearrange("p c t -> p (c t)")).then_inc(spilled, 16)
            wait(sp, tail_stored, 48)
            wait(sp, spilled, 16)

            def head_loads(h):
                u = head(h)
                wait(sp, ps_ready[1], u + 2)
                load(0, w_in, D, COL_V + h * DV)
                wait(sp, ps_ready[1], u + 3)
                load(1, w_in, D, COL_V + h * DV + PAIR)
                wait(sp, ps_ready[1], u + 5)
                load(0, w_in, D, COL_R + h * DV)
                wait(sp, ps_ready[1], u + 6)
                load(1, w_in, D, COL_R + h * DV + PAIR)

            with sp.Fori(0, HEADS - 1) as h:
                head_loads(h)
                wait(sp, ps_ready[0], head(h) + 8)
                load(0, w_in, D, COL_K + h * DK + DK)
                wait(sp, ps_ready[0], head(h) + 10)
                load(1, w_in, D, COL_Q + h * DK + DK)
            head_loads(HEADS - 1)
            wait(sp, ps_ready[0], head(HEADS - 1) + 8)
            load(0, w_in, D, COL_GB)
            wait(sp, ps_ready[0], head(HEADS - 1) + 10)
            load(1, a["w_gla_o"][0], D, 0)

            def gate_loads(i):
                wait(sp, ps_ready[1], USE_GATE + 4 * i + 1)
                load(0, w_in, D, COL_GA + i * PAIR)
                wait(sp, ps_ready[1], USE_GATE + 4 * i + 2)
                load(1, a["w_conv_out"][0], CONV, i * PAIR)

            with sp.Fori(0, D // PAIR - 1) as i:
                gate_loads(i)
                wait(sp, ps_ready[1], USE_GATE + 4 * i + 3)
                load(0, w_in, D, COL_GB + i * PAIR + PAIR)
                wait(sp, ps_ready[1], USE_GATE + 4 * i + 4)
                load(1, a["w_gla_o"][0], D, i * PAIR + PAIR)
            gate_loads(D // PAIR - 1)
            wait(sp, ps_ready[1], USE_MIX - 1)
            load(0, a["w_mix_out"][0], D, 0)
            wait(sp, ps_ready[1], USE_MIX)
            load(1, a["w_mix_out"][0], D, PAIR)
            with sp.Fori(1, D // PAIR // 2) as i:
                for slot in range(2):
                    wait(sp, ps_ready[1], USE_MIX + 2 * i - 1 + slot)
                    load(slot, a["w_mix_out"][0], D, (2 * i + slot) * PAIR)
            for slot in range(2):
                wait(sp, ps_ready[1], USE_H2 - 1 + slot)
                load(slot, a["peer_wq"][0], D, slot * (PH // 2) * PAIR)
            with sp.Fori(1, PH // 2) as i:
                for slot in range(2):
                    wait(sp, ps_ready[1], USE_WQ + 2 * i - 1 + slot)
                    load(slot, a["peer_wq"][0], D, i * PAIR + slot * (PH // 2) * PAIR)
            for t in range(TT):
                n = P if t < NT else NS
                wait(sp, y_ready, t + 1)
                sp.dma_start(o[0][0, span(t), :] if t < NT else o[1].rearrange("b s d -> (b s) d"),
                             resid[0:n, t, :]).then_inc(y_stored, 16)
            wait(sp, y_stored, 16 * TT)

        @block.gpsimd
        def _(pool):
            step = Chain(pool, pool_step)
            for first in (tails_kept, stores_done):
                pool.sem_inc(first, 1)
            step(pool.memset(ident[:, :], 0.0))
            step(pool.affine_select(out=ident[:, :], in_=ident[:, :], compare_op=ALU.not_equal, fill=1.0, base=0,
                                    pattern=[[-1, P]], channel_multiplier=1))
            step(pool.memset(tri[:, :], 1.0 / 16.0))
            step(pool.affine_select(out=tri[:, :], in_=tri[:, :], compare_op=ALU.is_ge, fill=0.0, base=0,
                                    pattern=[[1, P]], channel_multiplier=-1))
            t8 = tri8[:, :].rearrange("p (b t) -> p b t", b=DEC_B)
            step(pool.tensor_copy(tri8[:, :], tri[0:NS, 0:NS]))
            step(pool.affine_select(out=t8, in_=t8, compare_op=ALU.is_ge, fill=0.0, base=0,
                                    pattern=[[-DEC_S, DEC_B], [0, DEC_S]], channel_multiplier=1))
            step(pool.memset(bmask[:, :], 1.0))
            step(pool.affine_select(out=bmask[:, :], in_=bmask[:, :], compare_op=ALU.is_ge, fill=0.0, base=0,
                                    pattern=[[-DEC_S, DEC_B]], channel_multiplier=1))
            step(pool.affine_select(out=bmask[:, :], in_=bmask[:, :], compare_op=ALU.is_ge, fill=0.0, base=DEC_S - 1,
                                    pattern=[[DEC_S, DEC_B]], channel_multiplier=-1))
            step(pool.iota(iota16[:, :], pattern=[[1, 16]], base=0, channel_multiplier=0,
                           allow_small_or_imprecise_dtypes=True))
            pool.memset(zaT[:, :], 1.0).then_inc(consts_made, 1)
            pool.memset(ones[:, :], 1.0).then_inc(consts_made, 1)
            wait(pool, normT_ready, 2 * TT)
            pool.dma_start(gln[:, :], a["conv_ln_g"].rearrange("o (k p) -> p (o k)", p=P),
                           allow_slow_non_contiguous=True).then_inc(const_loaded, 16)
            pool.dma_start(bln[:, :], a["conv_ln_b"].rearrange("o (k p) -> p (o k)", p=P),
                           allow_slow_non_contiguous=True).then_inc(const_loaded, 16)
            pool.dma_start(bdw[:, :], a["b_dw"].rearrange("o (k p) -> p (o k)", p=P),
                           allow_slow_non_contiguous=True).then_inc(const_loaded, 16)
            pool.dma_start(ggla[:, :], a["gla_norm_g"].rearrange("o (k p) -> p (o k)", p=P),
                           allow_slow_non_contiguous=True).then_inc(const_loaded, 16)
            for c in range(CT):
                pool.dma_start(wdw[:, c, :], a["w_dw"][0, :, c * P:(c + 1) * P].rearrange("j p -> p j"),
                               allow_slow_non_contiguous=True).then_inc(const_loaded, 16)
            pool.dma_start(wza[:, :, :], w_in[:, COL_Z:COL_Z + RANK].rearrange("(k p) c -> p k c", p=P)
                           ).then_inc(const_loaded, 16)
            for g in range(2):
                pool.dma_start(tails[0:4 * HIST, 1 + g, :],
                               a["state_conv"][0, 4 * g:4 * g + 4, :, :].rearrange("b t c -> (b t) c")
                               ).then_inc(hist_loaded, 16)
            pool.memset(hist[:, :, 0:HIST], 0.0).then_inc(hist_zeroed, 1)
            wait(pool, hist_zeroed, 1)
            wait(pool, hist_ready, 2)
            with pool.Fori(0, CT // 2) as i:
                wait(pool, conv_done, 4 * i + 1)
                hv = hist[:, bass.ds(2 * i, 2), :]
                uv = uext[:, :, HIST + SEQ:].rearrange("p q (b t) -> p q b t", b=DEC_B)
                pool.tensor_copy(uext[:, :, 0:HIST], hv[:, :, 0:HIST]).then_inc(uext_hist, 1)
                for q in range(2):
                    pool.tensor_copy(uv[:, q, :, 0:HIST], hv[:, q, HIST:].rearrange("p (b t) -> p b t", b=DEC_B)
                                     ).then_inc(uext_hist, 1)
                wait(pool, uext_hist, 3 * i + 3)
                wait(pool, u_ready, 6 * i + 6)
                pool.tensor_copy(hv[:, :, 0:HIST], uext[:, :, SEQ:SEQ + HIST]).then_inc(tails_kept, 1)
                for q in range(2):
                    pool.tensor_copy(hv[:, q, HIST:].rearrange("p (b t) -> p b t", b=DEC_B), uv[:, q, :, DEC_S:]
                                     ).then_inc(tails_kept, 1)
                wait(pool, tails_kept, 3 * i + 3 + 1)

            wait(pool, spilled, 16)
            wait(pool, tail_stored, 48)
            wait(pool, za_ready, 1)
            base = step.base + step.n
            n = 0
            pool.memset(mask[:, :, :], 1.0).then_inc(pool_step, 1)
            pool.memset(qf[:, :, :, :], 0.0).then_inc(pool_step, 1)
            pool.memset(kf[:, :, :, :], 0.0).then_inc(pool_step, 1)
            n = 3
            wait(pool, pool_step, base + n)
            for l, w in enumerate(LEVELS[1:], 1):
                for b, mul, st in ((0, 1, -2 * w), (2 * w - 1, -1, 2 * w)):
                    mv = mask[:, l, :].rearrange("p (g w) -> p g w", w=2 * w)
                    pool.affine_select(out=mv, in_=mv, compare_op=ALU.is_ge, fill=0.0, base=b,
                                       pattern=[[st, P // (2 * w)], [0, 2 * w]], channel_multiplier=mul
                                       ).then_inc(pool_step, 1)
                    n += 1
                    wait(pool, pool_step, base + n)
            pool.tensor_copy(mask[:, NL, :], ident[:, :]).then_inc(masks_made, 1)

            def state_load(h, b):
                pool.dma_start(sring[:, b % 4, :, :],
                               a["state_gla"][0, b, bass.ds(h, 1), :, :].rearrange("o (j p) e -> p (o j) e", p=P)
                               ).then_inc(st_loaded[b % 4], 16)

            with pool.Fori(0, HEADS) as h:
                for b in range(4):
                    state_load(h, b)
                wait(pool, state_ready, NT * h + NT)
                pool.dma_start(o[3][0, 0, bass.ds(h, 1), :, :].rearrange("o (j p) e -> p (o j) e", p=P),
                               state[:, :, :]).then_inc(state_stored, 16)
                for b in range(DEC_B):
                    wait(pool, st_updated, 2 * DEC_B * h + 2 * b + 2)
                    pool.dma_start(o[5][0, b, bass.ds(h, 1), :, :].rearrange("o (j p) e -> p (o j) e", p=P),
                                   sring[:, b % 4, :, :]).then_inc(st_stored[b % 4], 16)
                    if b < 4:
                        wait(pool, st_stored[b], 32 * h + 16)
                        state_load(h, b + 4)
                for b in range(4):
                    wait(pool, st_stored[b], 32 * h + 32)
                wait(pool, state_stored, 16 * h + 16)
                pool.sem_inc(stores_done, 1)
            wait(pool, gla_ready, 4 * HEADS)
            pool.dma_start(convg[:, :, :].rearrange("p c t -> p (c t)"), conv_dram).then_inc(conv_back, 16)
            wait(pool, ps_ready[0], USE_MIX - 2)
            wait(pool, ps_ready[1], USE_MIX - 2)
            pool.dma_start(resid[:, 0:NT, :], a["x_prompt"][0].rearrange("(t p) d -> p t d", p=P)
                           ).then_inc(resid_loaded, 16)
            pool.dma_start(resid[0:NS, NT, :], a["x_sample"].rearrange("b s d -> (b s) d")).then_inc(resid_loaded, 16)
            wait(pool, merged_ready, D // PAIR + 1)
            pool.dma_start(ring[:, 0, :], a["norm2_g"].partition_broadcast(P)).then_inc(g2_loaded, 16)
            for half, key in enumerate(("peer_k1", "peer_k2")):
                pool.dma_start(ktab[:, half, :], a[key][0, :, :]).then_inc(ktab_loaded, 16)
            wait(pool, h2_ready, TT)
            pool.dma_start(h2[NS:P, NT, :], h2[0:NS, NT, :]).then_inc(h2_doubled, 16)
            with pool.Fori(0, PH // 2) as i:
                for m in range(ROWS):
                    unit, k = m // (2 * TOPK), m % (2 * TOPK)
                    if k == 0:
                        wait(pool, routed, UNITS * i + unit + 1 + 1)
                    wait(pool, rows_used, ROWS * i + m + 1)
                    pool.indirect_dma_start(
                        ring[:, m % RING, :], None, (a["peer_u"] if k < TOPK else a["peer_v"])[0],
                        bass.IndirectOffsetOnAxis(ap=idx[:, unit % 3, k % TOPK:k % TOPK + 1], axis=0),
                        bounds_check=NEXP - 1, oob_is_err=True).then_inc(rows_loaded[m % RING], 16)
            wait(pool, peer_done, 1)
            pool.dma_start(h2[0:NS, 1, :], resid[NS:P, NT, :]).then_inc(fold_loaded, 16)
            pool.dma_start(h2[:, 0, :], a["final_g"].rearrange("(o d) -> o d", o=1).partition_broadcast(P)
                           ).then_inc(fg_loaded, 16)

        @block.tensor
        def _(pe):
            pe.sem_inc(ps_free[0], 1)
            for first in (scores_ready, keyscores_ready):
                pe.sem_inc(first, 1)
            pe.sem_inc(ps_free[1], 1)

            def transposes(s, use, src, rows, n, ready):
                wait(pe, ps_free[s], use + 1)
                for k in range(n):
                    last = pe.transpose(flat(s)[:, k * P:k * P + rows], src(k), ident[0:rows, 0:rows])
                last.then_inc(ps_ready[s], 1)

            def project(s, use, j, slot, srcT, kt=KT):
                pe.wait_ge(ps_free[s], use + 1)
                for h in range(2):
                    for k in range(kt):
                        last = pe.matmul(ps[:, s, h, 0:HALF], wring[:, slot, k, j * P:(j + 1) * P],
                                         srcT[:, k, h * HALF:(h + 1) * HALF], start=(k == 0), stop=(k == kt - 1))
                last.then_inc(ps_ready[s], 1)

            pe.wait_ge(consts_made, 2)
            pe.wait_ge(pool_step, 2)
            for t in range(TT):
                rows = P if t < NT else NS
                pe.wait_ge(x_normed, t + 1)
                for s in range(2):
                    transposes(s, USE_X + t, lambda k: x_in[0:rows, t, (8 * s + k) * P:(8 * s + k + 1) * P], rows, 8, None)
            pe.wait_ge(hist_loaded, 32)
            for g in range(2):
                transposes(g, USE_HIST, lambda k: tails[0:4 * HIST, 1 + g, k * P:(k + 1) * P], 4 * HIST, CT, None)
            pe.wait_ge(normT_ready, 2 * TT)
            with pe.Fori(0, CT // 2) as i:
                for half in range(2):
                    pe.wait_ge(w_loaded[half], 16 * i + 16)
                    for j in range(2):
                        project(j, USE_CONV + 2 * i + half, j, half, normT)
            pe.wait_ge(tails_kept, 3 * CT // 2 + 1)
            for k, (s, use, n) in enumerate([(0, USE_TAIL, HIST), (1, USE_TAIL, 4 * HIST), (0, USE_TAIL + 1, 4 * HIST)]):
                at = (0, HIST, 5 * HIST)[k]
                pe.wait_ge(ps_free[s], use + 1)
                for c in range(CT):
                    last = pe.transpose(flat(s)[0:n, c * P:(c + 1) * P], hist[:, c, at:at + n], ident[:, :])
                last.then_inc(ps_ready[s], 1)
            pe.wait_ge(conv_kept, CT + 1)
            for s, use, src, ready in ((1, USE_MEAN1, conv, None), (0, USE_VAR0, sq_ln, sqln_ready)):
                pe.wait_ge(ps_free[s], use + 1)
                if ready is not None:
                    pe.wait_ge(ready, 1)
                for h in range(2):
                    for c in range(CT):
                        last = pe.matmul(ps[:, s, h, 0:HALF], ones[:, :], src[:, c, h * HALF:(h + 1) * HALF],
                                         start=(c == 0), stop=(c == CT - 1))
                last.then_inc(ps_ready[s], 1)
            pe.wait_ge(const_loaded, 16 * 13)
            pe.wait_ge(ps_free[1], USE_ZA1 + 1)
            for h in range(2):
                for k in range(KT):
                    last = pe.matmul(ps[0:RANK, 1, h, 0:HALF], wza[:, k, :], normT[:, k, h * HALF:(h + 1) * HALF],
                                     start=(k == 0), stop=(k == KT - 1))
            last.then_inc(ps_ready[1], 1)

            def project_tok(use, slot, srcT, kt=KT):
                for s in range(2):
                    pe.wait_ge(ps_free[s], use + 1)
                    for t in (range(NT) if s == 0 else [NT]):
                        n = span(t).stop - span(t).start
                        c0 = t * PAIR if s == 0 else 0
                        for k in range(kt):
                            last = pe.matmul(flat(s)[0:n, c0:c0 + PAIR], srcT[:, k, span(t)], wring[:, slot, k, :],
                                             start=(k == 0), stop=(k == kt - 1))
                    last.then_inc(ps_ready[s], 1)

            pe.wait_ge(wa2_loaded, 32)
            pe.wait_ge(za_ready, 1)
            with pe.Fori(0, HEADS) as h:
                u = head(h)
                for s in range(2):
                    wait(pe, ps_free[s], u + 1)
                    for t in (range(NT) if s == 0 else [NT]):
                        c0 = t * DK if s == 0 else 0
                        last = pe.matmul(flat(s)[:, c0:c0 + DK], zaT[:, t * P:(t + 1) * P], wa2[:, bass.ds(h * DK, DK)],
                                         start=True, stop=True)
                    last.then_inc(ps_ready[s], 1)
                for slot in range(2):
                    pe.wait_ge(w_loaded[slot], 48 * h + 80)
                    for j in range(2):
                        project(j, u + 1 + slot, j, slot, normT)
                pe.wait_ge(lg_ready, 2 * h + 2)
                for j in range(2):
                    pe.wait_ge(ps_free[j], u + 4)
                    for t in range(TT):
                        n = span(t).stop - span(t).start
                        last = pe.matmul(flat(j)[:, span(t)], lg[0:n, t, j * P:(j + 1) * P],
                                         tri[:, :] if t < NT else tri8[:, :], start=True, stop=True)
                    last.then_inc(ps_ready[j], 1)
                for slot in range(2):
                    pe.wait_ge(w_loaded[slot], 48 * h + 96)
                    project_tok(u + 4 + slot, slot, normT)

                def kd_and_scores(c):
                    n = span(c).stop - span(c).start
                    pe.wait_ge(decay_ready, TT * h + c + 1)
                    wait(pe, kd_ready, TT * h + c + 1)
                    for j in range(2):
                        last = pe.transpose(pm[0:n, 3, j * P:(j + 1) * P], kdec[:, j, 0:n], ident[:, :])
                    last.then_inc(kdT_ready, 1)
                    pe.wait_ge(factors_ready, TT * h + c + 1 + 1)
                    pe.wait_ge(att_ready, TT * h + c + 1)
                    sc = pm[:, 0:2, :].rearrange("p b (l t) -> p (b l) t", t=P)
                    for l, _ in levels(c) + [(NL, 0)]:
                        for j in range(2):
                            kk = kf[:, l, j, 0:n] if l < NL else kT[:, j, span(c)]
                            qq = qf[:, l, j, 0:n] if l < NL else qT[:, j, span(c)]
                            last = pe.matmul(sc[0:n, l, 0:n], kk, qq, start=(j == 0), stop=(j == 1))
                    last.then_inc(scores_ready, 1)

                for c in range(NT):
                    kd_and_scores(c)
                    if c % 2 == 0:
                        pe.wait_ge(w_loaded[c // 2], 48 * h + 112)
                    project(0, u + 6 + c, c % 2, c // 2, normT)
                    pe.wait_ge(v_ready, 4 * h + 4)
                    pe.wait_ge(att_ready, TT * h + c + 1 + 1)
                    pe.wait_ge(o_kept, TT * h + c + 1)
                    if c:
                        pe.wait_ge(state_ready, NT * h + c)
                    for e in range(4):
                        for j in range(2 if c else 0):
                            pe.matmul(pm[:, 2, e * P:(e + 1) * P], state[:, j, e * P:(e + 1) * P], qe[:, j, :],
                                      start=(j == 0), stop=False)
                        last = pe.matmul(pm[:, 2, e * P:(e + 1) * P], vt[:, c, e * P:(e + 1) * P], att[:, :],
                                         start=(c == 0), stop=True)
                    last.then_inc(o_ready, 1)
                    pe.wait_ge(kd_ready, TT * h + c + 1 + 1)
                    pe.wait_ge(ps_free[1], u + 7 + c)
                    for j in range(2):
                        last = pe.matmul(ps[:, 1, j, :], kd[:, j * P:(j + 1) * P], vt[:, c, :], start=True, stop=True)
                    last.then_inc(ps_ready[1], 1)
                kd_and_scores(NT)
                pe.wait_ge(att_ready, TT * h + TT + 1)
                pe.wait_ge(o_kept, TT * h + NT + 1)
                for e in range(4):
                    pe.matmul(pm[:, 2, e * P:e * P + NS], vt[0:NS, NT, e * P:(e + 1) * P], att[0:NS, 0:NS],
                              start=(e == 0), stop=False)
                for b in range(DEC_B):
                    pe.wait_ge(st_loaded[b % 4], 32 * h + 16 * (b // 4) + 16)
                    for e in range(4):
                        for j in range(2):
                            last = pe.matmul(pm[:, 2, e * P + b * DEC_S:e * P + (b + 1) * DEC_S],
                                             sring[:, b % 4, j, e * P:(e + 1) * P],
                                             qe[:, j, b * DEC_S:(b + 1) * DEC_S], start=False,
                                             stop=(b == DEC_B - 1 and e == 3 and j == 1))
                    if b == DEC_B - 1:
                        last.then_inc(o_ready, 1)
                    pe.wait_ge(kdm_ready, DEC_B * h + b + 1)
                    pe.wait_ge(ps_free[b % 2], u + 11 + b // 2)
                    for j in range(2):
                        last = pe.matmul(ps[:, b % 2, j, :], kdm[0:NS, b % 2, j * P:(j + 1) * P], vt[0:NS, NT, :],
                                         start=True, stop=True)
                    last.then_inc(ps_ready[b % 2], 1)
                pe.wait_ge(osq_ready, h + 1)
                for s in range(2):
                    pe.wait_ge(ps_free[s], u + 15)
                    for e in range(4):
                        last = pe.matmul(ps[:, s, 0, 0:HALF], ones[:, :], sq[:, e, s * HALF:(s + 1) * HALF],
                                         start=(e == 0), stop=(e == 3))
                    last.then_inc(ps_ready[s], 1)

            pe.wait_ge(conv_back, 16)
            pe.wait_ge(gla_ready, 4 * HEADS)
            with pe.Fori(0, D // PAIR) as i:
                for n, (src, kt) in enumerate(((normT, KT), (glaT, KT), (normT, KT), (convg, CT))):
                    pe.wait_ge(w_loaded[n % 2], 32 * i + 16 * (N_GATE // 2 + n // 2 + 1))
                    for j in range(2):
                        project(j, USE_GATE + 4 * i + n, j, n % 2, src, kt)
            pe.wait_ge(merged_ready, D // PAIR + 1)
            with pe.Fori(0, D // PAIR // 2) as i:
                for slot in range(2):
                    pe.wait_ge(w_loaded[slot], 16 * i + 16 * (N_MIX // 2 + 1))
                    project_tok(USE_MIX + 2 * i + slot, slot, merged)
            pe.wait_ge(ktab_loaded, 32)
            for half in range(2):
                last = pe.transpose(pm[:, 3, half * P:(half + 1) * P], ktab[:, half, :], ident[:, :])
            last.then_inc(kkT_ready, 1)
            for t in range(TT):
                rows = P if t < NT else NS
                pe.wait_ge(h2_ready, t + 1)
                for s in range(2):
                    transposes(s, USE_H2 + t, lambda k: h2[0:rows, t, (8 * s + k) * P:(8 * s + k + 1) * P], rows, 8, None)
            pe.wait_ge(h2T_ready, 2 * TT)
            pe.wait_ge(kk_ready, 1)
            with pe.Fori(0, PH // 2) as i:
                for unit in range(UNITS):
                    if unit in (0, NT):
                        hh = unit // NT
                        pe.wait_ge(w_loaded[hh], 16 * i + 16 * (N_WQ // 2 + 1))
                        for j in range(2):
                            project(j, USE_WQ + 2 * i + hh, j, hh, normT)
                        pe.wait_ge(qp_ready, 4 * i + 2 * hh + 2)
                    pe.wait_ge(routed, UNITS * i + max(unit - 3, 0) + 1)
                    for half in range(2):
                        out = pm[:, unit % 4, half * NKEY:(half + 1) * NKEY]
                        if unit < 2 * NT:
                            last = pe.matmul(out, qp[:, unit // NT, half, span(unit % NT)], kkT[:, half, :],
                                             start=True, stop=True)
                        else:
                            for hh in range(2):
                                last = pe.matmul(out[hh * NS:(hh + 1) * NS, :], qp[:, hh, half, SEQ:TOK],
                                                 kkT[:, half, :], start=True, stop=True)
                    last.then_inc(keyscores_ready, 1)

        @block.scalar
        def _(act):
            step = Chain(act, act_step)
            for first in (conv_kept, kd_ready, o_kept, b_ready, softmax_ready):
                act.sem_inc(first, 1)
            junk = wring
            for t in range(TT):
                rows = P if t < NT else NS
                wait(act, x_loaded[t], 16)
                step(nc.scalar.activation(regB[0:rows, 0:D], x_in[0:rows, t, :], ACT.Square,
                                          accum_out=small[0:rows, t:t + 1]))
            for t in range(TT):
                rows = P if t < NT else NS
                wait(act, ss_ready, t + 1)
                nc.scalar.activation(small[0:rows, TT + t:TT + t + 1], small[0:rows, TT + t:TT + t + 1], ACT.Sqrt
                                     ).then_inc(rms_ready, 1)
            for g in range(2):
                wait(act, ps_ready[g], USE_HIST + 1)
                nc.scalar.activation(hist[:, :, HIST + 4 * HIST * g:HIST + 4 * HIST * (g + 1)],
                                     flat(g).rearrange("p (c t) -> p c t", c=CT)[:, :, 0:4 * HIST], ACT.Copy
                                     ).then_inc(hist_ready, 1)
            wait(act, hist_ready, 2)
            act.sem_inc(ps_free[0], 1)
            act.sem_inc(ps_free[1], 1)
            wait(act, const_loaded, 16 * 13)
            def gates(i):
                if not isinstance(i, int):
                    wait(act, gate_used, 6 * i)
                for j in range(2):
                    wait(act, ps_ready[j], USE_CONV + 2 * i + 1)
                    nc.scalar.activation(th(gate_s[:, j, :]), halves(j), ACT.Tanh, scale=0.5).then_inc(ps_free[j], 1)
                    wait(act, ps_free[j], USE_CONV + 2 * i + 2)
                    nc.scalar.activation(gate_s[:, j, :], gate_s[:, j, :], ACT.Copy, scale=0.5, bias=0.5
                                         ).then_inc(gate_ready, 1)

            def keep_sums(i):
                wait(act, conv_done, 4 * i + 4 + 1)
                for j in range(2):
                    nc.scalar.activation(conv[:, bass.ds(2 * i + j, 1), :], acc[:, j:j + 1, :], ACT.Identity,
                                         bias=bdw[:, bass.ds(2 * i + j, 1)]).then_inc(conv_kept, 1)

            def taps_of(i):
                nc.scalar.activation(wcur[:, :, :], wdw[:, bass.ds(2 * i, 2), :], ACT.Copy).then_inc(wcur_ready, 1)

            taps_of(0)
            gates(0)
            with act.Fori(1, CT // 2) as i:
                gates(i)
                keep_sums(i - 1)
                taps_of(i)
            keep_sums(CT // 2 - 1)
            for k, (s, use, n) in enumerate([(0, USE_TAIL, HIST), (1, USE_TAIL, 4 * HIST), (0, USE_TAIL + 1, 4 * HIST)]):
                wait(act, ps_ready[s], use + 1)
                nc.scalar.activation(tails[0:n, k, :], flat(s)[0:n, :], ACT.Copy).then_inc(tail_ready, 1)
                wait(act, tail_ready, k + 1)
                act.sem_inc(ps_free[s], 1)
            wait(act, ps_ready[1], USE_MEAN1 + 1)
            nc.scalar.activation(th(mean_s[:, :]), halves(1), ACT.Copy, scale=1.0 / CONV).then_inc(mean_ready, 1)
            wait(act, mean_ready, 1)
            act.sem_inc(ps_free[1], 1)
            wait(act, centered, 1)
            nc.scalar.activation(sq_ln[:, :, :], conv[:, :, :], ACT.Square).then_inc(sqln_ready, 1)
            wait(act, ps_ready[0], USE_VAR0 + 1)
            wait(act, sd_ready, 1)
            nc.scalar.activation(mean_s[:, :], mean_s[:, :], ACT.Sqrt).then_inc(sd_ready, 1)
            wait(act, lned, 1)
            for c in range(CT):
                nc.scalar.activation(conv[:, c, :], conv[:, c, :], ACT.Identity, scale=gln[:, c:c + 1],
                                     bias=bln[:, c:c + 1]).then_inc(affined, 1)
            wait(act, affined, CT)
            nc.scalar.activation(sq_ln[:, :, :], conv[:, :, :], ACT.Tanh, scale=0.5).then_inc(tanhed, 1)
            wait(act, ps_ready[1], USE_ZA1 + 1)
            wait(act, consts_made, 2)
            nc.scalar.activation(th(zaT[0:RANK, 0:TOK]), ps[0:RANK, 1, :, 0:HALF], ACT.Copy).then_inc(za_ready, 1)
            wait(act, za_ready, 1)
            act.sem_inc(ps_free[1], 1)

            wait(act, spilled, 16)
            wait(act, tail_stored, 48)
            total = step.base + step.n
            step.base, step.n = total, 0
            with act.Fori(0, HEADS) as h:
                step.enter(h, 2 * 2)
                u = head(h)
                parts = ((0, lg[:, 0:NT, :].rearrange("p t d -> p (t d)"), flat(0)),
                         (1, lg[0:NS, NT, :], flat(1)[0:NS, 0:DK]))
                wait(act, b_ready, 2 * h + 1)
                for s, dst, src in parts:
                    wait(act, ps_ready[s], u + 1)
                    step(nc.scalar.activation(dst, src, ACT.Abs))
                    step(nc.scalar.activation(dst, dst, ACT.Exp, scale=-1.0))
                    nc.scalar.activation(dst, dst, ACT.Ln, bias=1.0).then_inc(lgabs_ready, 1)
                wait(act, factors_ready, TT * h + 1)
                wait(act, scores_ready, TT * h + 1)
                for s in range(2):
                    wait(act, ps_ready[s], u + 2)
                    nc.scalar.activation(th(kT[:, s, :]), halves(s), ACT.Copy).then_inc(k_ready, 1)
                    wait(act, k_ready, 2 * h + s + 1)
                    act.sem_inc(ps_free[s], 1)
                for s in range(2):
                    wait(act, ps_ready[s], u + 3)
                    nc.scalar.activation(th(qT[:, s, :]), halves(s), ACT.Copy, scale=DK ** -0.5).then_inc(q_ready, 1)
                    wait(act, q_ready, 2 * h + s + 1)
                    act.sem_inc(ps_free[s], 1)
                for s in range(2):
                    wait(act, ps_ready[s], u + 4)
                    nc.scalar.activation(bT[:, s, :], flat(s)[:, 0:TOK], ACT.Copy).then_inc(b_ready, 1)
                    wait(act, b_ready, 2 * h + s + 1 + 1)
                    act.sem_inc(ps_free[s], 1)

                def decays(c):
                    wait(act, earg_ready, TT * h + c + 1)
                    nc.scalar.activation(earg[:, 0:2 * NL, :, :] if c < NT else earg[:, 8:14, :, 0:NS // 2],
                                         earg[:, 0:2 * NL, :, :] if c < NT else earg[:, 8:14, :, 0:NS // 2],
                                         ACT.Exp).then_inc(exp_ready, 1)
                    n = span(c).stop - span(c).start
                    if c:
                        wait(act, o_ready, TT * h + c)
                        wait(act, kdT_ready, TT * h + c)
                        wait(act, state_ready, NT * h + c)
                    nc.scalar.activation(qe[:, :, 0:n], bT[:, :, span(c)], ACT.Exp).then_inc(exp_ready, 1)
                    if c < NT:
                        for j in range(2):
                            e = span(c).stop
                            nc.scalar.activation(kdec[:, j, :], bT[:, j, span(c)], ACT.Exp, scale=-1.0,
                                                 bias=bT[:, j, e - 1:e]).then_inc(exp_ready, 1)
                        nc.scalar.activation(dec[:, :, 0:1], bT[:, :, span(c).stop - 1:span(c).stop], ACT.Exp
                                             ).then_inc(exp_ready, 1)
                    else:
                        wait(act, kdarg_ready, h + 1)
                        nc.scalar.activation(kdec[:, :, 0:NS], kdec[:, :, 0:NS], ACT.Exp).then_inc(exp_ready, 1)
                        nc.scalar.activation(dec[:, :, :],
                                             bT[:, :, SEQ:].rearrange("p j (b t) -> p j b t", b=DEC_B)[:, :, :, DEC_S - 1],
                                             ACT.Exp).then_inc(exp_ready, 1)

                def v_keep(p):
                    wait(act, ps_ready[0], u + 5 + p)
                    nc.scalar.activation(vt[:, 0:NT, p * PAIR:(p + 1) * PAIR],
                                         flat(0).rearrange("p (t c) -> p t c", t=NT), ACT.Copy).then_inc(v_ready, 1)
                    wait(act, v_ready, 4 * h + 2 * p + 1)
                    act.sem_inc(ps_free[0], 1)
                    wait(act, ps_ready[1], u + 5 + p)
                    nc.scalar.activation(vt[0:NS, NT, p * PAIR:(p + 1) * PAIR], flat(1)[0:NS, 0:PAIR], ACT.Copy
                                         ).then_inc(v_ready, 1)
                    wait(act, v_ready, 4 * h + 2 * p + 2)
                    act.sem_inc(ps_free[1], 1)

                def kd_keep(c):
                    n = span(c).stop - span(c).start
                    wait(act, kdT_ready, TT * h + c + 1)
                    nc.scalar.activation(kd[0:n, :], pm[0:n, 3, 0:DK], ACT.Copy).then_inc(kd_ready, 1)

                def o_keep(c):
                    n = span(c).stop - span(c).start
                    wait(act, o_ready, TT * h + c + 1)
                    nc.scalar.activation(glaT[:, bass.ds(4 * h, 4), span(c)],
                                         pm[:, 2, :].rearrange("p (e t) -> p e t", e=4)[:, :, 0:n], ACT.Copy
                                         ).then_inc(o_kept, 1)

                decays(0)
                v_keep(0)
                v_keep(1)
                for c in range(NT):
                    kd_keep(c)
                    wait(act, ps_ready[0], u + 7 + c)
                    nc.scalar.activation(th(rs[:, c, :]), halves(0), ACT.Tanh, scale=0.5).then_inc(rtanh_ready, 1)
                    o_keep(c)
                    decays(c + 1)
                kd_keep(NT)
                o_keep(NT)
                wait(act, o_kept, TT * h + TT + 1)
                wait(act, ps_ready[1], u + 14)
                nc.scalar.activation(sq[:, :, :], glaT[:, bass.ds(4 * h, 4), :], ACT.Square).then_inc(osq_ready, 1)
                for s in range(2):
                    wait(act, ps_ready[s], u + 15)
                    nc.scalar.activation(rms[:, s * HALF:(s + 1) * HALF], ps[:, s, 0, 0:HALF], ACT.Copy,
                                         scale=1.0 / DV, bias=EPS).then_inc(rms_done, 1)
                    wait(act, rms_done, 3 * h + s + 1)
                    act.sem_inc(ps_free[s], 1)
                nc.scalar.activation(rms[:, :], rms[:, :], ACT.Sqrt).then_inc(rms_done, 1)
            step.leave(HEADS)
            wait(act, gla_ready, 4 * HEADS)
            wait(act, stores_done, HEADS + 1)
            with act.Fori(0, D // PAIR) as i:
                for n, (dst, ready, used) in enumerate(((gsigB, gateB_ready, mergedB_ready),
                                                        (gsigA, gateA_ready, part_ready))):
                    wait(act, used, 2 * i + 1)
                    for j in range(2):
                        wait(act, ps_ready[j], USE_GATE + 4 * i + 2 * n + 1)
                        nc.scalar.activation(th(dst[:, j, :]), halves(j), ACT.Tanh, scale=0.5).then_inc(ready, 1)
                        wait(act, ready, 2 * i + j + 1)
                        act.sem_inc(ps_free[j], 1)
            wait(act, kkT_ready, 1)
            nc.scalar.activation(kkT[:, :, :].rearrange("p a b -> p (a b)"), pm[:, 3, 0:2 * P], ACT.Copy
                                 ).then_inc(kk_ready, 1)
            for t in range(TT):
                rows = P if t < NT else NS
                wait(act, resid_ready, 16)
                if t:
                    wait(act, ss2_done, t)
                nc.scalar.activation(ring[0:rows, 1, :], resid[0:rows, t, :], ACT.Square,
                                     accum_out=small[0:rows, t:t + 1]).then_inc(ss2_done, 1)
            for t in range(TT):
                rows = P if t < NT else NS
                wait(act, ms2_ready, t + 1)
                nc.scalar.activation(small[0:rows, TT + t:TT + t + 1], small[0:rows, TT + t:TT + t + 1], ACT.Sqrt
                                     ).then_inc(rms2_ready, 1)
            for t in range(TT):
                rows = P if t < NT else NS
                for s in range(2):
                    wait(act, ps_ready[s], USE_H2 + t + 1)
                    nc.scalar.activation(normT[:, 8 * s:8 * s + 8, span(t)],
                                         flat(s).rearrange("p (k t) -> p k t", k=8)[:, :, 0:rows], ACT.Copy
                                         ).then_inc(h2T_ready, 1)
                    wait(act, h2T_ready, 2 * t + s + 1)
                    act.sem_inc(ps_free[s], 1)

            def queries(i, hh):
                wait(act, keyscores_ready, UNITS * i + 1)
                for j in range(2):
                    wait(act, ps_ready[j], USE_WQ + 2 * i + hh + 1)
                    nc.scalar.activation(th(qp[:, hh, j, :]), halves(j), ACT.Copy).then_inc(qp_ready, 1)
                    wait(act, qp_ready, 4 * i + 2 * hh + j + 1)
                    act.sem_inc(ps_free[j], 1)

            with act.Fori(0, PH // 2) as i:
                queries(i, 0)
                for unit in range(UNITS):
                    wait(act, negmax_ready, UNITS * i + unit + 1)
                    nc.scalar.activation(gexp[:, unit % 3, :], cs[:, 0:TOPK], ACT.Exp, bias=cs[:, TOPK:TOPK + 1],
                                         accum_out=gsum[:, unit % 3:unit % 3 + 1]).then_inc(softmax_ready, 1)
                    if unit == 0:
                        queries(i, 1)
                    wait(act, gelu_arg, UNITS * i + unit + 1)
                    nc.scalar.activation(gelu_t[:, :], gelu_t[:, :], ACT.Tanh, scale=float(np.sqrt(2.0 / np.pi))
                                         ).then_inc(gelu_tanh, 1)
            wait(act, folded, 1)
            for t in range(TT):
                rows = P if t < NT else NS
                if t:
                    wait(act, ss3_done, t)
                nc.scalar.activation(ring[0:rows, 0, :], resid[0:rows, t, :], ACT.Square,
                                     accum_out=small[0:rows, t:t + 1]).then_inc(ss3_done, 1)
            for t in range(TT):
                rows = P if t < NT else NS
                wait(act, ms3_ready, t + 1)
                nc.scalar.activation(small[0:rows, TT + t:TT + t + 1], small[0:rows, TT + t:TT + t + 1], ACT.Sqrt
                                     ).then_inc(rms3_ready, 1)

        @block.vector
        def _(dve):
            step = Chain(dve, dve_step)
            for first in (conv_done, att_ready, factors_ready, mergedB_ready, part_ready, merged_ready, routed):
                dve.sem_inc(first, 1)
            for t in range(TT):
                rows = P if t < NT else NS
                dve.wait_ge(act_step, t + 1)
                dve.tensor_scalar(small[0:rows, TT + t:TT + t + 1], small[0:rows, t:t + 1], 1.0 / D, EPS,
                                  ALU.mult, ALU.add).then_inc(ss_ready, 1)
                dve.wait_ge(rms_ready, t + 1)
                step(dve.reciprocal(small[0:rows, 2 * TT + t:2 * TT + t + 1], small[0:rows, TT + t:TT + t + 1]))
                dve.tensor_scalar(x_in[0:rows, t, :], x_in[0:rows, t, :], small[0:rows, 2 * TT + t:2 * TT + t + 1],
                                  None, ALU.mult).then_inc(x_normed, 1)
            dve.wait_ge(g1_loaded, 16)
            for t in range(TT):
                rows = P if t < NT else NS
                for s in range(2):
                    dve.wait_ge(ps_ready[s], USE_X + t + 1)
                    dve.tensor_tensor(normT[:, 8 * s:8 * s + 8, t * P:t * P + rows],
                                      flat(s).rearrange("p (k t) -> p k t", k=8)[:, :, 0:rows],
                                      g1[:, 8 * s:8 * s + 8].unsqueeze(2).to_broadcast([P, 8, rows]), ALU.mult
                                      ).then_inc(normT_ready, 1)
                    dve.wait_ge(normT_ready, 2 * t + s + 1)
                    dve.sem_inc(ps_free[s], 1)
            per = 6 + 4 * TAPS
            with dve.Fori(0, CT // 2) as i:
                uv = uext[:, :, HIST + SEQ:].rearrange("p q (b t) -> p q b t", b=DEC_B)
                b0 = SEQ - HALF
                for j in range(2):
                    dve.wait_ge(gate_ready, 2 * i + j + 1)
                    dve.wait_ge(ps_ready[j], USE_CONV + 2 * i + 2)
                    if j == 0:
                        dve.wait_ge(tails_kept, 3 * i + 1)
                        dve.wait_ge(conv_done, 4 * i + 1)
                    dve.tensor_tensor(uext[:, j, HIST:HIST + HALF], gate_s[:, j, 0:HALF], ps[:, j, 0, 0:HALF],
                                      ALU.mult).then_inc(u_ready, 1)
                    dve.tensor_tensor(uext[:, j, HIST + HALF:HIST + SEQ], gate_s[:, j, HALF:SEQ], ps[:, j, 1, 0:b0],
                                      ALU.mult).then_inc(u_ready, 1)
                    dve.tensor_tensor(uv[:, j, :, HIST:], gate_s[:, j, SEQ:].rearrange("p (b t) -> p b t", b=DEC_B),
                                      ps[:, j, 1, b0:HALF].rearrange("p (b t) -> p b t", b=DEC_B), ALU.mult
                                      ).then_inc(u_ready, 1)
                    dve.wait_ge(u_ready, 6 * i + 3 * j + 3)
                    dve.sem_inc(ps_free[j], 1)
                dve.sem_inc(gate_used, 6)
                dve.wait_ge(uext_hist, 3 * i + 3)
                dve.wait_ge(wcur_ready, i + 1)
                dve.wait_ge(conv_kept, 2 * i + 1)
                for tap in range(TAPS):
                    for q in range(4):
                        j, sample = q % 2, q // 2
                        out = acc[:, j, SEQ:].rearrange("p (b t) -> p b t", b=DEC_B) if sample else acc[:, j, 0:SEQ]
                        src = uv[:, j, :, tap:tap + DEC_S] if sample else uext[:, j, tap:tap + SEQ]
                        n = 4 * tap + q
                        if tap:
                            dve.wait_ge(dve_step, TT + i * 4 * (TAPS - 1) + n - 3)
                            ins = dve.scalar_tensor_tensor(out=out, in0=src, scalar=wcur[:, j, tap:tap + 1], in1=out,
                                                           op0=ALU.mult, op1=ALU.add)
                        else:
                            ins = dve.tensor_scalar(out, src, wcur[:, j, tap:tap + 1], None, ALU.mult)
                        ins.then_inc(conv_done if tap == TAPS - 1 else dve_step, 1)
            dve.wait_ge(mean_ready, 1)
            dve.wait_ge(conv_kept, CT + 1)
            dve.tensor_tensor(conv[:, :, :], conv[:, :, :], mean_s[:, :].unsqueeze(1).to_broadcast([P, CT, TOK]),
                              ALU.subtract).then_inc(centered, 1)
            dve.wait_ge(ps_ready[0], USE_VAR0 + 1)
            dve.wait_ge(centered, 1)
            dve.tensor_scalar(th(mean_s[:, :]), halves(0), 1.0 / CONV, EPS, ALU.mult, ALU.add).then_inc(sd_ready, 1)
            dve.wait_ge(sd_ready, 2)
            dve.sem_inc(ps_free[0], 1)
            base = TT + CT // 2 * 4 * (TAPS - 1)
            dve.reciprocal(mean_s[:, :], mean_s[:, :]).then_inc(dve_step, 1)
            dve.wait_ge(dve_step, base + 1)
            dve.tensor_tensor(conv[:, :, :], conv[:, :, :], mean_s[:, :].unsqueeze(1).to_broadcast([P, CT, TOK]),
                              ALU.mult).then_inc(lned, 1)
            dve.wait_ge(tanhed, 1)
            dve.scalar_tensor_tensor(out=conv[:, :, :], in0=sq_ln[:, :, :], scalar=1.0, in1=conv[:, :, :],
                                     op0=ALU.add, op1=ALU.mult).then_inc(silu_ready, 1)

            dve.wait_ge(spilled, 16)
            dve.wait_ge(tail_stored, 48)
            dve.wait_ge(za_ready, 1)
            dve.wait_ge(masks_made, 1)
            step.base, step.n = base + 1, 0
            with dve.Fori(0, HEADS) as h:
                step.enter(h, TT + 3 + 2)
                u = head(h)
                for s, dst, src in ((0, lg[:, 0:NT, :].rearrange("p t d -> p (t d)"), flat(0)),
                                    (1, lg[0:NS, NT, :], flat(1)[0:NS, 0:DK])):
                    dve.wait_ge(lgabs_ready, 2 * h + s + 1)
                    dve.scalar_tensor_tensor(out=dst, in0=src, scalar=0.0, in1=dst, op0=ALU.min, op1=ALU.subtract
                                             ).then_inc(lg_ready, 1)
                    dve.wait_ge(lg_ready, 2 * h + s + 1)
                    dve.sem_inc(ps_free[s], 1)
                dve.wait_ge(b_ready, 2 * h + 2 + 1)

                def views(x, c, w):
                    g = (P if c < NT else NS) // (2 * w)
                    return x.rearrange("p j (g u w) -> p j g u w", g=g, u=2)

                def arguments(c):
                    n = span(c).stop - span(c).start
                    for l, w in levels(c):
                        bv = views(bT[:, :, span(c)], c, w)
                        piv = bv[:, :, :, 0, w - 1:w].to_broadcast([P, 2, n // (2 * w), w])
                        eq = earg[:, 2 * l, :, 0:n // 2].rearrange("p j (g w) -> p j g w", w=w)
                        ek = earg[:, 2 * l + 1, :, 0:n // 2].rearrange("p j (g w) -> p j g w", w=w)
                        dve.tensor_tensor(eq, bv[:, :, :, 1, :], piv, ALU.subtract)
                        last = dve.tensor_tensor(ek, piv, bv[:, :, :, 0, :], ALU.subtract)
                    last.then_inc(earg_ready, 1)
                    if c == NT:
                        dve.wait_ge(kdT_ready, TT * h + c)
                        bb = bT[:, :, SEQ:].rearrange("p j (b t) -> p j b t", b=DEC_B)
                        dve.tensor_tensor(kdec[:, :, 0:NS].rearrange("p j (b t) -> p j b t", b=DEC_B),
                                          bb[:, :, :, DEC_S - 1:DEC_S].to_broadcast([P, 2, DEC_B, DEC_S]), bb,
                                          ALU.subtract).then_inc(kdarg_ready, 1)

                def factors(c):
                    n = span(c).stop - span(c).start
                    e = 5 * NT * h + 4 * h + 5 * c
                    dve.wait_ge(scores_ready, TT * h + c + 1)
                    dve.wait_ge(exp_ready, e + 1)
                    for l, w in levels(c):
                        eq = earg[:, 2 * l, :, 0:n // 2].rearrange("p j (g w) -> p j g w", w=w)
                        ek = earg[:, 2 * l + 1, :, 0:n // 2].rearrange("p j (g w) -> p j g w", w=w)
                        dve.tensor_tensor(views(qf[:, l, :, 0:n], c, w)[:, :, :, 1, :], eq,
                                          views(qT[:, :, span(c)], c, w)[:, :, :, 1, :], ALU.mult)
                        last = dve.tensor_tensor(views(kf[:, l, :, 0:n], c, w)[:, :, :, 0, :], ek,
                                                 views(kT[:, :, span(c)], c, w)[:, :, :, 0, :], ALU.mult)
                    last.then_inc(factors_ready, 1)
                    dve.wait_ge(exp_ready, e + (5 if c < NT else 4))
                    dve.tensor_tensor(qe[:, :, 0:n], qe[:, :, 0:n], qT[:, :, span(c)], ALU.mult)
                    dve.tensor_tensor(kdec[:, :, 0:n], kdec[:, :, 0:n], kT[:, :, span(c)], ALU.mult
                                      ).then_inc(decay_ready, 1)

                def attention(c):
                    n = span(c).stop - span(c).start
                    lo = levels(c)[0][0]
                    sc = pm[:, 0:2, :].rearrange("p b (l t) -> p (b l) t", t=P)
                    dve.wait_ge(scores_ready, TT * h + c + 1 + 1)
                    dve.wait_ge(factors_ready, TT * h + c + 1 + 1)
                    step(dve.tensor_tensor(masked[0:n, lo:NL + 1, 0:n], sc[0:n, lo:NL + 1, 0:n],
                                           mask[0:n, lo:NL + 1, 0:n], ALU.mult))
                    if c:
                        dve.wait_ge(o_ready, TT * h + c)
                    dve.tensor_reduce(att[0:n, 0:n], masked[0:n, lo:NL + 1, 0:n].rearrange("p l t -> p t l"), AX.X,
                                      ALU.add).then_inc(att_ready, 1)
                    dve.wait_ge(att_ready, TT * h + c + 1 + 1)

                dve.wait_ge(q_ready, 2 * h + 2)
                dve.wait_ge(k_ready, 2 * h + 2)
                arguments(0)
                factors(0)
                for c in range(NT):
                    attention(c)
                    arguments(c + 1)
                    dve.wait_ge(rtanh_ready, 4 * h + c + 1)
                    dve.scalar_tensor_tensor(out=th(rs[:, c, :]), in0=th(rs[:, c, :]), scalar=1.0, in1=halves(0),
                                             op0=ALU.add, op1=ALU.mult).then_inc(rsilu_ready, 1)
                    dve.wait_ge(rsilu_ready, 4 * h + c + 1)
                    dve.sem_inc(ps_free[0], 1)
                    dve.wait_ge(ps_ready[1], u + 7 + c)
                    if c == 0:
                        dve.wait_ge(stores_done, h + 1)
                        dve.tensor_copy(state[:, :, :], ps[:, 1, :, :]).then_inc(state_ready, 1)
                    else:
                        step(dve.scalar_tensor_tensor(out=state[:, 0, :], in0=state[:, 0, :], scalar=dec[:, 0, 0:1],
                                                      in1=ps[:, 1, 0, :], op0=ALU.mult, op1=ALU.add))
                        dve.scalar_tensor_tensor(out=state[:, 1, :], in0=state[:, 1, :], scalar=dec[:, 1, 0:1],
                                                 in1=ps[:, 1, 1, :], op0=ALU.mult, op1=ALU.add
                                                 ).then_inc(state_ready, 1)
                    dve.wait_ge(state_ready, NT * h + c + 1)
                    dve.sem_inc(ps_free[1], 1)
                    factors(c + 1)
                attention(NT)
                dve.wait_ge(kd_ready, TT * h + TT + 1)
                for b in range(DEC_B):
                    if b >= 2:
                        dve.wait_ge(ps_ready[b % 2], u + 10 + b // 2)
                    dve.tensor_scalar(kdm[0:NS, b % 2, :], kd[0:NS, :], bmask[:, b:b + 1], None, ALU.mult
                                      ).then_inc(kdm_ready, 1)
                    dve.wait_ge(ps_ready[b % 2], u + 11 + b // 2)
                    for j in range(2):
                        dve.scalar_tensor_tensor(out=sring[:, b % 4, j, :], in0=sring[:, b % 4, j, :],
                                                 scalar=dec[:, j, b:b + 1], in1=ps[:, b % 2, j, :], op0=ALU.mult,
                                                 op1=ALU.add).then_inc(st_updated, 1)
                    dve.wait_ge(st_updated, 2 * DEC_B * h + 2 * b + 2)
                    dve.sem_inc(ps_free[b % 2], 1)
                dve.wait_ge(rms_done, 3 * h + 3)
                step(dve.reciprocal(rms[:, :], rms[:, :]))
                step(dve.tensor_tensor(rs[:, :, :], rs[:, :, :], rms[:, :].unsqueeze(1).to_broadcast([P, 4, TOK]),
                                       ALU.mult))
                for e in range(4):
                    dve.scalar_tensor_tensor(out=glaT[:, bass.ds(4 * h + e, 1), :].rearrange("p a t -> p (a t)"),
                                             in0=glaT[:, bass.ds(4 * h + e, 1), :].rearrange("p a t -> p (a t)"),
                                             scalar=ggla[:, bass.ds(4 * h + e, 1)], in1=rs[:, e, :],
                                             op0=ALU.mult, op1=ALU.mult).then_inc(gla_ready, 1)
                dve.wait_ge(gla_ready, 4 * h + 4)
            step.leave(HEADS)
            dve.wait_ge(stores_done, HEADS + 1)
            with dve.Fori(0, D // PAIR) as i:
                for n, (gate, ready, done) in enumerate(((gsigB, gateB_ready, mergedB_ready),
                                                         (gsigA, gateA_ready, part_ready))):
                    if n:
                        dve.wait_ge(merged_ready, i + 1)
                    for j in range(2):
                        dve.wait_ge(ready, 2 * i + j + 1)
                        dve.wait_ge(ps_ready[j], USE_GATE + 4 * i + 2 * n + 2)
                        dst = th(part[:, j, :]) if n else merged[:, bass.ds(2 * i + j, 1), :].rearrange(
                            "p a (b n) -> p (a b) n", b=2)
                        dve.scalar_tensor_tensor(out=dst, in0=th(gate[:, j, :]), scalar=1.0, in1=halves(j),
                                                 op0=ALU.add, op1=ALU.mult).then_inc(done, 1)
                        dve.wait_ge(done, 2 * i + j + 1 + 1)
                        dve.sem_inc(ps_free[j], 1)
                dve.tensor_tensor(merged[:, bass.ds(2 * i, 2), :], merged[:, bass.ds(2 * i, 2), :], part[:, :, :],
                                  ALU.add).then_inc(merged_ready, 1)
            dve.wait_ge(resid_loaded, 32)
            with dve.Fori(0, D // PAIR) as i:
                for s, rows, dst, src in ((0, P, resid[:, 0:NT, bass.ds(i * PAIR, PAIR)],
                                           flat(0).rearrange("p (t c) -> p t c", t=NT)),
                                          (1, NS, resid[0:NS, NT, bass.ds(i * PAIR, PAIR)], flat(1)[0:NS, 0:PAIR])):
                    dve.wait_ge(ps_ready[s], USE_MIX + i + 1)
                    dve.scalar_tensor_tensor(out=dst, in0=src, scalar=0.25, in1=dst, op0=ALU.mult, op1=ALU.add
                                             ).then_inc(resid_ready, 1)
                    dve.wait_ge(resid_ready, 2 * i + s + 1)
                    dve.sem_inc(ps_free[s], 1)
            dve.wait_ge(g2_loaded, 16)
            for t in range(TT):
                rows = P if t < NT else NS
                dve.wait_ge(ss2_done, t + 1)
                dve.tensor_scalar(small[0:rows, TT + t:TT + t + 1], small[0:rows, t:t + 1], 1.0 / D, EPS,
                                  ALU.mult, ALU.add).then_inc(ms2_ready, 1)
            dve.wait_ge(rms2_ready, TT)
            for t in range(TT):
                rows = P if t < NT else NS
                step(dve.reciprocal(small[0:rows, 2 * TT + t:2 * TT + t + 1], small[0:rows, TT + t:TT + t + 1]))
                dve.scalar_tensor_tensor(out=h2[0:rows, t, :], in0=resid[0:rows, t, :],
                                         scalar=small[0:rows, 2 * TT + t:2 * TT + t + 1], in1=ring[0:rows, 0, :],
                                         op0=ALU.mult, op1=ALU.mult).then_inc(h2_ready, 1)
            dve.wait_ge(h2_ready, TT)
            step(dve.memset(resid[NS:P, NT, :], 0.0))
            dve.wait_ge(h2_doubled, 16)
            dve.wait_ge(kk_ready, 1)
            dve.sem_inc(rows_used, RING)

            def route(i, unit):
                wait(dve, keyscores_ready, UNITS * i + unit + 1 + 1)
                sc = pm[:, unit % 4, 0:2 * NKEY].rearrange("p (a n) -> p a n", a=2)
                for a_ in range(2):
                    step.mark(dve.max(v12[:, a_, 0:8], sc[:, a_, :]))
                for a_ in range(2):
                    step.wait(1)
                    step.mark(dve.max_index(i12[:, a_, 0:8], v12[:, a_, 0:8], sc[:, a_, :]))
                for a_ in range(2):
                    step.mark(dve.match_replace(sc2[:, a_, :], v12[:, a_, 0:8], sc[:, a_, :], NEG))
                for a_ in range(2):
                    step.wait(1)
                    step.mark(dve.max(v12[:, a_, 8:16], sc2[:, a_, :]))
                for a_ in range(2):
                    step.wait(1)
                    step.mark(dve.max_index(i12[:, a_, 8:16], v12[:, a_, 8:16], sc2[:, a_, :]))
                step(dve.tensor_tensor(cand[:, :, :], v12[:, 0, :].unsqueeze(2).to_broadcast([P, TOPK, TOPK]),
                                       v12[:, 1, :].unsqueeze(1).to_broadcast([P, TOPK, TOPK]), ALU.add))
                wait(dve, softmax_ready, UNITS * i + unit + 1)
                flatc = cand[:, :, :].rearrange("p a b -> p (a b)")
                step(dve.max(cs[:, 0:8], flatc))
                step.mark(dve.max_index(ci[:, 0:8], cs[:, 0:8], flatc))
                step(dve.match_replace(cand2[:, :], cs[:, 0:8], flatc, NEG))
                step(dve.max(cs[:, 8:16], cand2[:, :]))
                dve.tensor_scalar(cs[:, TOPK:TOPK + 1], cs[:, 0:1], -1.0, None, ALU.mult).then_inc(negmax_ready, 1)
                step(dve.max_index(ci[:, 8:16], cs[:, 8:16], cand2[:, :]))
                step.mark(dve.tensor_copy(i12f[:, :, :], i12[:, :, :]))
                step.mark(dve.tensor_scalar(abi[:, 0, :], ci[:, :], 4, None, ALU.logical_shift_right))
                step(dve.tensor_scalar(abi[:, 1, :], ci[:, :], TOPK - 1, None, ALU.bitwise_and))
                step(dve.tensor_copy(ab[:, :, :], abi[:, :, :]))
                for a_ in range(2):
                    step(dve.tensor_tensor(oh[:, :, :], ab[:, a_, :].unsqueeze(2).to_broadcast([P, TOPK, TOPK]),
                                           iota16[:, :].unsqueeze(1).to_broadcast([P, TOPK, TOPK]), ALU.is_equal))
                    step(dve.tensor_tensor(oh[:, :, :], oh[:, :, :],
                                           i12f[:, a_, :].unsqueeze(1).to_broadcast([P, TOPK, TOPK]), ALU.mult))
                    step(dve.tensor_reduce(esel[:, a_, :], oh[:, :, :], AX.X, ALU.add))
                dve.scalar_tensor_tensor(out=idx[:, unit % 3, :], in0=esel[:, 0, :], scalar=float(NKEY),
                                         in1=esel[:, 1, :], op0=ALU.mult, op1=ALU.add).then_inc(routed, 1)

            def arrived(i, m):
                dve.wait_ge(rows_loaded[m % RING], 16 * (ROWS // RING) * i + 16 * (m // RING) + 16)

            with dve.Fori(0, PH // 2) as i:
                step.enter(i, 32 * UNITS)
                route(i, 0)
                for unit in range(UNITS):
                    t = NT if unit == 2 * NT else unit % NT
                    m0 = 2 * TOPK * unit
                    for k in range(TOPK):
                        arrived(i, m0 + k)
                        tile = ring[:, (m0 + k) % RING, :]
                        dve.tensor_tensor_reduce(out=tile, in0=tile, in1=h2[:, t, :], scale=1.0, scalar=0.0,
                                                 op0=ALU.mult, op1=ALU.add, accum_out=hidden[:, k:k + 1]
                                                 ).then_inc(rows_used, 1)
                    dve.wait_ge(rows_used, ROWS * i + m0 + TOPK + RING)
                    step(dve.tensor_tensor(gelu_t[:, :], hidden[:, :], hidden[:, :], ALU.mult))
                    step(dve.tensor_scalar(gelu_t[:, :], gelu_t[:, :], 0.044715, 1.0, ALU.mult, ALU.add))
                    dve.tensor_tensor(gelu_t[:, :], gelu_t[:, :], hidden[:, :], ALU.mult).then_inc(gelu_arg, 1)
                    dve.wait_ge(softmax_ready, UNITS * i + unit + 1 + 1)
                    step.mark(dve.reciprocal(gsum[:, unit % 3:unit % 3 + 1], gsum[:, unit % 3:unit % 3 + 1]))
                    if unit + 1 < UNITS:
                        route(i, unit + 1)
                    dve.wait_ge(gelu_tanh, UNITS * i + unit + 1)
                    step(dve.scalar_tensor_tensor(out=wexp[:, :], in0=gelu_t[:, :], scalar=1.0, in1=hidden[:, :],
                                                  op0=ALU.add, op1=ALU.mult))
                    step(dve.tensor_scalar(wexp[:, :], wexp[:, :], gsum[:, unit % 3:unit % 3 + 1], 0.5,
                                           ALU.mult, ALU.mult))
                    step(dve.tensor_tensor(wexp[:, :], wexp[:, :], gexp[:, unit % 3, :], ALU.mult))
                    for k in range(TOPK):
                        m = m0 + TOPK + k
                        arrived(i, m)
                        dve.scalar_tensor_tensor(out=resid[:, t, :], in0=ring[:, m % RING, :],
                                                 scalar=wexp[:, k:k + 1], in1=resid[:, t, :],
                                                 op0=ALU.mult, op1=ALU.add).then_inc(rows_used, 1)
                        dve.wait_ge(rows_used, ROWS * i + m + 1 + RING)
            step.leave(PH // 2)
            dve.sem_inc(peer_done, 1)
            dve.wait_ge(fold_loaded, 16)
            dve.tensor_tensor(resid[0:NS, NT, :], resid[0:NS, NT, :], h2[0:NS, 1, :], ALU.add).then_inc(folded, 1)
            dve.wait_ge(fg_loaded, 16)
            for t in range(TT):
                rows = P if t < NT else NS
                dve.wait_ge(ss3_done, t + 1)
                dve.tensor_scalar(small[0:rows, TT + t:TT + t + 1], small[0:rows, t:t + 1], 1.0 / D, EPS,
                                  ALU.mult, ALU.add).then_inc(ms3_ready, 1)
            dve.wait_ge(rms3_ready, TT)
            for t in range(TT):
                rows = P if t < NT else NS
                step(dve.reciprocal(small[0:rows, 2 * TT + t:2 * TT + t + 1], small[0:rows, TT + t:TT + t + 1]))
                dve.scalar_tensor_tensor(out=resid[0:rows, t, :], in0=resid[0:rows, t, :],
                                         scalar=small[0:rows, 2 * TT + t:2 * TT + t + 1], in1=h2[0:rows, 0, :],
                                         op0=ALU.mult, op1=ALU.mult).then_inc(y_ready, 1)


_INS = ['x_prompt', 'x_sample', 'state_conv', 'state_gla', 'norm1_g', 'w_in', 'w_a2', 'b_a', 'w_dw', 'b_dw',
        'conv_ln_g', 'conv_ln_b', 'w_conv_out', 'gla_norm_g', 'w_gla_o', 'w_mix_out', 'norm2_g', 'peer_wq',
        'peer_k1', 'peer_k2', 'peer_u', 'peer_v', 'final_g']
_OUTS = [(1, 512, 2048), (8, 8, 2048), (1, 1, 30, 1024), (1, 1, 4, 256, 512), (1, 8, 30, 1024), (1, 8, 4, 256, 512)]


def kernel(**inputs):
    import numpy as _np
    import concourse.bacc as _bacc
    from concourse import mybir as _mybir
    from concourse.bass_utils import run_bass_kernel_spmd as _run

    nc = _bacc.Bacc("TRN2", target_bir_lowering=False, num_devices=1)
    arrays, ins = {}, {}
    for name in _INS:
        x = _np.ascontiguousarray(inputs[name])
        arrays[f"in_{name}"] = x
        ins[name] = nc.dram_tensor(f"in_{name}", x.shape, _mybir.dt.from_np(x.dtype), kind="ExternalInput").ap()
    outs = [nc.dram_tensor(f"out_{i}", s, _mybir.dt.float32, kind="ExternalOutput").ap() for i, s in enumerate(_OUTS)]
    trunk(nc, ins, outs)
    r = _run(nc, [arrays], core_ids=[0])
    return tuple(r.results[0][f"out_{i}"] for i in range(len(_OUTS)))
```

```python
from contextlib import ExitStack

import numpy as np
import concourse.bass as bass
from concourse import mybir

F32 = mybir.dt.float32
I32 = mybir.dt.int32
U32 = mybir.dt.uint32
ACT = mybir.ActivationFunctionType
ALU = mybir.AluOpType
AX = mybir.AxisListType

P = 128
D = 2048
SEQ, DEC_B, DEC_S = 512, 8, 8
NS = DEC_B * DEC_S
TOK = SEQ + NS
HALF = TOK // 2
KT = D // P
NT = SEQ // P
TT = NT + 1
CONV = 1024
CT = CONV // P
TAPS = 31
HIST = TAPS - 1
HEADS, DK, DV = 4, 256, 512
RANK = 16
PAIR = 256
EPS = 1e-6
PH, NKEY, TOPK, NEXP = 8, 128, 16, 16384
COL_A, COL_G, COL_Q, COL_K, COL_V, COL_R, COL_Z = 0, 1024, 2048, 3072, 4096, 6144, 8192
COL_GA, COL_GB = COL_Z + RANK, COL_Z + RANK + D
LEVELS = [64, 32, 16, 8, 4, 2, 1]
NL = len(LEVELS)
RING = 4
UNITS = 2 * TT
GT = 2
DT = TT - GT
D0 = GT * P
DN = TOK - D0
SLOTS = PH * TOPK
SET, STAGED = 8, 32
SETS = 8
NST = DN // STAGED
NG = NEXP // (2 * P)
STEPS = NG // PH
PER = 2 * GT * TOPK // STEPS
ROWS = PER * STEPS
QUADS = 8
NEG = -3.0e38

USE_X = 0
USE_HIST = 5
USE_CONV = 6
USE_TAIL = 14
USE_MEAN1, USE_VAR0 = 15, 16
USE_ZA1 = 16
USE_HEAD, PER_HEAD = 17, 15
USE_GATE = USE_HEAD + HEADS * PER_HEAD
USE_MIX = USE_GATE + 32
USE_H2 = USE_MIX + 8
USE_RT = USE_H2 + TT
USE_WQ = USE_RT + DT
USE_SEL = USE_WQ + PH
USE_G = USE_SEL + 1
USE_V = USE_G + DN // SET // 2
USE_OUT = USE_V + NG * QUADS // 2
N_HEAD, N_GATE, N_MIX, N_WQ = 8, 32, 64, 72


eng_passed = {}


def wait(eng, sem, value):
    if isinstance(value, int) and value <= 0:
        return
    eng.wait_ge(sem, value)
    if not isinstance(value, int):
        eng.sem_inc(eng_passed[eng.engine], 1)


class Chain:

    def __init__(self, eng, sem):
        self.eng, self.sem, self.base, self.n = eng, sem, 0, 0

    def mark(self, ins):
        self.n += 1
        ins.then_inc(self.sem, 1)

    def wait(self, back=0):
        wait(self.eng, self.sem, self.base + self.n - back)

    def __call__(self, ins):
        self.mark(ins)
        self.wait()

    def enter(self, i, per_trip, first=0):
        self.start, self.per = self.base + self.n, per_trip
        self.base, self.n = self.start - first * per_trip + i * per_trip, 0

    def leave(self, trips):
        assert self.n == self.per, self.n
        self.base, self.n = self.start + self.per * trips, 0


def trunk(nc, a, o):
    eng_passed.clear()
    ctx = ExitStack()
    with ctx:
        def sb(name, shape, dt=F32):
            return ctx.enter_context(nc.sbuf_tensor(name, shape, dt))

        def sem(name):
            return ctx.enter_context(nc.semaphore(name))

        normT = sb("normT", [P, KT, TOK])
        wring = sb("wring", [P, 2, KT, PAIR])
        regB = sb("regB", [P, TT * D])
        glaT = regB[:, 0:KT * TOK].rearrange("p (k t) -> p k t", k=KT)
        resid = regB[:, :].rearrange("p (t d) -> p t d", t=TT)
        ident = sb("ident", [P, P])
        ones = sb("ones", [P, P])
        tri = sb("tri", [P, P])
        tri8 = sb("tri8", [NS, NS])
        bmask = sb("bmask", [NS, DEC_B])
        g1 = sb("g1", [P, KT])
        gln = sb("gln", [P, CT])
        bln = sb("bln", [P, CT])
        bdw = sb("bdw", [P, CT])
        ggla = sb("ggla", [P, KT])
        small = sb("small", [P, 3 * TT])
        zaT = sb("zaT", [RANK + 1, TT * P])
        wa2 = sb("wa2", [RANK + 1, HEADS * DK])
        i12 = sb("i12", [P, 2, 16], U32)
        ci = sb("ci", [P, 16], U32)
        abi = sb("abi", [P, 2, 16], U32)
        idx = sb("idx", [P, GT, TOPK], I32)
        iota16 = sb("iota16", [P, 16])
        ARENA = nc.sbuf_bytes_remaining // 4 - 8
        arena = sb("arena", [P, ARENA])

        def layout(*parts):
            out, at = [], 0
            for shape in parts:
                n = int(np.prod(shape))
                v = arena[:, at:at + n]
                if len(shape) == 2:
                    v = v.rearrange("p (a b) -> p a b", a=shape[0])
                elif len(shape) == 3:
                    v = v.rearrange("p (a b c) -> p a b c", a=shape[0], b=shape[1])
                out.append(v)
                at += n
            assert at <= ARENA, (at, ARENA)
            return out

        (x_in,) = layout((TT, D))
        EXT = HIST + SEQ + DEC_B * (HIST + DEC_S)
        conv, hist, uext, gate_s, acc, sq_ln, mean_s, wdw, wcur, wza, tails = layout(
            (CT, TOK), (CT, HIST * 9), (2, EXT), (2, TOK), (2, TOK), (CT, TOK), (TOK,), (CT, TAPS), (2, TAPS),
            (KT, RANK), (3, CONV))
        (qT, kT, lg, bT, vt, qf, kf, earg, mask, att, state, sring, qe, kdec, kd, kdm, dec, rs, rms) = layout(
            (2, TOK), (2, TOK), (TT, DK), (2, TOK), (TT, DV), (NL, 2, P), (NL, 2, P), (2 * NL, 2, P // 2),
            (NL + 1, P), (P,), (2, DV), (4, 2, DV), (2, P), (2, P), (DK,), (2, DK), (2, DEC_B), (4, TOK), (TOK,))
        masked = earg.rearrange("p a b c -> p (a b c)")[:, 0:(NL + 1) * P].rearrange("p (l t) -> p l t", l=NL + 1)
        sq = vt.rearrange("p t e -> p (t e)")[:, 0:4 * TOK].rearrange("p (e t) -> p e t", e=4)
        merged, convg, gsigB, gsigA, part = layout((KT, TOK), (CT, TOK), (2, TOK), (2, TOK), (2, TOK))
        def part_of(buf, at, *shape):
            n = int(np.prod(shape))
            v = buf[:, at:at + n]
            if len(shape) == 2:
                return v.rearrange("p (a b) -> p a b", a=shape[0])
            if len(shape) == 3:
                return v.rearrange("p (a b c) -> p a b c", a=shape[0], b=shape[1])
            if len(shape) == 4:
                return v.rearrange("p (a b c e) -> p a b c e", a=shape[0], b=shape[1], c=shape[2])
            return v

        h2 = part_of(arena, 0, TT, D)
        ring = part_of(arena, GT * D, RING, D)
        g2 = part_of(arena, TT * D, D)
        seld = part_of(arena, TT * D, DT, 3, SLOTS)
        at = (GT + RING) * D
        accT = part_of(arena, at, KT, DN)
        squares = part_of(arena, at, D)
        at += KT * DN
        qp = part_of(arena, at, 2, 2, TOK)
        selT = part_of(arena, at, 3, DN)
        gT = part_of(arena, at, 2, NST, 2 * STAGED)
        at += 4 * TOK
        gall = part_of(arena, at, GT, SLOTS)
        idxs = part_of(arena, at + GT * SLOTS, GT, SLOTS).bitcast(I32)
        at += 2 * GT * SLOTS
        work = arena[:, at:ARENA]
        ktab, kkT, sc2 = (part_of(work, n * 2 * P, 2, P) for n in range(3))
        cand, oh = (part_of(work, 6 * P + n * 2 * P, TOPK, TOPK) for n in range(2))
        cand2 = part_of(work, 10 * P, TOPK * TOPK)
        v12, i12f, ab, esel = (part_of(work, 12 * P + n * 2 * TOPK, 2, TOPK) for n in range(4))
        cs = part_of(work, 13 * P, TOPK + 1)
        gsum = part_of(work, 13 * P + 32, PH)
        iota128 = part_of(work, 14 * P, P)
        x2 = part_of(work, 0, 2, DN)
        WT = part_of(work, 2 * DN, 2, 2, DN)
        hidden, gelu_t, wexp = (part_of(work, 6 * DN + n * TOPK, TOPK) for n in range(3))
        assert at + 6 * DN + 3 * TOPK <= ARENA and at + 15 * P <= ARENA, (at, ARENA)
        ohs = part_of(regB, GT * D, 2, 2, SET, P)
        stage = [part_of(wring[:, st, :, :].rearrange("p k c -> p (k c)"), 0, P, STAGED) for st in range(2)]
        uraw = wring[:, 0, :, :].rearrange("p k c -> p (k c)").rearrange("p (b d) -> p b d", b=2)
        UT = wring[:, 1, :, :].rearrange("p k c -> p (k c)").rearrange("p (n e) -> p n e", n=2 * KT)
        h2T = normT[:, :, D0:TOK]

        def vblock(pair, b):
            if pair == 0:
                return normT[:, b * KT // 2:(b + 1) * KT // 2, 0:PAIR]
            return regB[:, (GT + b) * D:(GT + b + 1) * D].rearrange("p (k c) -> p k c", c=PAIR)

        ps = ctx.enter_context(nc.psum_tensor("ps", [P, 2, 2, 512], F32))
        pm = ctx.enter_context(nc.psum_tensor("pm", [P, 4, 512], F32))
        gates_dram = nc.dram_tensor("gates", [NST, P, P * STAGED], F32, kind="Internal").ap()
        conv_dram = nc.dram_tensor("conv_spill", [P, CT * TOK], F32, kind="Internal").ap()

        def flat(s):
            return ps[:, s, :, :].rearrange("p b n -> p (b n)")

        def halves(s):
            return ps[:, s, :, 0:HALF]

        def th(ap):
            return ap.rearrange("p (b n) -> p b n", b=2)

        def head(h):
            return USE_HEAD + PER_HEAD * h

        def span(c):
            return slice(c * P, c * P + (P if c < NT else NS))

        def levels(c):
            return [(l, w) for l, w in enumerate(LEVELS) if c < NT or w < DEC_S]

        for e in (nc.sync, nc.gpsimd, nc.tensor, nc.scalar, nc.vector):
            eng_passed[e.engine] = sem(f"waits_passed_{len(eng_passed)}")
        w_loaded = [sem("w_loaded0"), sem("w_loaded1")]
        ps_ready = [sem("ps_ready0"), sem("ps_ready1")]
        ps_free = [sem("ps_free0"), sem("ps_free1")]
        const_loaded = sem("const_loaded")
        x_loaded = [sem(f"x_loaded{t}") for t in range(TT)]
        g1_loaded = sem("g1_loaded")
        hist_loaded = sem("hist_loaded")
        consts_made = sem("consts_made")
        act_step, dve_step, pool_step = sem("act_step"), sem("dve_step"), sem("pool_step")
        ss_ready, rms_ready, x_normed = sem("ss_ready"), sem("rms_ready"), sem("x_normed")
        normT_ready = sem("normT_ready")
        hist_zeroed, hist_ready, uext_hist, u_ready, tails_kept = sem("hist_zeroed"), sem("hist_ready"), sem("uext_hist"), sem("u_ready"), sem("tails_kept")
        gate_ready, gate_used = sem("gate_ready"), sem("gate_used")
        wcur_ready, conv_done, conv_kept = sem("wcur_ready"), sem("conv_done"), sem("conv_kept")
        tail_ready, tail_stored = sem("tail_ready"), sem("tail_stored")
        mean_ready, centered, sqln_ready, sd_ready, lned, affined, tanhed, silu_ready = (
            sem("mean_ready"), sem("centered"), sem("sqln_ready"), sem("sd_ready"), sem("lned"), sem("affined"),
            sem("tanhed"), sem("silu_ready"))
        spilled, reloaded = sem("spilled"), sem("reloaded")
        za_ready = sem("za_ready")
        wa2_loaded = sem("wa2_loaded")
        stores_done = sem("stores_done")
        za_ready2 = sem("za_ready2")
        masks_made = sem("masks_made")
        lgabs_ready, lg_ready, k_ready, q_ready, b_ready, v_ready = (
            sem("lgabs_ready"), sem("lg_ready"), sem("k_ready"), sem("q_ready"), sem("b_ready"), sem("v_ready"))
        earg_ready, exp_ready, kdarg_ready, decay_ready = (
            sem("earg_ready"), sem("exp_ready"), sem("kdarg_ready"), sem("decay_ready"))
        factors_ready, scores_ready, att_ready, o_ready, o_kept = (
            sem("factors_ready"), sem("scores_ready"), sem("att_ready"), sem("o_ready"), sem("o_kept"))
        kdT_ready, kd_ready, kdm_ready = sem("kdT_ready"), sem("kd_ready"), sem("kdm_ready")
        rtanh_ready, rsilu_ready = sem("rtanh_ready"), sem("rsilu_ready")
        state_ready, state_stored = sem("state_ready"), sem("state_stored")
        st_updated = sem("st_updated")
        st_loaded = [sem(f"st_loaded{k}") for k in range(4)]
        st_stored = [sem(f"st_stored{k}") for k in range(4)]
        gateB_ready, gateA_ready, mergedB_ready, part_ready, merged_ready = (
            sem("gateB_ready"), sem("gateA_ready"), sem("mergedB_ready"), sem("part_ready"), sem("merged_ready"))
        conv_back, resid_loaded, g2_loaded, resid_ready = (
            sem("conv_back"), sem("resid_loaded"), sem("g2_loaded"), sem("resid_ready"))
        ktab_loaded, kkT_ready, kk_ready = sem("ktab_loaded"), sem("kkT_ready"), sem("kk_ready")
        ss2_done, ms2_ready, rms2_ready, h2_ready, h2T_ready = (
            sem("ss2_done"), sem("ms2_ready"), sem("rms2_ready"), sem("h2_ready"), sem("h2T_ready"))
        qp_ready, keyscores_ready, routed, negmax_ready, softmax_ready, cs_free = (
            sem("qp_ready"), sem("keyscores_ready"), sem("routed"), sem("negmax_ready"), sem("softmax_ready"),
            sem("cs_free"))
        rows_used, gelu_arg, gelu_tanh, hidden_ready = (
            sem("rows_used"), sem("gelu_arg"), sem("gelu_tanh"), sem("hidden_ready"))
        accT_ready, iota_ready, sel_ready, selT_ready, onehot_ready, gated_ready, g_staged, stage_free = (
            sem("accT_ready"), sem("iota_ready"), sem("sel_ready"), sem("selT_ready"), sem("onehot_ready"),
            sem("gated_ready"), sem("g_staged"), sem("stage_free"))
        u_done, tr_done, ut_ready, sq_ready, arg_ready, tanh_ready, x1_ready, wt_ready, back_ready = (
            sem("u_done"), sem("tr_done"), sem("ut_ready"), sem("sq_ready"), sem("arg_ready"), sem("tanh_ready"),
            sem("x1_ready"), sem("wt_ready"), sem("back_ready"))
        idx_ready = sem("idx_ready")
        g_stored, gt_loaded, u_loaded, v_loaded = (
            [sem(f"{name}{k}") for k in range(2)] for name in ("g_stored", "gt_loaded", "u_loaded", "v_loaded"))
        rows_loaded = [sem(f"rows_loaded{k}") for k in range(RING)]
        fg_loaded, peer_done, ss3_done, ms3_ready, rms3_ready, y_ready, y_stored = (
            sem("fg_loaded"), sem("peer_done"), sem("ss3_done"), sem("ms3_ready"),
            sem("rms3_ready"), sem("y_ready"), sem("y_stored"))
        osq_ready, rms_done, gla_ready = sem("osq_ready"), sem("rms_done"), sem("gla_ready")

        block = ctx.enter_context(nc.Block())
        w_in = a["w_in"][0]

        @block.sync
        def _(sp):
            def load(slot, w, rows, col):
                k = rows // P
                sp.dma_start(wring[:, slot, 0:k, :],
                             w[:, bass.ds(col, PAIR)].rearrange("(k p) c -> p k c", p=P)).then_inc(w_loaded[slot], 16)

            for t in range(NT):
                sp.dma_start(x_in[:, t, :], a["x_prompt"][0, t * P:(t + 1) * P, :]).then_inc(x_loaded[t], 16)
            sp.dma_start(x_in[0:NS, NT, :], a["x_sample"].rearrange("b s d -> (b s) d")).then_inc(x_loaded[NT], 16)
            sp.dma_start(g1[:, :], a["norm1_g"].rearrange("o (k p) -> p (o k)", p=P),
                         allow_slow_non_contiguous=True).then_inc(g1_loaded, 16)
            load(0, w_in, D, COL_G)
            load(1, w_in, D, COL_A)
            with sp.Fori(1, CT // 2) as i:
                wait(sp, ps_ready[1], USE_CONV + 2 * i - 1)
                load(0, w_in, D, COL_G + i * PAIR)
                wait(sp, ps_ready[1], USE_CONV + 2 * i)
                load(1, w_in, D, COL_A + i * PAIR)

            wait(sp, ps_ready[1], USE_CONV + CT - 1)
            load(0, w_in, D, COL_K)
            wait(sp, ps_ready[1], USE_CONV + CT)
            load(1, w_in, D, COL_Q)
            sp.dma_start(wa2[0:RANK, :], a["w_a2"][0, :, :]).then_inc(wa2_loaded, 16)
            sp.dma_start(wa2[RANK:RANK + 1, :], a["b_a"]).then_inc(wa2_loaded, 16)
            for k in range(3):
                wait(sp, tail_ready, k + 1)
                if k == 0:
                    sp.dma_start(o[2][0, 0, :, :], tails[0:HIST, 0, :]).then_inc(tail_stored, 16)
                else:
                    sp.dma_start(o[4][0, 4 * (k - 1):4 * k, :, :].rearrange("b t c -> (b t) c"),
                                 tails[0:4 * HIST, k, :]).then_inc(tail_stored, 16)
            wait(sp, silu_ready, 1)
            sp.dma_start(conv_dram, conv[:, :, :].rearrange("p c t -> p (c t)")).then_inc(spilled, 16)
            wait(sp, tail_stored, 48)
            wait(sp, spilled, 16)

            def head_loads(h):
                u = head(h)
                wait(sp, ps_ready[1], u + 2)
                load(0, w_in, D, COL_V + h * DV)
                wait(sp, ps_ready[1], u + 3)
                load(1, w_in, D, COL_V + h * DV + PAIR)
                wait(sp, ps_ready[1], u + 5)
                load(0, w_in, D, COL_R + h * DV)
                wait(sp, ps_ready[1], u + 6)
                load(1, w_in, D, COL_R + h * DV + PAIR)

            with sp.Fori(0, HEADS - 1) as h:
                head_loads(h)
                wait(sp, ps_ready[0], head(h) + 8)
                load(0, w_in, D, COL_K + h * DK + DK)
                wait(sp, ps_ready[0], head(h) + 10)
                load(1, w_in, D, COL_Q + h * DK + DK)
            head_loads(HEADS - 1)
            wait(sp, ps_ready[0], head(HEADS - 1) + 8)
            load(0, w_in, D, COL_GB)
            wait(sp, ps_ready[0], head(HEADS - 1) + 10)
            load(1, a["w_gla_o"][0], D, 0)

            def gate_loads(i):
                wait(sp, ps_ready[1], USE_GATE + 4 * i + 1)
                load(0, w_in, D, COL_GA + i * PAIR)
                wait(sp, ps_ready[1], USE_GATE + 4 * i + 2)
                load(1, a["w_conv_out"][0], CONV, i * PAIR)

            with sp.Fori(0, D // PAIR - 1) as i:
                gate_loads(i)
                wait(sp, ps_ready[1], USE_GATE + 4 * i + 3)
                load(0, w_in, D, COL_GB + i * PAIR + PAIR)
                wait(sp, ps_ready[1], USE_GATE + 4 * i + 4)
                load(1, a["w_gla_o"][0], D, i * PAIR + PAIR)
            gate_loads(D // PAIR - 1)
            wait(sp, ps_ready[1], USE_MIX - 1)
            load(0, a["w_mix_out"][0], D, 0)
            wait(sp, ps_ready[1], USE_MIX)
            load(1, a["w_mix_out"][0], D, PAIR)
            with sp.Fori(1, D // PAIR // 2) as i:
                for slot in range(2):
                    wait(sp, ps_ready[1], USE_MIX + 2 * i - 1 + slot)
                    load(slot, a["w_mix_out"][0], D, (2 * i + slot) * PAIR)
            for slot in range(2):
                wait(sp, ps_ready[1], USE_H2 - 1 + slot)
                load(slot, a["peer_wq"][0], D, slot * PAIR)
            with sp.Fori(1, PH // 2) as i:
                for slot in range(2):
                    wait(sp, ps_ready[1], USE_WQ + 2 * i - 1 + slot)
                    load(slot, a["peer_wq"][0], D, (2 * i + slot) * PAIR)

            def v_load(g, pair):
                for b in range(2):
                    sp.dma_start(vblock(pair, b),
                                 a["peer_v"][0, bass.ds(g * 2 * P + b * P, P), :].rearrange("p (k c) -> p k c", c=PAIR)
                                 ).then_inc(v_loaded[pair], 16)

            def u_load(g, b):
                sp.dma_start(uraw[:, b, :], a["peer_u"][0, bass.ds(g * 2 * P + b * P, P), :]).then_inc(u_loaded[b], 16)

            def gates_load(g, slot):
                sp.dma_start(gT[:, slot, :, :],
                             gates_dram[:, :, bass.ds(g * 2 * STAGED, 2 * STAGED)].rearrange("t p c -> p t c")
                             ).then_inc(gt_loaded[slot], 16)

            wait(sp, ps_ready[1], USE_WQ + PH)
            v_load(0, 0)
            sp.sem_inc(stage_free, 2)
            with sp.Fori(0, DN // (SET * SETS)) as r:
                for st in range(2):
                    wait(sp, g_staged, SETS * r + 4 * st + 4)
                    sp.dma_start(gates_dram[bass.ds(2 * r + st, 1), :, :].rearrange("o p c -> p (o c)"),
                                 stage[st].rearrange("p i n -> p (i n)")).then_inc(g_stored[st], 16)
                    wait(sp, g_stored[st], 16 * r + 16)
                    sp.sem_inc(stage_free, 1)
            for b in range(2):
                u_load(0, b)
            gates_load(0, 0)

            def dense_loads(i, j, last=False):
                g = STEPS * i + j
                if not last:
                    wait(sp, tr_done, QUADS * g + 4)
                    u_load(g + 1, 0)
                    wait(sp, wt_ready, g)
                    gates_load(g + 1, (j + 1) % 2)
                    wait(sp, tr_done, QUADS * g + 8)
                    u_load(g + 1, 1)
                if not isinstance(i, int) or g:
                    wait(sp, ps_ready[1], USE_V + 4 * g - 4)
                    v_load(g, j % 2)

            for j in range(STEPS):
                dense_loads(0, j)
            with sp.Fori(1, PH - 1) as i:
                for j in range(STEPS):
                    dense_loads(i, j)
            for j in range(STEPS):
                dense_loads(PH - 1, j, j == STEPS - 1)
            for t in range(TT):
                n = P if t < NT else NS
                wait(sp, y_ready, t + 1)
                sp.dma_start(o[0][0, span(t), :] if t < NT else o[1].rearrange("b s d -> (b s) d"),
                             resid[0:n, t, :]).then_inc(y_stored, 16)
            wait(sp, y_stored, 16 * TT)

        @block.gpsimd
        def _(pool):
            step = Chain(pool, pool_step)
            for first in (tails_kept, stores_done):
                pool.sem_inc(first, 1)
            step(pool.memset(ident[:, :], 0.0))
            step(pool.affine_select(out=ident[:, :], in_=ident[:, :], compare_op=ALU.not_equal, fill=1.0, base=0,
                                    pattern=[[-1, P]], channel_multiplier=1))
            step(pool.memset(tri[:, :], 1.0 / 16.0))
            step(pool.affine_select(out=tri[:, :], in_=tri[:, :], compare_op=ALU.is_ge, fill=0.0, base=0,
                                    pattern=[[1, P]], channel_multiplier=-1))
            t8 = tri8[:, :].rearrange("p (b t) -> p b t", b=DEC_B)
            step(pool.tensor_copy(tri8[:, :], tri[0:NS, 0:NS]))
            step(pool.affine_select(out=t8, in_=t8, compare_op=ALU.is_ge, fill=0.0, base=0,
                                    pattern=[[-DEC_S, DEC_B], [0, DEC_S]], channel_multiplier=1))
            step(pool.memset(bmask[:, :], 1.0))
            step(pool.affine_select(out=bmask[:, :], in_=bmask[:, :], compare_op=ALU.is_ge, fill=0.0, base=0,
                                    pattern=[[-DEC_S, DEC_B]], channel_multiplier=1))
            step(pool.affine_select(out=bmask[:, :], in_=bmask[:, :], compare_op=ALU.is_ge, fill=0.0, base=DEC_S - 1,
                                    pattern=[[DEC_S, DEC_B]], channel_multiplier=-1))
            step(pool.iota(iota16[:, :], pattern=[[1, 16]], base=0, channel_multiplier=0,
                           allow_small_or_imprecise_dtypes=True))
            pool.memset(zaT[:, :], 1.0).then_inc(consts_made, 1)
            pool.memset(ones[:, :], 1.0).then_inc(consts_made, 1)
            wait(pool, normT_ready, 2 * TT)
            pool.dma_start(gln[:, :], a["conv_ln_g"].rearrange("o (k p) -> p (o k)", p=P),
                           allow_slow_non_contiguous=True).then_inc(const_loaded, 16)
            pool.dma_start(bln[:, :], a["conv_ln_b"].rearrange("o (k p) -> p (o k)", p=P),
                           allow_slow_non_contiguous=True).then_inc(const_loaded, 16)
            pool.dma_start(bdw[:, :], a["b_dw"].rearrange("o (k p) -> p (o k)", p=P),
                           allow_slow_non_contiguous=True).then_inc(const_loaded, 16)
            pool.dma_start(ggla[:, :], a["gla_norm_g"].rearrange("o (k p) -> p (o k)", p=P),
                           allow_slow_non_contiguous=True).then_inc(const_loaded, 16)
            for c in range(CT):
                pool.dma_start(wdw[:, c, :], a["w_dw"][0, :, c * P:(c + 1) * P].rearrange("j p -> p j"),
                               allow_slow_non_contiguous=True).then_inc(const_loaded, 16)
            pool.dma_start(wza[:, :, :], w_in[:, COL_Z:COL_Z + RANK].rearrange("(k p) c -> p k c", p=P)
                           ).then_inc(const_loaded, 16)
            for g in range(2):
                pool.dma_start(tails[0:4 * HIST, 1 + g, :],
                               a["state_conv"][0, 4 * g:4 * g + 4, :, :].rearrange("b t c -> (b t) c")
                               ).then_inc(hist_loaded, 16)
            pool.memset(hist[:, :, 0:HIST], 0.0).then_inc(hist_zeroed, 1)
            wait(pool, hist_zeroed, 1)
            wait(pool, hist_ready, 2)
            with pool.Fori(0, CT // 2) as i:
                wait(pool, conv_done, 4 * i + 1)
                hv = hist[:, bass.ds(2 * i, 2), :]
                uv = uext[:, :, HIST + SEQ:].rearrange("p q (b t) -> p q b t", b=DEC_B)
                pool.tensor_copy(uext[:, :, 0:HIST], hv[:, :, 0:HIST]).then_inc(uext_hist, 1)
                for q in range(2):
                    pool.tensor_copy(uv[:, q, :, 0:HIST], hv[:, q, HIST:].rearrange("p (b t) -> p b t", b=DEC_B)
                                     ).then_inc(uext_hist, 1)
                wait(pool, uext_hist, 3 * i + 3)
                wait(pool, u_ready, 6 * i + 6)
                pool.tensor_copy(hv[:, :, 0:HIST], uext[:, :, SEQ:SEQ + HIST]).then_inc(tails_kept, 1)
                for q in range(2):
                    pool.tensor_copy(hv[:, q, HIST:].rearrange("p (b t) -> p b t", b=DEC_B), uv[:, q, :, DEC_S:]
                                     ).then_inc(tails_kept, 1)
                wait(pool, tails_kept, 3 * i + 3 + 1)

            wait(pool, spilled, 16)
            wait(pool, tail_stored, 48)
            wait(pool, za_ready, 1)
            base = step.base + step.n
            n = 0
            pool.memset(mask[:, :, :], 1.0).then_inc(pool_step, 1)
            pool.memset(qf[:, :, :, :], 0.0).then_inc(pool_step, 1)
            pool.memset(kf[:, :, :, :], 0.0).then_inc(pool_step, 1)
            n = 3
            wait(pool, pool_step, base + n)
            for l, w in enumerate(LEVELS[1:], 1):
                for b, mul, st in ((0, 1, -2 * w), (2 * w - 1, -1, 2 * w)):
                    mv = mask[:, l, :].rearrange("p (g w) -> p g w", w=2 * w)
                    pool.affine_select(out=mv, in_=mv, compare_op=ALU.is_ge, fill=0.0, base=b,
                                       pattern=[[st, P // (2 * w)], [0, 2 * w]], channel_multiplier=mul
                                       ).then_inc(pool_step, 1)
                    n += 1
                    wait(pool, pool_step, base + n)
            pool.tensor_copy(mask[:, NL, :], ident[:, :]).then_inc(masks_made, 1)

            def state_load(h, b):
                pool.dma_start(sring[:, b % 4, :, :],
                               a["state_gla"][0, b, bass.ds(h, 1), :, :].rearrange("o (j p) e -> p (o j) e", p=P)
                               ).then_inc(st_loaded[b % 4], 16)

            with pool.Fori(0, HEADS) as h:
                for b in range(4):
                    state_load(h, b)
                wait(pool, state_ready, NT * h + NT)
                pool.dma_start(o[3][0, 0, bass.ds(h, 1), :, :].rearrange("o (j p) e -> p (o j) e", p=P),
                               state[:, :, :]).then_inc(state_stored, 16)
                for b in range(DEC_B):
                    wait(pool, st_updated, 2 * DEC_B * h + 2 * b + 2)
                    pool.dma_start(o[5][0, b, bass.ds(h, 1), :, :].rearrange("o (j p) e -> p (o j) e", p=P),
                                   sring[:, b % 4, :, :]).then_inc(st_stored[b % 4], 16)
                    if b < 4:
                        wait(pool, st_stored[b], 32 * h + 16)
                        state_load(h, b + 4)
                for b in range(4):
                    wait(pool, st_stored[b], 32 * h + 32)
                wait(pool, state_stored, 16 * h + 16)
                pool.sem_inc(stores_done, 1)
            wait(pool, gla_ready, 4 * HEADS)
            pool.dma_start(convg[:, :, :].rearrange("p c t -> p (c t)"), conv_dram).then_inc(conv_back, 16)
            wait(pool, ps_ready[0], USE_MIX - 2)
            wait(pool, ps_ready[1], USE_MIX - 2)
            pool.dma_start(resid[:, 0:NT, :], a["x_prompt"][0].rearrange("(t p) d -> p t d", p=P)
                           ).then_inc(resid_loaded, 16)
            pool.dma_start(resid[0:NS, NT, :], a["x_sample"].rearrange("b s d -> (b s) d")).then_inc(resid_loaded, 16)
            wait(pool, merged_ready, D // PAIR + 1)
            pool.dma_start(g2, a["norm2_g"].partition_broadcast(P)).then_inc(g2_loaded, 16)
            for half, key in enumerate(("peer_k1", "peer_k2")):
                pool.dma_start(ktab[:, half, :], a[key][0, :, :]).then_inc(ktab_loaded, 16)
            pool.iota(iota128, pattern=[[1, P]], base=0, channel_multiplier=0,
                      allow_small_or_imprecise_dtypes=True).then_inc(iota_ready, 1)
            wait(pool, selT_ready, DT)
            with pool.Fori(0, DN // (SET * SETS)) as r:
                for j in range(SETS):
                    wait(pool, onehot_ready, SETS * r + j + 1)
                    pool.tensor_tensor(ohs[:, j % 2, 0, :, :], ohs[:, j % 2, 0, :, :],
                                       selT[:, 2, bass.ds(SET * SETS * r + SET * j, SET)].unsqueeze(2).to_broadcast(
                                           [P, SET, P]), ALU.mult).then_inc(gated_ready, 1)

            def gathers(i):
                for m in range(ROWS):
                    t, k = m // (2 * TOPK), m % (2 * TOPK)
                    if k == 0:
                        wait(pool, rows_used, ROWS * i + m + 1)
                        pool.tensor_copy(idx[:, t, :], idxs[:, t, bass.ds(i * TOPK, TOPK)]).then_inc(idx_ready, 1)
                        wait(pool, idx_ready, GT * i + t + 1)
                    wait(pool, rows_used, ROWS * i + m + 1)
                    pool.indirect_dma_start(
                        ring[:, m % RING, :], None, (a["peer_u"] if k < TOPK else a["peer_v"])[0],
                        bass.IndirectOffsetOnAxis(ap=idx[:, t, k % TOPK:k % TOPK + 1], axis=0),
                        bounds_check=NEXP - 1, oob_is_err=True).then_inc(rows_loaded[m % RING], 16)

            with pool.Fori(0, PH) as i:
                gathers(i)
            wait(pool, peer_done, 1)
            pool.dma_start(h2[:, 0, :], a["final_g"].rearrange("(o d) -> o d", o=1).partition_broadcast(P)
                           ).then_inc(fg_loaded, 16)

        @block.tensor
        def _(pe):
            pe.sem_inc(ps_free[0], 1)
            for first in (scores_ready, keyscores_ready):
                pe.sem_inc(first, 1)
            pe.sem_inc(ps_free[1], 1)

            def transposes(s, use, src, rows, n, ready):
                wait(pe, ps_free[s], use + 1)
                for k in range(n):
                    last = pe.transpose(flat(s)[:, k * P:k * P + rows], src(k), ident[0:rows, 0:rows])
                last.then_inc(ps_ready[s], 1)

            def project(s, use, j, slot, srcT, kt=KT):
                pe.wait_ge(ps_free[s], use + 1)
                for h in range(2):
                    for k in range(kt):
                        last = pe.matmul(ps[:, s, h, 0:HALF], wring[:, slot, k, j * P:(j + 1) * P],
                                         srcT[:, k, h * HALF:(h + 1) * HALF], start=(k == 0), stop=(k == kt - 1))
                last.then_inc(ps_ready[s], 1)

            pe.wait_ge(consts_made, 2)
            pe.wait_ge(pool_step, 2)
            for t in range(TT):
                rows = P if t < NT else NS
                pe.wait_ge(x_normed, t + 1)
                for s in range(2):
                    transposes(s, USE_X + t, lambda k: x_in[0:rows, t, (8 * s + k) * P:(8 * s + k + 1) * P], rows, 8, None)
            pe.wait_ge(hist_loaded, 32)
            for g in range(2):
                transposes(g, USE_HIST, lambda k: tails[0:4 * HIST, 1 + g, k * P:(k + 1) * P], 4 * HIST, CT, None)
            pe.wait_ge(normT_ready, 2 * TT)
            with pe.Fori(0, CT // 2) as i:
                for half in range(2):
                    pe.wait_ge(w_loaded[half], 16 * i + 16)
                    for j in range(2):
                        project(j, USE_CONV + 2 * i + half, j, half, normT)
            pe.wait_ge(tails_kept, 3 * CT // 2 + 1)
            for k, (s, use, n) in enumerate([(0, USE_TAIL, HIST), (1, USE_TAIL, 4 * HIST), (0, USE_TAIL + 1, 4 * HIST)]):
                at = (0, HIST, 5 * HIST)[k]
                pe.wait_ge(ps_free[s], use + 1)
                for c in range(CT):
                    last = pe.transpose(flat(s)[0:n, c * P:(c + 1) * P], hist[:, c, at:at + n], ident[:, :])
                last.then_inc(ps_ready[s], 1)
            pe.wait_ge(conv_kept, CT + 1)
            for s, use, src, ready in ((1, USE_MEAN1, conv, None), (0, USE_VAR0, sq_ln, sqln_ready)):
                pe.wait_ge(ps_free[s], use + 1)
                if ready is not None:
                    pe.wait_ge(ready, 1)
                for h in range(2):
                    for c in range(CT):
                        last = pe.matmul(ps[:, s, h, 0:HALF], ones[:, :], src[:, c, h * HALF:(h + 1) * HALF],
                                         start=(c == 0), stop=(c == CT - 1))
                last.then_inc(ps_ready[s], 1)
            pe.wait_ge(const_loaded, 16 * 13)
            pe.wait_ge(ps_free[1], USE_ZA1 + 1)
            for h in range(2):
                for k in range(KT):
                    last = pe.matmul(ps[0:RANK, 1, h, 0:HALF], wza[:, k, :], normT[:, k, h * HALF:(h + 1) * HALF],
                                     start=(k == 0), stop=(k == KT - 1))
            last.then_inc(ps_ready[1], 1)

            def project_tok(use, slot, srcT, kt=KT):
                for s in range(2):
                    pe.wait_ge(ps_free[s], use + 1)
                    for t in (range(NT) if s == 0 else [NT]):
                        n = span(t).stop - span(t).start
                        c0 = t * PAIR if s == 0 else 0
                        for k in range(kt):
                            last = pe.matmul(flat(s)[0:n, c0:c0 + PAIR], srcT[:, k, span(t)], wring[:, slot, k, :],
                                             start=(k == 0), stop=(k == kt - 1))
                    last.then_inc(ps_ready[s], 1)

            pe.wait_ge(wa2_loaded, 32)
            pe.wait_ge(za_ready, 1)
            with pe.Fori(0, HEADS) as h:
                u = head(h)
                for s in range(2):
                    wait(pe, ps_free[s], u + 1)
                    for t in (range(NT) if s == 0 else [NT]):
                        c0 = t * DK if s == 0 else 0
                        last = pe.matmul(flat(s)[:, c0:c0 + DK], zaT[:, t * P:(t + 1) * P], wa2[:, bass.ds(h * DK, DK)],
                                         start=True, stop=True)
                    last.then_inc(ps_ready[s], 1)
                for slot in range(2):
                    pe.wait_ge(w_loaded[slot], 48 * h + 80)
                    for j in range(2):
                        project(j, u + 1 + slot, j, slot, normT)
                pe.wait_ge(lg_ready, 2 * h + 2)
                for j in range(2):
                    pe.wait_ge(ps_free[j], u + 4)
                    for t in range(TT):
                        n = span(t).stop - span(t).start
                        last = pe.matmul(flat(j)[:, span(t)], lg[0:n, t, j * P:(j + 1) * P],
                                         tri[:, :] if t < NT else tri8[:, :], start=True, stop=True)
                    last.then_inc(ps_ready[j], 1)
                for slot in range(2):
                    pe.wait_ge(w_loaded[slot], 48 * h + 96)
                    project_tok(u + 4 + slot, slot, normT)

                def kd_and_scores(c):
                    n = span(c).stop - span(c).start
                    pe.wait_ge(decay_ready, TT * h + c + 1)
                    wait(pe, kd_ready, TT * h + c + 1)
                    for j in range(2):
                        last = pe.transpose(pm[0:n, 3, j * P:(j + 1) * P], kdec[:, j, 0:n], ident[:, :])
                    last.then_inc(kdT_ready, 1)
                    pe.wait_ge(factors_ready, TT * h + c + 1 + 1)
                    pe.wait_ge(att_ready, TT * h + c + 1)
                    sc = pm[:, 0:2, :].rearrange("p b (l t) -> p (b l) t", t=P)
                    for l, _ in levels(c) + [(NL, 0)]:
                        for j in range(2):
                            kk = kf[:, l, j, 0:n] if l < NL else kT[:, j, span(c)]
                            qq = qf[:, l, j, 0:n] if l < NL else qT[:, j, span(c)]
                            last = pe.matmul(sc[0:n, l, 0:n], kk, qq, start=(j == 0), stop=(j == 1))
                    last.then_inc(scores_ready, 1)

                for c in range(NT):
                    kd_and_scores(c)
                    if c % 2 == 0:
                        pe.wait_ge(w_loaded[c // 2], 48 * h + 112)
                    project(0, u + 6 + c, c % 2, c // 2, normT)
                    pe.wait_ge(v_ready, 4 * h + 4)
                    pe.wait_ge(att_ready, TT * h + c + 1 + 1)
                    pe.wait_ge(o_kept, TT * h + c + 1)
                    if c:
                        pe.wait_ge(state_ready, NT * h + c)
                    for e in range(4):
                        for j in range(2 if c else 0):
                            pe.matmul(pm[:, 2, e * P:(e + 1) * P], state[:, j, e * P:(e + 1) * P], qe[:, j, :],
                                      start=(j == 0), stop=False)
                        last = pe.matmul(pm[:, 2, e * P:(e + 1) * P], vt[:, c, e * P:(e + 1) * P], att[:, :],
                                         start=(c == 0), stop=True)
                    last.then_inc(o_ready, 1)
                    pe.wait_ge(kd_ready, TT * h + c + 1 + 1)
                    pe.wait_ge(ps_free[1], u + 7 + c)
                    for j in range(2):
                        last = pe.matmul(ps[:, 1, j, :], kd[:, j * P:(j + 1) * P], vt[:, c, :], start=True, stop=True)
                    last.then_inc(ps_ready[1], 1)
                kd_and_scores(NT)
                pe.wait_ge(att_ready, TT * h + TT + 1)
                pe.wait_ge(o_kept, TT * h + NT + 1)
                for e in range(4):
                    pe.matmul(pm[:, 2, e * P:e * P + NS], vt[0:NS, NT, e * P:(e + 1) * P], att[0:NS, 0:NS],
                              start=(e == 0), stop=False)
                for b in range(DEC_B):
                    pe.wait_ge(st_loaded[b % 4], 32 * h + 16 * (b // 4) + 16)
                    for e in range(4):
                        for j in range(2):
                            last = pe.matmul(pm[:, 2, e * P + b * DEC_S:e * P + (b + 1) * DEC_S],
                                             sring[:, b % 4, j, e * P:(e + 1) * P],
                                             qe[:, j, b * DEC_S:(b + 1) * DEC_S], start=False,
                                             stop=(b == DEC_B - 1 and e == 3 and j == 1))
                    if b == DEC_B - 1:
                        last.then_inc(o_ready, 1)
                    pe.wait_ge(kdm_ready, DEC_B * h + b + 1)
                    pe.wait_ge(ps_free[b % 2], u + 11 + b // 2)
                    for j in range(2):
                        last = pe.matmul(ps[:, b % 2, j, :], kdm[0:NS, b % 2, j * P:(j + 1) * P], vt[0:NS, NT, :],
                                         start=True, stop=True)
                    last.then_inc(ps_ready[b % 2], 1)
                pe.wait_ge(osq_ready, h + 1)
                for s in range(2):
                    pe.wait_ge(ps_free[s], u + 15)
                    for e in range(4):
                        last = pe.matmul(ps[:, s, 0, 0:HALF], ones[:, :], sq[:, e, s * HALF:(s + 1) * HALF],
                                         start=(e == 0), stop=(e == 3))
                    last.then_inc(ps_ready[s], 1)

            pe.wait_ge(conv_back, 16)
            pe.wait_ge(gla_ready, 4 * HEADS)
            with pe.Fori(0, D // PAIR) as i:
                for n, (src, kt) in enumerate(((normT, KT), (glaT, KT), (normT, KT), (convg, CT))):
                    pe.wait_ge(w_loaded[n % 2], 32 * i + 16 * (N_GATE // 2 + n // 2 + 1))
                    for j in range(2):
                        project(j, USE_GATE + 4 * i + n, j, n % 2, src, kt)
            pe.wait_ge(merged_ready, D // PAIR + 1)
            with pe.Fori(0, D // PAIR // 2) as i:
                for slot in range(2):
                    pe.wait_ge(w_loaded[slot], 16 * i + 16 * (N_MIX // 2 + 1))
                    project_tok(USE_MIX + 2 * i + slot, slot, merged)
            pe.wait_ge(ktab_loaded, 32)
            for half in range(2):
                last = pe.transpose(pm[:, 3, half * P:(half + 1) * P], ktab[:, half, :], ident[:, :])
            last.then_inc(kkT_ready, 1)
            for t in range(TT):
                rows = P if t < NT else NS
                pe.wait_ge(h2_ready, t + 1)
                for s in range(2):
                    transposes(s, USE_H2 + t, lambda k: h2[0:rows, t, (8 * s + k) * P:(8 * s + k + 1) * P], rows, 8, None)
            pe.wait_ge(h2T_ready, 2 * TT)
            pe.wait_ge(kk_ready, 1)
            for t in range(GT, TT):
                rows = P if t < NT else NS
                for s in range(2):
                    transposes(s, USE_RT + t - GT, lambda k: resid[0:rows, t, (8 * s + k) * P:(8 * s + k + 1) * P],
                               rows, 8, None)
            with pe.Fori(0, PH // 2) as i:
                for unit in range(UNITS):
                    hh, t = unit // TT, unit % TT
                    if t == 0:
                        pe.wait_ge(w_loaded[hh], 16 * i + 16 * (N_WQ // 2 + 1))
                        for j in range(2):
                            project(j, USE_WQ + 2 * i + hh, j, hh, normT)
                        pe.wait_ge(qp_ready, 4 * i + 2 * hh + 2)
                    wait(pe, routed, UNITS * i + max(unit - 3, 0) + 1)
                    rows = P if t < NT else NS
                    for half in range(2):
                        last = pe.matmul(pm[0:rows, unit % 4, half * NKEY:(half + 1) * NKEY],
                                         qp[:, hh, half, span(t)], kkT[:, half, :], start=True, stop=True)
                    last.then_inc(keyscores_ready, 1)
            pe.wait_ge(sel_ready, DT)
            for s, tiles in ((0, (0, 1)), (1, (2,))):
                pe.wait_ge(ps_free[s], USE_SEL + 1)
                for t in tiles:
                    rows = P if t < NT - GT else NS
                    for kind in range(3):
                        at = (3 * (t % 2) + kind) * P
                        last = pe.transpose(flat(s)[:, at:at + rows], seld[0:rows, t, kind, :], ident[0:rows, 0:rows])
                last.then_inc(ps_ready[s], 1)
            with pe.Fori(0, DN // (SET * SETS)) as r:
                for j in range(SETS):
                    wait(pe, gated_ready, SETS * r + j + 1)
                    wait(pe, ps_free[j % 2], USE_G + 4 * r + j // 2 + 1)
                    for n in range(SET):
                        last = pe.matmul(flat(j % 2)[:, n * P:(n + 1) * P], ohs[:, j % 2, 1, n, :],
                                         ohs[:, j % 2, 0, n, :], start=True, stop=True)
                    last.then_inc(ps_ready[j % 2], 1)

            def transpose_u(g, q):
                if q % 4 == 0:
                    wait(pe, u_loaded[q // 4], 16 * g + 16)
                wait(pe, ut_ready, QUADS * g + q - 1)
                for n in range(4):
                    kb = 4 * q + n
                    last = pe.transpose(pm[:, 2 + q % 2, n * P:(n + 1) * P],
                                        uraw[:, kb // KT, (kb % KT) * P:(kb % KT + 1) * P], ident[:, :])
                last.then_inc(tr_done, 1)

            def products_v(g, par, q):
                if q == 0:
                    wait(pe, wt_ready, g + 1)
                    wait(pe, v_loaded[par], 16 * (g - par) + 32)
                wait(pe, ps_free[q % 2], USE_V + 4 * g + q // 2 + 1)
                for h in range(2):
                    for b in range(2):
                        last = pe.matmul(ps[:, q % 2, h, 0:DN], vblock(par, b)[:, q, h * P:(h + 1) * P],
                                         WT[:, par, b, :], start=(b == 0), stop=(b == 1))
                last.then_inc(ps_ready[q % 2], 1)

            def dense(i, j, first=False, final=False):
                g = STEPS * i + j
                wait(pe, ut_ready, QUADS * g + QUADS)
                wait(pe, wt_ready, g)
                for b in range(2):
                    for k in range(KT):
                        last = pe.matmul(pm[:, b, 0:DN], UT[:, b * KT + k, :], h2T[:, k, :],
                                         start=(k == 0), stop=(k == KT - 1))
                last.then_inc(u_done, 1)
                for q in range(QUADS):
                    if not first:
                        products_v(g - 1, (j + 1) % 2, q)
                    if not final:
                        transpose_u(g + 1, q)

            for q in range(QUADS):
                transpose_u(0, q)
            for j in range(STEPS):
                dense(0, j, first=j == 0)
            with pe.Fori(1, PH - 1) as i:
                for j in range(STEPS):
                    dense(i, j)
            for j in range(STEPS):
                dense(PH - 1, j, final=j == STEPS - 1)
            for q in range(QUADS):
                products_v(NG - 1, 1, q)
            for s in range(2):
                pe.wait_ge(ps_free[s], USE_OUT + 1)
            for t in range(DT):
                rows = P if t < NT - GT else NS
                for s in range(2):
                    pe.wait_ge(ps_free[s], USE_OUT + t + 1)
                    for k in range(8):
                        last = pe.transpose(flat(s)[0:rows, k * P:(k + 1) * P], accT[:, 8 * s + k, t * P:t * P + rows],
                                            ident[:, :])
                    last.then_inc(ps_ready[s], 1)

        @block.scalar
        def _(act):
            step = Chain(act, act_step)
            for first in (conv_kept, kd_ready, o_kept, b_ready, softmax_ready):
                act.sem_inc(first, 1)
            junk = wring
            for t in range(TT):
                rows = P if t < NT else NS
                wait(act, x_loaded[t], 16)
                step(nc.scalar.activation(regB[0:rows, 0:D], x_in[0:rows, t, :], ACT.Square,
                                          accum_out=small[0:rows, t:t + 1]))
            for t in range(TT):
                rows = P if t < NT else NS
                wait(act, ss_ready, t + 1)
                nc.scalar.activation(small[0:rows, TT + t:TT + t + 1], small[0:rows, TT + t:TT + t + 1], ACT.Sqrt
                                     ).then_inc(rms_ready, 1)
            for g in range(2):
                wait(act, ps_ready[g], USE_HIST + 1)
                nc.scalar.activation(hist[:, :, HIST + 4 * HIST * g:HIST + 4 * HIST * (g + 1)],
                                     flat(g).rearrange("p (c t) -> p c t", c=CT)[:, :, 0:4 * HIST], ACT.Copy
                                     ).then_inc(hist_ready, 1)
            wait(act, hist_ready, 2)
            act.sem_inc(ps_free[0], 1)
            act.sem_inc(ps_free[1], 1)
            wait(act, const_loaded, 16 * 13)
            def gates(i):
                if not isinstance(i, int):
                    wait(act, gate_used, 6 * i)
                for j in range(2):
                    wait(act, ps_ready[j], USE_CONV + 2 * i + 1)
                    nc.scalar.activation(th(gate_s[:, j, :]), halves(j), ACT.Tanh, scale=0.5).then_inc(ps_free[j], 1)
                    wait(act, ps_free[j], USE_CONV + 2 * i + 2)
                    nc.scalar.activation(gate_s[:, j, :], gate_s[:, j, :], ACT.Copy, scale=0.5, bias=0.5
                                         ).then_inc(gate_ready, 1)

            def keep_sums(i):
                wait(act, conv_done, 4 * i + 4 + 1)
                for j in range(2):
                    nc.scalar.activation(conv[:, bass.ds(2 * i + j, 1), :], acc[:, j:j + 1, :], ACT.Identity,
                                         bias=bdw[:, bass.ds(2 * i + j, 1)]).then_inc(conv_kept, 1)

            def taps_of(i):
                nc.scalar.activation(wcur[:, :, :], wdw[:, bass.ds(2 * i, 2), :], ACT.Copy).then_inc(wcur_ready, 1)

            taps_of(0)
            gates(0)
            with act.Fori(1, CT // 2) as i:
                gates(i)
                keep_sums(i - 1)
                taps_of(i)
            keep_sums(CT // 2 - 1)
            for k, (s, use, n) in enumerate([(0, USE_TAIL, HIST), (1, USE_TAIL, 4 * HIST), (0, USE_TAIL + 1, 4 * HIST)]):
                wait(act, ps_ready[s], use + 1)
                nc.scalar.activation(tails[0:n, k, :], flat(s)[0:n, :], ACT.Copy).then_inc(tail_ready, 1)
                wait(act, tail_ready, k + 1)
                act.sem_inc(ps_free[s], 1)
            wait(act, ps_ready[1], USE_MEAN1 + 1)
            nc.scalar.activation(th(mean_s[:, :]), halves(1), ACT.Copy, scale=1.0 / CONV).then_inc(mean_ready, 1)
            wait(act, mean_ready, 1)
            act.sem_inc(ps_free[1], 1)
            wait(act, centered, 1)
            nc.scalar.activation(sq_ln[:, :, :], conv[:, :, :], ACT.Square).then_inc(sqln_ready, 1)
            wait(act, ps_ready[0], USE_VAR0 + 1)
            wait(act, sd_ready, 1)
            nc.scalar.activation(mean_s[:, :], mean_s[:, :], ACT.Sqrt).then_inc(sd_ready, 1)
            wait(act, lned, 1)
            for c in range(CT):
                nc.scalar.activation(conv[:, c, :], conv[:, c, :], ACT.Identity, scale=gln[:, c:c + 1],
                                     bias=bln[:, c:c + 1]).then_inc(affined, 1)
            wait(act, affined, CT)
            nc.scalar.activation(sq_ln[:, :, :], conv[:, :, :], ACT.Tanh, scale=0.5).then_inc(tanhed, 1)
            wait(act, ps_ready[1], USE_ZA1 + 1)
            wait(act, consts_made, 2)
            nc.scalar.activation(th(zaT[0:RANK, 0:TOK]), ps[0:RANK, 1, :, 0:HALF], ACT.Copy).then_inc(za_ready, 1)
            wait(act, za_ready, 1)
            act.sem_inc(ps_free[1], 1)

            wait(act, spilled, 16)
            wait(act, tail_stored, 48)
            total = step.base + step.n
            step.base, step.n = total, 0
            with act.Fori(0, HEADS) as h:
                step.enter(h, 2 * 2)
                u = head(h)
                parts = ((0, lg[:, 0:NT, :].rearrange("p t d -> p (t d)"), flat(0)),
                         (1, lg[0:NS, NT, :], flat(1)[0:NS, 0:DK]))
                wait(act, b_ready, 2 * h + 1)
                for s, dst, src in parts:
                    wait(act, ps_ready[s], u + 1)
                    step(nc.scalar.activation(dst, src, ACT.Abs))
                    step(nc.scalar.activation(dst, dst, ACT.Exp, scale=-1.0))
                    nc.scalar.activation(dst, dst, ACT.Ln, bias=1.0).then_inc(lgabs_ready, 1)
                wait(act, factors_ready, TT * h + 1)
                wait(act, scores_ready, TT * h + 1)
                for s in range(2):
                    wait(act, ps_ready[s], u + 2)
                    nc.scalar.activation(th(kT[:, s, :]), halves(s), ACT.Copy).then_inc(k_ready, 1)
                    wait(act, k_ready, 2 * h + s + 1)
                    act.sem_inc(ps_free[s], 1)
                for s in range(2):
                    wait(act, ps_ready[s], u + 3)
                    nc.scalar.activation(th(qT[:, s, :]), halves(s), ACT.Copy, scale=DK ** -0.5).then_inc(q_ready, 1)
                    wait(act, q_ready, 2 * h + s + 1)
                    act.sem_inc(ps_free[s], 1)
                for s in range(2):
                    wait(act, ps_ready[s], u + 4)
                    nc.scalar.activation(bT[:, s, :], flat(s)[:, 0:TOK], ACT.Copy).then_inc(b_ready, 1)
                    wait(act, b_ready, 2 * h + s + 1 + 1)
                    act.sem_inc(ps_free[s], 1)

                def decays(c):
                    wait(act, earg_ready, TT * h + c + 1)
                    nc.scalar.activation(earg[:, 0:2 * NL, :, :] if c < NT else earg[:, 8:14, :, 0:NS // 2],
                                         earg[:, 0:2 * NL, :, :] if c < NT else earg[:, 8:14, :, 0:NS // 2],
                                         ACT.Exp).then_inc(exp_ready, 1)
                    n = span(c).stop - span(c).start
                    if c:
                        wait(act, o_ready, TT * h + c)
                        wait(act, kdT_ready, TT * h + c)
                        wait(act, state_ready, NT * h + c)
                    nc.scalar.activation(qe[:, :, 0:n], bT[:, :, span(c)], ACT.Exp).then_inc(exp_ready, 1)
                    if c < NT:
                        for j in range(2):
                            e = span(c).stop
                            nc.scalar.activation(kdec[:, j, :], bT[:, j, span(c)], ACT.Exp, scale=-1.0,
                                                 bias=bT[:, j, e - 1:e]).then_inc(exp_ready, 1)
                        nc.scalar.activation(dec[:, :, 0:1], bT[:, :, span(c).stop - 1:span(c).stop], ACT.Exp
                                             ).then_inc(exp_ready, 1)
                    else:
                        wait(act, kdarg_ready, h + 1)
                        nc.scalar.activation(kdec[:, :, 0:NS], kdec[:, :, 0:NS], ACT.Exp).then_inc(exp_ready, 1)
                        nc.scalar.activation(dec[:, :, :],
                                             bT[:, :, SEQ:].rearrange("p j (b t) -> p j b t", b=DEC_B)[:, :, :, DEC_S - 1],
                                             ACT.Exp).then_inc(exp_ready, 1)

                def v_keep(p):
                    wait(act, ps_ready[0], u + 5 + p)
                    nc.scalar.activation(vt[:, 0:NT, p * PAIR:(p + 1) * PAIR],
                                         flat(0).rearrange("p (t c) -> p t c", t=NT), ACT.Copy).then_inc(v_ready, 1)
                    wait(act, v_ready, 4 * h + 2 * p + 1)
                    act.sem_inc(ps_free[0], 1)
                    wait(act, ps_ready[1], u + 5 + p)
                    nc.scalar.activation(vt[0:NS, NT, p * PAIR:(p + 1) * PAIR], flat(1)[0:NS, 0:PAIR], ACT.Copy
                                         ).then_inc(v_ready, 1)
                    wait(act, v_ready, 4 * h + 2 * p + 2)
                    act.sem_inc(ps_free[1], 1)

                def kd_keep(c):
                    n = span(c).stop - span(c).start
                    wait(act, kdT_ready, TT * h + c + 1)
                    nc.scalar.activation(kd[0:n, :], pm[0:n, 3, 0:DK], ACT.Copy).then_inc(kd_ready, 1)

                def o_keep(c):
                    n = span(c).stop - span(c).start
                    wait(act, o_ready, TT * h + c + 1)
                    nc.scalar.activation(glaT[:, bass.ds(4 * h, 4), span(c)],
                                         pm[:, 2, :].rearrange("p (e t) -> p e t", e=4)[:, :, 0:n], ACT.Copy
                                         ).then_inc(o_kept, 1)

                decays(0)
                v_keep(0)
                v_keep(1)
                for c in range(NT):
                    kd_keep(c)
                    wait(act, ps_ready[0], u + 7 + c)
                    nc.scalar.activation(th(rs[:, c, :]), halves(0), ACT.Tanh, scale=0.5).then_inc(rtanh_ready, 1)
                    o_keep(c)
                    decays(c + 1)
                kd_keep(NT)
                o_keep(NT)
                wait(act, o_kept, TT * h + TT + 1)
                wait(act, ps_ready[1], u + 14)
                nc.scalar.activation(sq[:, :, :], glaT[:, bass.ds(4 * h, 4), :], ACT.Square).then_inc(osq_ready, 1)
                for s in range(2):
                    wait(act, ps_ready[s], u + 15)
                    nc.scalar.activation(rms[:, s * HALF:(s + 1) * HALF], ps[:, s, 0, 0:HALF], ACT.Copy,
                                         scale=1.0 / DV, bias=EPS).then_inc(rms_done, 1)
                    wait(act, rms_done, 3 * h + s + 1)
                    act.sem_inc(ps_free[s], 1)
                nc.scalar.activation(rms[:, :], rms[:, :], ACT.Sqrt).then_inc(rms_done, 1)
            step.leave(HEADS)
            wait(act, gla_ready, 4 * HEADS)
            wait(act, stores_done, HEADS + 1)
            with act.Fori(0, D // PAIR) as i:
                for n, (dst, ready, used) in enumerate(((gsigB, gateB_ready, mergedB_ready),
                                                        (gsigA, gateA_ready, part_ready))):
                    wait(act, used, 2 * i + 1)
                    for j in range(2):
                        wait(act, ps_ready[j], USE_GATE + 4 * i + 2 * n + 1)
                        nc.scalar.activation(th(dst[:, j, :]), halves(j), ACT.Tanh, scale=0.5).then_inc(ready, 1)
                        wait(act, ready, 2 * i + j + 1)
                        act.sem_inc(ps_free[j], 1)
            wait(act, kkT_ready, 1)
            nc.scalar.activation(kkT[:, :, :].rearrange("p a b -> p (a b)"), pm[:, 3, 0:2 * P], ACT.Copy
                                 ).then_inc(kk_ready, 1)
            for t in range(TT):
                rows = P if t < NT else NS
                wait(act, resid_ready, 16)
                if t:
                    wait(act, ss2_done, t)
                nc.scalar.activation(squares[0:rows, :], resid[0:rows, t, :], ACT.Square,
                                     accum_out=small[0:rows, t:t + 1]).then_inc(ss2_done, 1)
            for t in range(TT):
                rows = P if t < NT else NS
                wait(act, ms2_ready, t + 1)
                nc.scalar.activation(small[0:rows, TT + t:TT + t + 1], small[0:rows, TT + t:TT + t + 1], ACT.Sqrt
                                     ).then_inc(rms2_ready, 1)
            for t in range(TT):
                rows = P if t < NT else NS
                for s in range(2):
                    wait(act, ps_ready[s], USE_H2 + t + 1)
                    nc.scalar.activation(normT[:, 8 * s:8 * s + 8, span(t)],
                                         flat(s).rearrange("p (k t) -> p k t", k=8)[:, :, 0:rows], ACT.Copy
                                         ).then_inc(h2T_ready, 1)
                    wait(act, h2T_ready, 2 * t + s + 1)
                    act.sem_inc(ps_free[s], 1)

            for t in range(DT):
                rows = P if t < NT - GT else NS
                for s in range(2):
                    wait(act, ps_ready[s], USE_RT + t + 1)
                    nc.scalar.activation(accT[:, 8 * s:8 * s + 8, t * P:t * P + rows],
                                         flat(s).rearrange("p (k t) -> p k t", k=8)[:, :, 0:rows], ACT.Copy
                                         ).then_inc(accT_ready, 1)
                    wait(act, accT_ready, 2 * t + s + 1)
                    act.sem_inc(ps_free[s], 1)

            def queries(i, hh):
                wait(act, keyscores_ready, UNITS * i + 1)
                for j in range(2):
                    wait(act, ps_ready[j], USE_WQ + 2 * i + hh + 1)
                    nc.scalar.activation(th(qp[:, hh, j, :]), halves(j), ACT.Copy).then_inc(qp_ready, 1)
                    wait(act, qp_ready, 4 * i + 2 * hh + j + 1)
                    act.sem_inc(ps_free[j], 1)

            with act.Fori(0, PH // 2) as i:
                queries(i, 0)
                for unit in range(UNITS):
                    hh, t = unit // TT, unit % TT
                    rows = P if t < NT else NS
                    cols = bass.ds((2 * i + hh) * TOPK, TOPK)
                    wait(act, negmax_ready, UNITS * i + unit + 1)
                    nc.scalar.activation(gall[:, t, cols] if t < GT else seld[0:rows, t - GT, 2, cols],
                                         cs[0:rows, 0:TOPK], ACT.Exp, bias=cs[0:rows, TOPK:TOPK + 1]
                                         ).then_inc(softmax_ready, 1)
                    if unit == 0:
                        queries(i, 1)
            for t in range(DT):
                rows = P if t < NT - GT else NS
                wait(act, ps_ready[t // 2], USE_SEL + 1)
                at = 3 * (t % 2) * P
                nc.scalar.activation(selT[:, :, t * P:t * P + rows],
                                     flat(t // 2)[:, at:at + 3 * P].rearrange("p (k n) -> p k n", k=3)[:, :, 0:rows],
                                     ACT.Copy).then_inc(selT_ready, 1)
            wait(act, selT_ready, DT)
            for s in range(2):
                act.sem_inc(ps_free[s], 1)
            with act.Fori(0, DN // (SET * SETS)) as r:
                for j in range(SETS):
                    st = j // 4
                    if j % 4 == 0:
                        wait(act, stage_free, 2 * r + st + 1)
                    wait(act, ps_ready[j % 2], USE_G + 4 * r + j // 2 + 1)
                    nc.scalar.activation(stage[st][:, :, SET * (j % 4):SET * (j % 4) + SET],
                                         flat(j % 2).rearrange("p (n i) -> p i n", n=SET), ACT.Copy
                                         ).then_inc(g_staged, 1)
                    wait(act, g_staged, SETS * r + j + 1)
                    act.sem_inc(ps_free[j % 2], 1)

            def keep_u(g, q):
                wait(act, tr_done, QUADS * g + q + 1)
                nc.scalar.activation(UT[:, 4 * q:4 * q + 4, :].rearrange("p n e -> p (n e)"), pm[:, 2 + q % 2, :],
                                     ACT.Copy).then_inc(ut_ready, 1)

            def gelu(i, j, final=False):
                g = STEPS * i + j
                wait(act, u_done, g + 1)
                nc.scalar.activation(x2[:, :, :], pm[:, 0:2, 0:DN], ACT.Square, scale=float(np.sqrt(0.044715))
                                     ).then_inc(sq_ready, 1)
                for q in range(QUADS):
                    if not final:
                        keep_u(g + 1, q)
                    if q == 1:
                        wait(act, arg_ready, g + 1)
                        nc.scalar.activation(x2[:, :, :], x2[:, :, :], ACT.Tanh, scale=float(np.sqrt(2.0 / np.pi))
                                             ).then_inc(tanh_ready, 1)
                if j % 4 == 1:
                    wait(act, gelu_arg, GT * i + j // 4 + 1)
                    nc.scalar.activation(gelu_t, gelu_t, ACT.Tanh, scale=float(np.sqrt(2.0 / np.pi))
                                         ).then_inc(gelu_tanh, 1)

            wait(act, stage_free, NST + 2)
            for q in range(QUADS):
                keep_u(0, q)
            for j in range(STEPS):
                gelu(0, j)
            with act.Fori(1, PH - 1) as i:
                for j in range(STEPS):
                    gelu(i, j)
            for j in range(STEPS):
                gelu(PH - 1, j, final=j == STEPS - 1)
            for t in range(DT):
                rows = P if t < NT - GT else NS
                for s in range(2):
                    wait(act, ps_ready[s], USE_OUT + t + 1)
                    nc.scalar.activation(resid[0:rows, GT + t, s * D // 2:(s + 1) * D // 2], flat(s)[0:rows, :],
                                         ACT.Copy).then_inc(back_ready, 1)
                    wait(act, back_ready, 2 * t + s + 1)
                    act.sem_inc(ps_free[s], 1)
            wait(act, peer_done, 1)
            for t in range(TT):
                rows = P if t < NT else NS
                if t:
                    wait(act, ss3_done, t)
                nc.scalar.activation(ring[0:rows, 0, :], resid[0:rows, t, :], ACT.Square,
                                     accum_out=small[0:rows, t:t + 1]).then_inc(ss3_done, 1)
            for t in range(TT):
                rows = P if t < NT else NS
                wait(act, ms3_ready, t + 1)
                nc.scalar.activation(small[0:rows, TT + t:TT + t + 1], small[0:rows, TT + t:TT + t + 1], ACT.Sqrt
                                     ).then_inc(rms3_ready, 1)

        @block.vector
        def _(dve):
            step = Chain(dve, dve_step)
            for first in (conv_done, att_ready, factors_ready, mergedB_ready, part_ready, merged_ready, routed):
                dve.sem_inc(first, 1)
            for t in range(TT):
                rows = P if t < NT else NS
                dve.wait_ge(act_step, t + 1)
                dve.tensor_scalar(small[0:rows, TT + t:TT + t + 1], small[0:rows, t:t + 1], 1.0 / D, EPS,
                                  ALU.mult, ALU.add).then_inc(ss_ready, 1)
                dve.wait_ge(rms_ready, t + 1)
                step(dve.reciprocal(small[0:rows, 2 * TT + t:2 * TT + t + 1], small[0:rows, TT + t:TT + t + 1]))
                dve.tensor_scalar(x_in[0:rows, t, :], x_in[0:rows, t, :], small[0:rows, 2 * TT + t:2 * TT + t + 1],
                                  None, ALU.mult).then_inc(x_normed, 1)
            dve.wait_ge(g1_loaded, 16)
            for t in range(TT):
                rows = P if t < NT else NS
                for s in range(2):
                    dve.wait_ge(ps_ready[s], USE_X + t + 1)
                    dve.tensor_tensor(normT[:, 8 * s:8 * s + 8, t * P:t * P + rows],
                                      flat(s).rearrange("p (k t) -> p k t", k=8)[:, :, 0:rows],
                                      g1[:, 8 * s:8 * s + 8].unsqueeze(2).to_broadcast([P, 8, rows]), ALU.mult
                                      ).then_inc(normT_ready, 1)
                    dve.wait_ge(normT_ready, 2 * t + s + 1)
                    dve.sem_inc(ps_free[s], 1)
            per = 6 + 4 * TAPS
            with dve.Fori(0, CT // 2) as i:
                uv = uext[:, :, HIST + SEQ:].rearrange("p q (b t) -> p q b t", b=DEC_B)
                b0 = SEQ - HALF
                for j in range(2):
                    dve.wait_ge(gate_ready, 2 * i + j + 1)
                    dve.wait_ge(ps_ready[j], USE_CONV + 2 * i + 2)
                    if j == 0:
                        dve.wait_ge(tails_kept, 3 * i + 1)
                        dve.wait_ge(conv_done, 4 * i + 1)
                    dve.tensor_tensor(uext[:, j, HIST:HIST + HALF], gate_s[:, j, 0:HALF], ps[:, j, 0, 0:HALF],
                                      ALU.mult).then_inc(u_ready, 1)
                    dve.tensor_tensor(uext[:, j, HIST + HALF:HIST + SEQ], gate_s[:, j, HALF:SEQ], ps[:, j, 1, 0:b0],
                                      ALU.mult).then_inc(u_ready, 1)
                    dve.tensor_tensor(uv[:, j, :, HIST:], gate_s[:, j, SEQ:].rearrange("p (b t) -> p b t", b=DEC_B),
                                      ps[:, j, 1, b0:HALF].rearrange("p (b t) -> p b t", b=DEC_B), ALU.mult
                                      ).then_inc(u_ready, 1)
                    dve.wait_ge(u_ready, 6 * i + 3 * j + 3)
                    dve.sem_inc(ps_free[j], 1)
                dve.sem_inc(gate_used, 6)
                dve.wait_ge(uext_hist, 3 * i + 3)
                dve.wait_ge(wcur_ready, i + 1)
                dve.wait_ge(conv_kept, 2 * i + 1)
                for tap in range(TAPS):
                    for q in range(4):
                        j, sample = q % 2, q // 2
                        out = acc[:, j, SEQ:].rearrange("p (b t) -> p b t", b=DEC_B) if sample else acc[:, j, 0:SEQ]
                        src = uv[:, j, :, tap:tap + DEC_S] if sample else uext[:, j, tap:tap + SEQ]
                        n = 4 * tap + q
                        if tap:
                            dve.wait_ge(dve_step, TT + i * 4 * (TAPS - 1) + n - 3)
                            ins = dve.scalar_tensor_tensor(out=out, in0=src, scalar=wcur[:, j, tap:tap + 1], in1=out,
                                                           op0=ALU.mult, op1=ALU.add)
                        else:
                            ins = dve.tensor_scalar(out, src, wcur[:, j, tap:tap + 1], None, ALU.mult)
                        ins.then_inc(conv_done if tap == TAPS - 1 else dve_step, 1)
            dve.wait_ge(mean_ready, 1)
            dve.wait_ge(conv_kept, CT + 1)
            dve.tensor_tensor(conv[:, :, :], conv[:, :, :], mean_s[:, :].unsqueeze(1).to_broadcast([P, CT, TOK]),
                              ALU.subtract).then_inc(centered, 1)
            dve.wait_ge(ps_ready[0], USE_VAR0 + 1)
            dve.wait_ge(centered, 1)
            dve.tensor_scalar(th(mean_s[:, :]), halves(0), 1.0 / CONV, EPS, ALU.mult, ALU.add).then_inc(sd_ready, 1)
            dve.wait_ge(sd_ready, 2)
            dve.sem_inc(ps_free[0], 1)
            base = TT + CT // 2 * 4 * (TAPS - 1)
            dve.reciprocal(mean_s[:, :], mean_s[:, :]).then_inc(dve_step, 1)
            dve.wait_ge(dve_step, base + 1)
            dve.tensor_tensor(conv[:, :, :], conv[:, :, :], mean_s[:, :].unsqueeze(1).to_broadcast([P, CT, TOK]),
                              ALU.mult).then_inc(lned, 1)
            dve.wait_ge(tanhed, 1)
            dve.scalar_tensor_tensor(out=conv[:, :, :], in0=sq_ln[:, :, :], scalar=1.0, in1=conv[:, :, :],
                                     op0=ALU.add, op1=ALU.mult).then_inc(silu_ready, 1)

            dve.wait_ge(spilled, 16)
            dve.wait_ge(tail_stored, 48)
            dve.wait_ge(za_ready, 1)
            dve.wait_ge(masks_made, 1)
            step.base, step.n = base + 1, 0
            with dve.Fori(0, HEADS) as h:
                step.enter(h, TT + 3 + 2)
                u = head(h)
                for s, dst, src in ((0, lg[:, 0:NT, :].rearrange("p t d -> p (t d)"), flat(0)),
                                    (1, lg[0:NS, NT, :], flat(1)[0:NS, 0:DK])):
                    dve.wait_ge(lgabs_ready, 2 * h + s + 1)
                    dve.scalar_tensor_tensor(out=dst, in0=src, scalar=0.0, in1=dst, op0=ALU.min, op1=ALU.subtract
                                             ).then_inc(lg_ready, 1)
                    dve.wait_ge(lg_ready, 2 * h + s + 1)
                    dve.sem_inc(ps_free[s], 1)
                dve.wait_ge(b_ready, 2 * h + 2 + 1)

                def views(x, c, w):
                    g = (P if c < NT else NS) // (2 * w)
                    return x.rearrange("p j (g u w) -> p j g u w", g=g, u=2)

                def arguments(c):
                    n = span(c).stop - span(c).start
                    for l, w in levels(c):
                        bv = views(bT[:, :, span(c)], c, w)
                        piv = bv[:, :, :, 0, w - 1:w].to_broadcast([P, 2, n // (2 * w), w])
                        eq = earg[:, 2 * l, :, 0:n // 2].rearrange("p j (g w) -> p j g w", w=w)
                        ek = earg[:, 2 * l + 1, :, 0:n // 2].rearrange("p j (g w) -> p j g w", w=w)
                        dve.tensor_tensor(eq, bv[:, :, :, 1, :], piv, ALU.subtract)
                        last = dve.tensor_tensor(ek, piv, bv[:, :, :, 0, :], ALU.subtract)
                    last.then_inc(earg_ready, 1)
                    if c == NT:
                        dve.wait_ge(kdT_ready, TT * h + c)
                        bb = bT[:, :, SEQ:].rearrange("p j (b t) -> p j b t", b=DEC_B)
                        dve.tensor_tensor(kdec[:, :, 0:NS].rearrange("p j (b t) -> p j b t", b=DEC_B),
                                          bb[:, :, :, DEC_S - 1:DEC_S].to_broadcast([P, 2, DEC_B, DEC_S]), bb,
                                          ALU.subtract).then_inc(kdarg_ready, 1)

                def factors(c):
                    n = span(c).stop - span(c).start
                    e = 5 * NT * h + 4 * h + 5 * c
                    dve.wait_ge(scores_ready, TT * h + c + 1)
                    dve.wait_ge(exp_ready, e + 1)
                    for l, w in levels(c):
                        eq = earg[:, 2 * l, :, 0:n // 2].rearrange("p j (g w) -> p j g w", w=w)
                        ek = earg[:, 2 * l + 1, :, 0:n // 2].rearrange("p j (g w) -> p j g w", w=w)
                        dve.tensor_tensor(views(qf[:, l, :, 0:n], c, w)[:, :, :, 1, :], eq,
                                          views(qT[:, :, span(c)], c, w)[:, :, :, 1, :], ALU.mult)
                        last = dve.tensor_tensor(views(kf[:, l, :, 0:n], c, w)[:, :, :, 0, :], ek,
                                                 views(kT[:, :, span(c)], c, w)[:, :, :, 0, :], ALU.mult)
                    last.then_inc(factors_ready, 1)
                    dve.wait_ge(exp_ready, e + (5 if c < NT else 4))
                    dve.tensor_tensor(qe[:, :, 0:n], qe[:, :, 0:n], qT[:, :, span(c)], ALU.mult)
                    dve.tensor_tensor(kdec[:, :, 0:n], kdec[:, :, 0:n], kT[:, :, span(c)], ALU.mult
                                      ).then_inc(decay_ready, 1)

                def attention(c):
                    n = span(c).stop - span(c).start
                    lo = levels(c)[0][0]
                    sc = pm[:, 0:2, :].rearrange("p b (l t) -> p (b l) t", t=P)
                    dve.wait_ge(scores_ready, TT * h + c + 1 + 1)
                    dve.wait_ge(factors_ready, TT * h + c + 1 + 1)
                    step(dve.tensor_tensor(masked[0:n, lo:NL + 1, 0:n], sc[0:n, lo:NL + 1, 0:n],
                                           mask[0:n, lo:NL + 1, 0:n], ALU.mult))
                    if c:
                        dve.wait_ge(o_ready, TT * h + c)
                    dve.tensor_reduce(att[0:n, 0:n], masked[0:n, lo:NL + 1, 0:n].rearrange("p l t -> p t l"), AX.X,
                                      ALU.add).then_inc(att_ready, 1)
                    dve.wait_ge(att_ready, TT * h + c + 1 + 1)

                dve.wait_ge(q_ready, 2 * h + 2)
                dve.wait_ge(k_ready, 2 * h + 2)
                arguments(0)
                factors(0)
                for c in range(NT):
                    attention(c)
                    arguments(c + 1)
                    dve.wait_ge(rtanh_ready, 4 * h + c + 1)
                    dve.scalar_tensor_tensor(out=th(rs[:, c, :]), in0=th(rs[:, c, :]), scalar=1.0, in1=halves(0),
                                             op0=ALU.add, op1=ALU.mult).then_inc(rsilu_ready, 1)
                    dve.wait_ge(rsilu_ready, 4 * h + c + 1)
                    dve.sem_inc(ps_free[0], 1)
                    dve.wait_ge(ps_ready[1], u + 7 + c)
                    if c == 0:
                        dve.wait_ge(stores_done, h + 1)
                        dve.tensor_copy(state[:, :, :], ps[:, 1, :, :]).then_inc(state_ready, 1)
                    else:
                        step(dve.scalar_tensor_tensor(out=state[:, 0, :], in0=state[:, 0, :], scalar=dec[:, 0, 0:1],
                                                      in1=ps[:, 1, 0, :], op0=ALU.mult, op1=ALU.add))
                        dve.scalar_tensor_tensor(out=state[:, 1, :], in0=state[:, 1, :], scalar=dec[:, 1, 0:1],
                                                 in1=ps[:, 1, 1, :], op0=ALU.mult, op1=ALU.add
                                                 ).then_inc(state_ready, 1)
                    dve.wait_ge(state_ready, NT * h + c + 1)
                    dve.sem_inc(ps_free[1], 1)
                    factors(c + 1)
                attention(NT)
                dve.wait_ge(kd_ready, TT * h + TT + 1)
                for b in range(DEC_B):
                    if b >= 2:
                        dve.wait_ge(ps_ready[b % 2], u + 10 + b // 2)
                    dve.tensor_scalar(kdm[0:NS, b % 2, :], kd[0:NS, :], bmask[:, b:b + 1], None, ALU.mult
                                      ).then_inc(kdm_ready, 1)
                    dve.wait_ge(ps_ready[b % 2], u + 11 + b // 2)
                    for j in range(2):
                        dve.scalar_tensor_tensor(out=sring[:, b % 4, j, :], in0=sring[:, b % 4, j, :],
                                                 scalar=dec[:, j, b:b + 1], in1=ps[:, b % 2, j, :], op0=ALU.mult,
                                                 op1=ALU.add).then_inc(st_updated, 1)
                    dve.wait_ge(st_updated, 2 * DEC_B * h + 2 * b + 2)
                    dve.sem_inc(ps_free[b % 2], 1)
                dve.wait_ge(rms_done, 3 * h + 3)
                step(dve.reciprocal(rms[:, :], rms[:, :]))
                step(dve.tensor_tensor(rs[:, :, :], rs[:, :, :], rms[:, :].unsqueeze(1).to_broadcast([P, 4, TOK]),
                                       ALU.mult))
                for e in range(4):
                    dve.scalar_tensor_tensor(out=glaT[:, bass.ds(4 * h + e, 1), :].rearrange("p a t -> p (a t)"),
                                             in0=glaT[:, bass.ds(4 * h + e, 1), :].rearrange("p a t -> p (a t)"),
                                             scalar=ggla[:, bass.ds(4 * h + e, 1)], in1=rs[:, e, :],
                                             op0=ALU.mult, op1=ALU.mult).then_inc(gla_ready, 1)
                dve.wait_ge(gla_ready, 4 * h + 4)
            step.leave(HEADS)
            dve.wait_ge(stores_done, HEADS + 1)
            with dve.Fori(0, D // PAIR) as i:
                for n, (gate, ready, done) in enumerate(((gsigB, gateB_ready, mergedB_ready),
                                                         (gsigA, gateA_ready, part_ready))):
                    if n:
                        dve.wait_ge(merged_ready, i + 1)
                    for j in range(2):
                        dve.wait_ge(ready, 2 * i + j + 1)
                        dve.wait_ge(ps_ready[j], USE_GATE + 4 * i + 2 * n + 2)
                        dst = th(part[:, j, :]) if n else merged[:, bass.ds(2 * i + j, 1), :].rearrange(
                            "p a (b n) -> p (a b) n", b=2)
                        dve.scalar_tensor_tensor(out=dst, in0=th(gate[:, j, :]), scalar=1.0, in1=halves(j),
                                                 op0=ALU.add, op1=ALU.mult).then_inc(done, 1)
                        dve.wait_ge(done, 2 * i + j + 1 + 1)
                        dve.sem_inc(ps_free[j], 1)
                dve.tensor_tensor(merged[:, bass.ds(2 * i, 2), :], merged[:, bass.ds(2 * i, 2), :], part[:, :, :],
                                  ALU.add).then_inc(merged_ready, 1)
            dve.wait_ge(resid_loaded, 32)
            with dve.Fori(0, D // PAIR) as i:
                for s, rows, dst, src in ((0, P, resid[:, 0:NT, bass.ds(i * PAIR, PAIR)],
                                           flat(0).rearrange("p (t c) -> p t c", t=NT)),
                                          (1, NS, resid[0:NS, NT, bass.ds(i * PAIR, PAIR)], flat(1)[0:NS, 0:PAIR])):
                    dve.wait_ge(ps_ready[s], USE_MIX + i + 1)
                    dve.scalar_tensor_tensor(out=dst, in0=src, scalar=0.25, in1=dst, op0=ALU.mult, op1=ALU.add
                                             ).then_inc(resid_ready, 1)
                    dve.wait_ge(resid_ready, 2 * i + s + 1)
                    dve.sem_inc(ps_free[s], 1)
            dve.wait_ge(g2_loaded, 16)
            for t in range(TT):
                rows = P if t < NT else NS
                dve.wait_ge(ss2_done, t + 1)
                dve.tensor_scalar(small[0:rows, TT + t:TT + t + 1], small[0:rows, t:t + 1], 1.0 / D, EPS,
                                  ALU.mult, ALU.add).then_inc(ms2_ready, 1)
            dve.wait_ge(rms2_ready, TT)
            for t in range(TT):
                rows = P if t < NT else NS
                step(dve.reciprocal(small[0:rows, 2 * TT + t:2 * TT + t + 1], small[0:rows, TT + t:TT + t + 1]))
                dve.scalar_tensor_tensor(out=h2[0:rows, t, :], in0=resid[0:rows, t, :],
                                         scalar=small[0:rows, 2 * TT + t:2 * TT + t + 1], in1=g2[0:rows, :],
                                         op0=ALU.mult, op1=ALU.mult).then_inc(h2_ready, 1)
            dve.wait_ge(h2_ready, TT)
            dve.wait_ge(kk_ready, 1)

            def route(i, unit):
                hh, t = unit // TT, unit % TT
                n = P if t < NT else NS
                cols = bass.ds((2 * i + hh) * TOPK, TOPK)
                wait(dve, keyscores_ready, UNITS * i + unit + 1 + 1)
                sc = pm[0:n, unit % 4, 0:2 * NKEY].rearrange("p (a n) -> p a n", a=2)
                for a_ in range(2):
                    step.mark(dve.max(v12[0:n, a_, 0:8], sc[:, a_, :]))
                for a_ in range(2):
                    step.wait(1)
                    step.mark(dve.max_index(i12[0:n, a_, 0:8], v12[0:n, a_, 0:8], sc[:, a_, :]))
                for a_ in range(2):
                    step.mark(dve.match_replace(sc2[0:n, a_, :], v12[0:n, a_, 0:8], sc[:, a_, :], NEG))
                for a_ in range(2):
                    step.wait(1)
                    step.mark(dve.max(v12[0:n, a_, 8:16], sc2[0:n, a_, :]))
                for a_ in range(2):
                    step.wait(1)
                    step.mark(dve.max_index(i12[0:n, a_, 8:16], v12[0:n, a_, 8:16], sc2[0:n, a_, :]))
                step(dve.tensor_tensor(cand[0:n, :, :], v12[0:n, 0, :].unsqueeze(2).to_broadcast([n, TOPK, TOPK]),
                                       v12[0:n, 1, :].unsqueeze(1).to_broadcast([n, TOPK, TOPK]), ALU.add))
                wait(dve, softmax_ready, UNITS * i + unit + 1)
                flatc = cand[0:n, :, :].rearrange("p a b -> p (a b)")
                step(dve.max(cs[0:n, 0:8], flatc))
                step.mark(dve.max_index(ci[0:n, 0:8], cs[0:n, 0:8], flatc))
                step(dve.match_replace(cand2[0:n, :], cs[0:n, 0:8], flatc, NEG))
                step(dve.max(cs[0:n, 8:16], cand2[0:n, :]))
                dve.tensor_scalar(cs[0:n, TOPK:TOPK + 1], cs[0:n, 0:1], -1.0, None, ALU.mult
                                  ).then_inc(negmax_ready, 1)
                step(dve.max_index(ci[0:n, 8:16], cs[0:n, 8:16], cand2[0:n, :]))
                step.mark(dve.tensor_copy(i12f[0:n, :, :], i12[0:n, :, :]))
                step.mark(dve.tensor_scalar(abi[0:n, 0, :], ci[0:n, :], 4, None, ALU.logical_shift_right))
                step(dve.tensor_scalar(abi[0:n, 1, :], ci[0:n, :], TOPK - 1, None, ALU.bitwise_and))
                step(dve.tensor_copy(ab[0:n, :, :], abi[0:n, :, :]))
                for a_ in range(2):
                    step(dve.tensor_tensor(oh[0:n, :, :], ab[0:n, a_, :].unsqueeze(2).to_broadcast([n, TOPK, TOPK]),
                                           iota16[0:n, :].unsqueeze(1).to_broadcast([n, TOPK, TOPK]), ALU.is_equal))
                    step(dve.tensor_tensor(oh[0:n, :, :], oh[0:n, :, :],
                                           i12f[0:n, a_, :].unsqueeze(1).to_broadcast([n, TOPK, TOPK]), ALU.mult))
                    step(dve.tensor_reduce(esel[0:n, a_, :], oh[0:n, :, :], AX.X, ALU.add))
                if t < GT:
                    dve.scalar_tensor_tensor(out=idxs[:, t, cols], in0=esel[:, 0, :], scalar=float(NKEY),
                                             in1=esel[:, 1, :], op0=ALU.mult, op1=ALU.add).then_inc(routed, 1)
                else:
                    dve.tensor_tensor(seld[0:n, t - GT, 0:2, cols], esel[0:n, :, :],
                                      ones[0:n, 0:2 * TOPK].rearrange("p (a k) -> p a k", a=2), ALU.mult
                                      ).then_inc(routed, 1)
                wait(dve, routed, UNITS * i + unit + 1 + 1)

            with dve.Fori(0, PH // 2) as i:
                step.enter(i, 26 * UNITS)
                for unit in range(UNITS):
                    route(i, unit)
            step.leave(PH // 2)
            wait(dve, softmax_ready, UNITS * PH // 2 + 1)
            for t in range(TT):
                n = P if t < NT else NS
                gates = (gall[:, t, :] if t < GT else seld[0:n, t - GT, 2, :]).rearrange("p (h k) -> p h k", h=PH)
                step(dve.tensor_reduce(gsum[0:n, :], gates, AX.X, ALU.add))
                step(dve.reciprocal(gsum[0:n, :], gsum[0:n, :]))
                step(dve.tensor_scalar(gsum[0:n, :], gsum[0:n, :], 0.5, None, ALU.mult))
                last = dve.tensor_tensor(gates, gates, gsum[0:n, :].unsqueeze(2).to_broadcast([n, PH, TOPK]), ALU.mult)
                if t < GT:
                    step(last)
                else:
                    last.then_inc(sel_ready, 1)
                    wait(dve, sel_ready, t - GT + 1)
            wait(dve, iota_ready, 1)
            wait(dve, selT_ready, DT)
            dve.sem_inc(rows_used, RING)
            with dve.Fori(0, DN // (SET * SETS)) as r:
                for j in range(SETS):
                    wait(dve, ps_ready[j % 2], USE_G + 4 * r + j // 2)
                    dve.tensor_tensor(ohs[:, j % 2, :, :, :],
                                      iota128.unsqueeze(1).unsqueeze(1).to_broadcast([P, 2, SET, P]),
                                      selT[:, 0:2, bass.ds(SET * SETS * r + SET * j, SET)].unsqueeze(3).to_broadcast(
                                          [P, 2, SET, P]), ALU.is_equal).then_inc(onehot_ready, 1)

            def gathered(i, j, r):
                m = PER * j + r
                t, k = m // (2 * TOPK), m % (2 * TOPK)
                tile = ring[:, m % RING, :]
                if k < TOPK:
                    dve.wait_ge(rows_loaded[m % RING], 16 * (ROWS // RING) * i + 16 * (m // RING) + 16)
                    dve.tensor_tensor_reduce(out=tile, in0=tile, in1=h2[:, t, :], scale=1.0, scalar=0.0,
                                             op0=ALU.mult, op1=ALU.add, accum_out=hidden[:, k:k + 1]
                                             ).then_inc(rows_used, 1)
                else:
                    wait(dve, rows_used, ROWS * i + m + RING)
                    dve.wait_ge(rows_loaded[m % RING], 16 * (ROWS // RING) * i + 16 * (m // RING) + 16)
                    dve.scalar_tensor_tensor(out=resid[:, t, :], in0=tile, scalar=wexp[:, k - TOPK:k - TOPK + 1],
                                             in1=resid[:, t, :], op0=ALU.mult, op1=ALU.add).then_inc(rows_used, 1)

            def add_v(g, q):
                dve.wait_ge(ps_ready[q % 2], USE_V + 4 * g + q // 2 + 1)
                dve.tensor_tensor(accT[:, 2 * q:2 * q + 2, :], ps[:, q % 2, :, 0:DN], accT[:, 2 * q:2 * q + 2, :],
                                  ALU.add).then_inc(ps_free[q % 2], 1)

            def weights(i, j, first=False):
                g = STEPS * i + j

                def add(*qs):
                    for q in qs:
                        if not first:
                            add_v(g - 1, q)

                for r in range(PER - 1):
                    gathered(i, j, r)
                add(0)
                dve.wait_ge(sq_ready, g + 1)
                dve.scalar_tensor_tensor(out=x2[:, :, :], in0=x2[:, :, :], scalar=1.0, in1=pm[:, 0:2, 0:DN],
                                         op0=ALU.add, op1=ALU.mult).then_inc(arg_ready, 1)
                add(1, 2)
                dve.wait_ge(tanh_ready, g + 1)
                dve.scalar_tensor_tensor(out=x2[:, :, :], in0=x2[:, :, :], scalar=1.0, in1=pm[:, 0:2, 0:DN],
                                         op0=ALU.add, op1=ALU.mult).then_inc(x1_ready, 1)
                add(3)
                wait(dve, x1_ready, g + 1)
                dve.wait_ge(gt_loaded[j % 2], 16 * (STEPS // 2) * i + 16 * (j // 2) + 16)
                dve.tensor_tensor(WT[:, j % 2, :, :].rearrange("p b (t n) -> p b t n", t=NST),
                                  x2[:, :, :].rearrange("p b (t n) -> p b t n", t=NST),
                                  gT[:, j % 2, :, :].rearrange("p t (b n) -> p b t n", b=2), ALU.mult
                                  ).then_inc(wt_ready, 1)
                gathered(i, j, PER - 1)
                tile = GT * i + j // 4
                if j % 4 == 1:
                    dve.wait_ge(rows_used, ROWS * i + PER * (j + 1) + RING)
                    step(dve.tensor_tensor(gelu_t, hidden, hidden, ALU.mult))
                    step(dve.tensor_scalar(gelu_t, gelu_t, 0.044715, 1.0, ALU.mult, ALU.add))
                    dve.tensor_tensor(gelu_t, gelu_t, hidden, ALU.mult).then_inc(gelu_arg, 1)
                add(4, 5, 6, 7)
                if j % 4 == 1:
                    dve.wait_ge(gelu_tanh, tile + 1)
                    step(dve.scalar_tensor_tensor(out=wexp, in0=gelu_t, scalar=1.0, in1=hidden,
                                                  op0=ALU.add, op1=ALU.mult))
                    step(dve.tensor_tensor(wexp, wexp, gall[:, j // 4, bass.ds(i * TOPK, TOPK)], ALU.mult))

            for j in range(STEPS):
                weights(0, j, first=j == 0)
            with dve.Fori(1, PH - 1) as i:
                step.enter(i, 4 * GT, 1)
                for j in range(STEPS):
                    weights(i, j)
            step.leave(PH - 2)
            for j in range(STEPS):
                weights(PH - 1, j)
            for q in range(QUADS):
                add_v(NG - 1, q)
            dve.wait_ge(rows_used, ROWS * PH + RING)
            dve.sem_inc(peer_done, 1)
            dve.wait_ge(fg_loaded, 16)
            for t in range(TT):
                rows = P if t < NT else NS
                dve.wait_ge(ss3_done, t + 1)
                dve.tensor_scalar(small[0:rows, TT + t:TT + t + 1], small[0:rows, t:t + 1], 1.0 / D, EPS,
                                  ALU.mult, ALU.add).then_inc(ms3_ready, 1)
            dve.wait_ge(rms3_ready, TT)
            for t in range(TT):
                rows = P if t < NT else NS
                step(dve.reciprocal(small[0:rows, 2 * TT + t:2 * TT + t + 1], small[0:rows, TT + t:TT + t + 1]))
                dve.scalar_tensor_tensor(out=resid[0:rows, t, :], in0=resid[0:rows, t, :],
                                         scalar=small[0:rows, 2 * TT + t:2 * TT + t + 1], in1=h2[0:rows, 0, :],
                                         op0=ALU.mult, op1=ALU.mult).then_inc(y_ready, 1)


_INS = ['x_prompt', 'x_sample', 'state_conv', 'state_gla', 'norm1_g', 'w_in', 'w_a2', 'b_a', 'w_dw', 'b_dw',
        'conv_ln_g', 'conv_ln_b', 'w_conv_out', 'gla_norm_g', 'w_gla_o', 'w_mix_out', 'norm2_g', 'peer_wq',
        'peer_k1', 'peer_k2', 'peer_u', 'peer_v', 'final_g']
_OUTS = [(1, 512, 2048), (8, 8, 2048), (1, 1, 30, 1024), (1, 1, 4, 256, 512), (1, 8, 30, 1024), (1, 8, 4, 256, 512)]


def kernel(**inputs):
    import numpy as _np
    import concourse.bacc as _bacc
    from concourse import mybir as _mybir
    from concourse.bass_utils import run_bass_kernel_spmd as _run

    nc = _bacc.Bacc("TRN2", target_bir_lowering=False, num_devices=1)
    arrays, ins = {}, {}
    for name in _INS:
        x = _np.ascontiguousarray(inputs[name])
        arrays[f"in_{name}"] = x
        ins[name] = nc.dram_tensor(f"in_{name}", x.shape, _mybir.dt.from_np(x.dtype), kind="ExternalInput").ap()
    outs = [nc.dram_tensor(f"out_{i}", s, _mybir.dt.float32, kind="ExternalOutput").ap() for i, s in enumerate(_OUTS)]
    trunk(nc, ins, outs)
    r = _run(nc, [arrays], core_ids=[0])
    return tuple(r.results[0][f"out_{i}"] for i in range(len(_OUTS)))
```

```python
from contextlib import ExitStack

import numpy as np
import concourse.bass as bass
from concourse import mybir

F32 = mybir.dt.float32
I32 = mybir.dt.int32
U32 = mybir.dt.uint32
ACT = mybir.ActivationFunctionType
ALU = mybir.AluOpType
AX = mybir.AxisListType

P = 128
D = 2048
SEQ, DEC_B, DEC_S = 512, 8, 8
NS = DEC_B * DEC_S
TOK = SEQ + NS
HALF = TOK // 2
KT = D // P
NT = SEQ // P
TT = NT + 1
CONV = 1024
CT = CONV // P
TAPS = 31
HIST = TAPS - 1
HEADS, DK, DV = 4, 256, 512
RANK = 16
PAIR = 256
EPS = 1e-6
PH, NKEY, TOPK, NEXP = 8, 128, 16, 16384
COL_A, COL_G, COL_Q, COL_K, COL_V, COL_R, COL_Z = 0, 1024, 2048, 3072, 4096, 6144, 8192
COL_GA, COL_GB = COL_Z + RANK, COL_Z + RANK + D
LEVELS = [64, 32, 16, 8, 4, 2, 1]
NL = len(LEVELS)
RING = 4
UNITS = 2 * TT
GT = 2
DT = TT - GT
D0 = GT * P
DN = TOK - D0
SLOTS = PH * TOPK
SET, STAGED = 8, 32
SETS = 8
NST = DN // STAGED
NG = NEXP // (2 * P)
STEPS = NG // PH
PER = 2 * GT * TOPK // STEPS
ROWS = PER * STEPS
QUADS = 8
NEG = -3.0e38

USE_X = 0
USE_HIST = 5
USE_CONV = 6
USE_TAIL = 14
USE_ZA1, USE_MEAN1, USE_VAR0 = 15, 16, 16
USE_HEAD, PER_HEAD = 17, 14
USE_GATE = USE_HEAD + HEADS * PER_HEAD
USE_MIX = USE_GATE + 32
USE_H2 = USE_MIX + 8
USE_RT = USE_H2 + TT
USE_WQ = USE_RT + DT
USE_SEL = USE_WQ + PH
USE_G = USE_SEL + 1
USE_V = USE_G + DN // SET // 2
USE_OUT = USE_V + NG * QUADS // 2
N_HEAD, N_GATE, N_MIX, N_WQ = 8, 32, 64, 72


eng_passed = {}


def wait(eng, sem, value):
    if isinstance(value, int) and value <= 0:
        return
    eng.wait_ge(sem, value)
    if not isinstance(value, int):
        eng.sem_inc(eng_passed[eng.engine], 1)


class Chain:

    def __init__(self, eng, sem):
        self.eng, self.sem, self.base, self.n = eng, sem, 0, 0

    def mark(self, ins):
        self.n += 1
        ins.then_inc(self.sem, 1)

    def wait(self, back=0):
        wait(self.eng, self.sem, self.base + self.n - back)

    def __call__(self, ins):
        self.mark(ins)
        self.wait()

    def enter(self, i, per_trip, first=0):
        self.start, self.per = self.base + self.n, per_trip
        self.base, self.n = self.start - first * per_trip + i * per_trip, 0

    def leave(self, trips):
        assert self.n == self.per, self.n
        self.base, self.n = self.start + self.per * trips, 0


def trunk(nc, a, o):
    eng_passed.clear()
    ctx = ExitStack()
    with ctx:
        def sb(name, shape, dt=F32):
            return ctx.enter_context(nc.sbuf_tensor(name, shape, dt))

        def sem(name):
            return ctx.enter_context(nc.semaphore(name))

        normT = sb("normT", [P, KT, TOK])
        wring = sb("wring", [P, 2, KT, PAIR])
        regB = sb("regB", [P, TT * D])
        glaT = regB[:, 0:KT * TOK].rearrange("p (k t) -> p k t", k=KT)
        resid = regB[:, :].rearrange("p (t d) -> p t d", t=TT)
        ident = sb("ident", [P, P])
        ones = sb("ones", [P, P])
        tri = sb("tri", [P, P])
        tri8 = sb("tri8", [NS, NS])
        bmask = sb("bmask", [NS, DEC_B])
        g1 = sb("g1", [P, KT])
        gln = sb("gln", [P, CT])
        bln = sb("bln", [P, CT])
        bdw = sb("bdw", [P, CT])
        ggla = sb("ggla", [P, KT])
        small = sb("small", [P, 3 * TT])
        zaT = sb("zaT", [RANK + 1, TT * P])
        wa2 = sb("wa2", [RANK + 1, HEADS * DK])
        i12 = sb("i12", [P, 2, 2, 16], U32)
        ci = sb("ci", [P, 2, 16], U32)
        abi = sb("abi", [P, 2, 2, 16], U32)
        idx = sb("idx", [P, GT, TOPK], I32)
        iota16 = sb("iota16", [P, 16])
        ARENA = nc.sbuf_bytes_remaining // 4 - 8
        arena = sb("arena", [P, ARENA])

        def layout(*parts):
            out, at = [], 0
            for shape in parts:
                n = int(np.prod(shape))
                v = arena[:, at:at + n]
                if len(shape) == 2:
                    v = v.rearrange("p (a b) -> p a b", a=shape[0])
                elif len(shape) == 3:
                    v = v.rearrange("p (a b c) -> p a b c", a=shape[0], b=shape[1])
                out.append(v)
                at += n
            assert at <= ARENA, (at, ARENA)
            return out

        def part_of(buf, at, *shape):
            n = int(np.prod(shape))
            v = buf[:, at:at + n]
            if len(shape) == 2:
                return v.rearrange("p (a b) -> p a b", a=shape[0])
            if len(shape) == 3:
                return v.rearrange("p (a b c) -> p a b c", a=shape[0], b=shape[1])
            if len(shape) == 4:
                return v.rearrange("p (a b c e) -> p a b c e", a=shape[0], b=shape[1], c=shape[2])
            return v

        (x_in,) = layout((TT, D))
        EXT = HIST + SEQ + DEC_B * (HIST + DEC_S)
        conv, hist, uext, gate_s, acc, sq_ln, mean_s, wdw, wcur, wza, tails = layout(
            (CT, TOK), (CT, HIST * 9), (2, EXT), (2, TOK), (2, TOK), (CT, TOK), (TOK,), (CT, TAPS), (2, TAPS),
            (KT, RANK), (3, CONV))
        (qT, kT, lg, bT, vt, qf, kf, earg, mask, att, state, sring, qe, kdec, kd, kdm, dec, rs, rms) = layout(
            (2, TOK), (2, TOK), (TT, DK), (2, TOK), (TT, DV), (NL, 2, P), (NL, 2, P), (2 * NL, 2, P // 2),
            (NL + 1, P), (P,), (2, DV), (4, 2, DV), (2, P), (2, P), (DK,), (2, DK), (2, DEC_B), (4, TOK), (TOK,))
        masked = earg.rearrange("p a b c -> p (a b c)")[:, 0:(NL + 1) * P].rearrange("p (l t) -> p l t", l=NL + 1)
        assert TT * D - KT * TOK >= 2 * DEC_B * NS
        qs = part_of(regB, KT * TOK, 2, DEC_B * NS)
        os_tok = earg.rearrange("p a b c -> p (a b c)")[0:NS, 0:DV]
        sq = vt.rearrange("p t e -> p (t e)")[:, 0:4 * TOK].rearrange("p (e t) -> p e t", e=4)
        merged, convg, gsigB, gsigA, part = layout((KT, TOK), (CT, TOK), (2, TOK), (2, TOK), (2, TOK))
        h2 = part_of(arena, 0, TT, D)
        ring = part_of(arena, GT * D, RING, D)
        g2 = part_of(arena, TT * D, D)
        seld = part_of(arena, TT * D, DT, 3, SLOTS)
        at = (GT + RING) * D
        accT = part_of(arena, at, KT, DN)
        squares = part_of(arena, at, D)
        at += KT * DN
        qp = part_of(arena, at, 2, 2, TOK)
        selT = part_of(arena, at, 3, DN)
        gT = part_of(arena, at, 2, NST, 2 * STAGED)
        at += 4 * TOK
        gall = part_of(arena, at, GT, SLOTS)
        idxs = part_of(arena, at + GT * SLOTS, GT, SLOTS).bitcast(I32)
        at += 2 * GT * SLOTS
        work = arena[:, at:ARENA]
        ktab, kkT = (part_of(work, n * 2 * P, 2, P) for n in range(2))
        EACH = 7 * P + 2 * TOPK
        route_at = [4 * P + b * EACH for b in range(2)]
        sc2, cand, oh = ([part_of(work, r + off, *shape) for r in route_at] for off, shape in (
            (0, (2, NKEY)), (2 * P, (TOPK, TOPK)), (2 * P, (2, TOPK, TOPK))))
        cand2 = [part_of(work, r, TOPK * TOPK) for r in route_at]
        v12, i12f, ab, esel = ([part_of(work, r + 6 * P + n * 2 * TOPK, 2, TOPK) for r in route_at] for n in range(4))
        cs = [part_of(work, r + 7 * P, TOPK + 1) for r in route_at]
        gsum = part_of(work, 4 * P + 2 * EACH, PH)
        iota128 = part_of(work, 4 * P + 2 * EACH + PH, P)
        x2 = part_of(work, 0, 2, DN)
        WT = part_of(work, 2 * DN, 2, 2, DN)
        hidden, gelu_t, wexp = (part_of(work, 6 * DN + n * TOPK, TOPK) for n in range(3))
        assert at + 6 * DN + 3 * TOPK <= ARENA and at + 5 * P + 2 * EACH + PH <= ARENA, (at, ARENA)
        ohs = part_of(regB, GT * D, 4, 2, SET // 2 * P).rearrange("p s k (n i) -> p s k n i", n=SET // 2)
        stage = [part_of(arena, GT * D + st * P * STAGED, P, STAGED) for st in range(2)]
        uraw = wring[:, 0, :, :].rearrange("p k c -> p (k c)").rearrange("p (b d) -> p b d", b=2)
        UT = wring[:, 1, :, :].rearrange("p k c -> p (k c)").rearrange("p (n e) -> p n e", n=2 * KT)
        final_g = uraw[:, 0, :]
        h2T = normT[:, :, D0:TOK]

        def vblock(pair, b):
            if pair == 0:
                return normT[:, b * KT // 2:(b + 1) * KT // 2, 0:PAIR]
            return regB[:, (GT + b) * D:(GT + b + 1) * D].rearrange("p (k c) -> p k c", c=PAIR)

        ps = ctx.enter_context(nc.psum_tensor("ps", [P, 2, 2, 512], F32))
        pm = ctx.enter_context(nc.psum_tensor("pm", [P, 4, 512], F32))
        gates_dram = nc.dram_tensor("gates", [NST, P, P * STAGED], F32, kind="Internal").ap()
        conv_dram = nc.dram_tensor("conv_spill", [P, CT * TOK], F32, kind="Internal").ap()

        def flat(s):
            return ps[:, s, :, :].rearrange("p b n -> p (b n)")

        def halves(s):
            return ps[:, s, :, 0:HALF]

        def th(ap):
            return ap.rearrange("p (b n) -> p b n", b=2)

        def key_scores(unit, rows):
            return pm[0:rows, unit % 8 // 2, unit % 2 * PAIR:(unit % 2 + 1) * PAIR].rearrange(
                "p (a n) -> p a n", a=2)

        z_ps = pm[:, 0:3, :].rearrange("p b n -> p (b n)")

        def head(h):
            return USE_HEAD - 1 + PER_HEAD * h

        def span(c):
            return slice(c * P, c * P + (P if c < NT else NS))

        def levels(c):
            return [(l, w) for l, w in enumerate(LEVELS) if c < NT or w < DEC_S]

        for e in (nc.sync, nc.gpsimd, nc.tensor, nc.scalar, nc.vector):
            eng_passed[e.engine] = sem(f"waits_passed_{len(eng_passed)}")
        w_loaded = [sem("w_loaded0"), sem("w_loaded1")]
        ps_ready = [sem("ps_ready0"), sem("ps_ready1")]
        ps_free = [sem("ps_free0"), sem("ps_free1")]
        const_loaded = sem("const_loaded")
        x_loaded = [sem(f"x_loaded{t}") for t in range(TT)]
        g1_loaded = sem("g1_loaded")
        hist_loaded = sem("hist_loaded")
        consts_made = sem("consts_made")
        act_step, dve_step, pool_step = sem("act_step"), sem("dve_step"), sem("pool_step")
        ss_ready, rms_ready, x_normed = sem("ss_ready"), sem("rms_ready"), sem("x_normed")
        normT_ready = sem("normT_ready")
        hist_zeroed, hist_ready, uext_hist, u_ready, tails_kept = sem("hist_zeroed"), sem("hist_ready"), sem("uext_hist"), sem("u_ready"), sem("tails_kept")
        gate_ready, gate_used = sem("gate_ready"), sem("gate_used")
        wcur_ready, conv_done, conv_kept = sem("wcur_ready"), sem("conv_done"), sem("conv_kept")
        tail_ready, tail_stored = sem("tail_ready"), sem("tail_stored")
        mean_ready, centered, sqln_ready, sd_ready, lned, affined, tanhed, silu_ready = (
            sem("mean_ready"), sem("centered"), sem("sqln_ready"), sem("sd_ready"), sem("lned"), sem("affined"),
            sem("tanhed"), sem("silu_ready"))
        spilled = sem("spilled")
        za_ready = sem("za_ready")
        wa2_loaded = sem("wa2_loaded")
        stores_done = sem("stores_done")
        masks_made = sem("masks_made")
        os_ready, os_kept = sem("os_ready"), sem("os_kept")
        z_ready = sem("z_ready")
        lgabs_ready, lg_ready, k_ready, q_ready, b_ready, v_ready = (
            sem("lgabs_ready"), sem("lg_ready"), sem("k_ready"), sem("q_ready"), sem("b_ready"), sem("v_ready"))
        earg_ready, exp_ready, kdarg_ready, decay_ready = (
            sem("earg_ready"), sem("exp_ready"), sem("kdarg_ready"), sem("decay_ready"))
        factors_ready, scores_ready, att_ready, o_ready, o_kept = (
            sem("factors_ready"), sem("scores_ready"), sem("att_ready"), sem("o_ready"), sem("o_kept"))
        kdT_ready, kd_ready, kdm_ready = sem("kdT_ready"), sem("kd_ready"), sem("kdm_ready")
        rtanh_ready, rsilu_ready = sem("rtanh_ready"), sem("rsilu_ready")
        state_ready, state_stored = sem("state_ready"), sem("state_stored")
        st_updated = sem("st_updated")
        st_loaded = [sem(f"st_loaded{k}") for k in range(4)]
        st_stored = [sem(f"st_stored{k}") for k in range(4)]
        gateB_ready, gateA_ready, mergedB_ready, part_ready, merged_ready = (
            sem("gateB_ready"), sem("gateA_ready"), sem("mergedB_ready"), sem("part_ready"), sem("merged_ready"))
        conv_back, resid_loaded, g2_loaded, resid_ready = (
            sem("conv_back"), sem("resid_loaded"), sem("g2_loaded"), sem("resid_ready"))
        ktab_loaded, kkT_ready, kk_ready = sem("ktab_loaded"), sem("kkT_ready"), sem("kk_ready")
        ss2_done, ms2_ready, rms2_ready, h2_ready, h2T_ready = (
            sem("ss2_done"), sem("ms2_ready"), sem("rms2_ready"), sem("h2_ready"), sem("h2T_ready"))
        qp_ready, keyscores_ready, routed, negmax_ready, softmax_ready = (
            sem("qp_ready"), sem("keyscores_ready"), sem("routed"), sem("negmax_ready"), sem("softmax_ready"))
        rows_used, gelu_arg, gelu_tanh = (
            sem("rows_used"), sem("gelu_arg"), sem("gelu_tanh"))
        accT_ready, iota_ready, sel_ready, selT_ready, onehot_ready, g_staged, stage_free = (
            sem("accT_ready"), sem("iota_ready"), sem("sel_ready"), sem("selT_ready"), sem("onehot_ready"), sem("g_staged"), sem("stage_free"))
        u_done, tr_done, ut_ready, sq_ready, arg_ready, tanh_ready, x1_ready, wt_ready, back_ready = (
            sem("u_done"), sem("tr_done"), sem("ut_ready"), sem("sq_ready"), sem("arg_ready"), sem("tanh_ready"),
            sem("x1_ready"), sem("wt_ready"), sem("back_ready"))
        idx_ready = sem("idx_ready")
        gated_ready = sem("gated_ready")
        g_stored, gt_loaded, u_loaded, v_loaded = (
            [sem(f"{name}{k}") for k in range(2)] for name in ("g_stored", "gt_loaded", "u_loaded", "v_loaded"))
        rows_loaded = [sem(f"rows_loaded{k}") for k in range(RING)]
        fg_loaded, peer_done, ss3_done, ms3_ready, rms3_ready, y_ready, y_stored = (
            sem("fg_loaded"), sem("peer_done"), sem("ss3_done"), sem("ms3_ready"),
            sem("rms3_ready"), sem("y_ready"), sem("y_stored"))
        osq_ready, rms_done, gla_ready = sem("osq_ready"), sem("rms_done"), sem("gla_ready")

        block = ctx.enter_context(nc.Block())
        w_in = a["w_in"][0]

        @block.sync
        def _(sp):
            def load(slot, w, rows, col):
                k = rows // P
                sp.dma_start(wring[:, slot, 0:k, :],
                             w[:, bass.ds(col, PAIR)].rearrange("(k p) c -> p k c", p=P)).then_inc(w_loaded[slot], 16)

            for t in range(NT):
                sp.dma_start(x_in[:, t, :], a["x_prompt"][0, t * P:(t + 1) * P, :]).then_inc(x_loaded[t], 16)
            sp.dma_start(x_in[0:NS, NT, :], a["x_sample"].rearrange("b s d -> (b s) d")).then_inc(x_loaded[NT], 16)
            sp.dma_start(g1[:, :], a["norm1_g"].rearrange("o (k p) -> p (o k)", p=P),
                         allow_slow_non_contiguous=True).then_inc(g1_loaded, 16)
            load(0, w_in, D, COL_G)
            load(1, w_in, D, COL_A)
            with sp.Fori(1, CT // 2) as i:
                wait(sp, ps_ready[1], USE_CONV + 2 * i - 1)
                load(0, w_in, D, COL_G + i * PAIR)
                wait(sp, ps_ready[1], USE_CONV + 2 * i)
                load(1, w_in, D, COL_A + i * PAIR)

            wait(sp, ps_ready[1], USE_CONV + CT - 1)
            load(0, w_in, D, COL_K)
            wait(sp, ps_ready[1], USE_CONV + CT)
            load(1, w_in, D, COL_Q)
            sp.dma_start(wa2[0:RANK, :], a["w_a2"][0, :, :]).then_inc(wa2_loaded, 16)
            sp.dma_start(wa2[RANK:RANK + 1, :], a["b_a"]).then_inc(wa2_loaded, 16)
            for k in range(3):
                wait(sp, tail_ready, k + 1)
                if k == 0:
                    sp.dma_start(o[2][0, 0, :, :], tails[0:HIST, 0, :]).then_inc(tail_stored, 16)
                else:
                    sp.dma_start(o[4][0, 4 * (k - 1):4 * k, :, :].rearrange("b t c -> (b t) c"),
                                 tails[0:4 * HIST, k, :]).then_inc(tail_stored, 16)
            wait(sp, silu_ready, 1)
            sp.dma_start(conv_dram, conv[:, :, :].rearrange("p c t -> p (c t)")).then_inc(spilled, 16)
            wait(sp, tail_stored, 48)
            wait(sp, spilled, 16)

            def head_loads(h):
                u = head(h)
                wait(sp, ps_ready[1], u + 2)
                load(0, w_in, D, COL_V + h * DV)
                wait(sp, ps_ready[1], u + 3)
                load(1, w_in, D, COL_V + h * DV + PAIR)
                wait(sp, ps_ready[1], u + 5)
                load(0, w_in, D, COL_R + h * DV)
                wait(sp, ps_ready[1], u + 6)
                load(1, w_in, D, COL_R + h * DV + PAIR)

            with sp.Fori(0, HEADS - 1) as h:
                head_loads(h)
                wait(sp, ps_ready[0], head(h) + 8)
                load(0, w_in, D, COL_K + h * DK + DK)
                wait(sp, ps_ready[0], head(h) + 10)
                load(1, w_in, D, COL_Q + h * DK + DK)
            head_loads(HEADS - 1)
            wait(sp, ps_ready[0], head(HEADS - 1) + 8)
            load(0, w_in, D, COL_GB)
            wait(sp, ps_ready[0], head(HEADS - 1) + 10)
            load(1, a["w_gla_o"][0], D, 0)

            def gate_loads(i):
                wait(sp, ps_ready[1], USE_GATE + 4 * i + 1)
                load(0, w_in, D, COL_GA + i * PAIR)
                wait(sp, ps_ready[1], USE_GATE + 4 * i + 2)
                load(1, a["w_conv_out"][0], CONV, i * PAIR)

            with sp.Fori(0, D // PAIR - 1) as i:
                gate_loads(i)
                wait(sp, ps_ready[1], USE_GATE + 4 * i + 3)
                load(0, w_in, D, COL_GB + i * PAIR + PAIR)
                wait(sp, ps_ready[1], USE_GATE + 4 * i + 4)
                load(1, a["w_gla_o"][0], D, i * PAIR + PAIR)
            gate_loads(D // PAIR - 1)
            wait(sp, ps_ready[1], USE_MIX - 1)
            load(0, a["w_mix_out"][0], D, 0)
            wait(sp, ps_ready[1], USE_MIX)
            load(1, a["w_mix_out"][0], D, PAIR)
            with sp.Fori(1, D // PAIR // 2) as i:
                for slot in range(2):
                    wait(sp, ps_ready[1], USE_MIX + 2 * i - 1 + slot)
                    load(slot, a["w_mix_out"][0], D, (2 * i + slot) * PAIR)
            for slot in range(2):
                wait(sp, ps_ready[1], USE_H2 - 1 + slot)
                load(slot, a["peer_wq"][0], D, slot * PAIR)
            with sp.Fori(1, PH // 2) as i:
                for slot in range(2):
                    wait(sp, ps_ready[1], USE_WQ + 2 * i - 1 + slot)
                    load(slot, a["peer_wq"][0], D, (2 * i + slot) * PAIR)

            def v_load(g, pair):
                for b in range(2):
                    sp.dma_start(vblock(pair, b),
                                 a["peer_v"][0, bass.ds(g * 2 * P + b * P, P), :].rearrange("p (k c) -> p k c", c=PAIR)
                                 ).then_inc(v_loaded[pair], 16)

            def u_load(g, b):
                sp.dma_start(uraw[:, b, :], a["peer_u"][0, bass.ds(g * 2 * P + b * P, P), :]).then_inc(u_loaded[b], 16)

            def gates_load(g, slot):
                sp.dma_start(gT[:, slot, :, :],
                             gates_dram[:, :, bass.ds(g * 2 * STAGED, 2 * STAGED)].rearrange("t p c -> p t c")
                             ).then_inc(gt_loaded[slot], 16)

            wait(sp, ps_ready[1], USE_WQ + PH)
            for b in range(2):
                u_load(0, b)
            v_load(0, 0)
            for b in range(2):
                wait(sp, tr_done, 4 * b + 4)
                u_load(1, b)
            sp.sem_inc(stage_free, 2)
            with sp.Fori(0, DN // (SET * SETS)) as r:
                for st in range(2):
                    wait(sp, g_staged, SETS * r + 4 * st + 4)
                    sp.dma_start(gates_dram[bass.ds(2 * r + st, 1), :, :].rearrange("o p c -> p (o c)"),
                                 stage[st].rearrange("p i n -> p (i n)")).then_inc(g_stored[st], 16)
                    wait(sp, g_stored[st], 16 * r + 16)
                    sp.sem_inc(stage_free, 1)
            gates_load(0, 0)

            def dense_loads(i, j, first=False, last=False):
                g = STEPS * i + j
                if not last:
                    if not first:
                        wait(sp, tr_done, QUADS * g + 4)
                        u_load(g + 1, 0)
                    wait(sp, wt_ready, g)
                    gates_load(g + 1, (j + 1) % 2)
                    if not first:
                        wait(sp, tr_done, QUADS * g + 8)
                        u_load(g + 1, 1)
                if not first:
                    wait(sp, ps_ready[1], USE_V + 4 * g - 4)
                    v_load(g, j % 2)

            for j in range(STEPS):
                dense_loads(0, j, first=j == 0)
            with sp.Fori(1, PH - 1) as i:
                for j in range(STEPS):
                    dense_loads(i, j)
            for j in range(STEPS):
                dense_loads(PH - 1, j, last=j == STEPS - 1)
            for t in range(TT):
                n = P if t < NT else NS
                wait(sp, y_ready, t + 1)
                sp.dma_start(o[0][0, span(t), :] if t < NT else o[1].rearrange("b s d -> (b s) d"),
                             resid[0:n, t, :]).then_inc(y_stored, 16)
            wait(sp, y_stored, 16 * TT)

        @block.gpsimd
        def _(pool):
            step = Chain(pool, pool_step)
            for first in (tails_kept, stores_done):
                pool.sem_inc(first, 1)
            step(pool.memset(ident[:, :], 0.0))
            step(pool.affine_select(out=ident[:, :], in_=ident[:, :], compare_op=ALU.not_equal, fill=1.0, base=0,
                                    pattern=[[-1, P]], channel_multiplier=1))
            step(pool.memset(tri[:, :], 1.0 / 16.0))
            step(pool.affine_select(out=tri[:, :], in_=tri[:, :], compare_op=ALU.is_ge, fill=0.0, base=0,
                                    pattern=[[1, P]], channel_multiplier=-1))
            t8 = tri8[:, :].rearrange("p (b t) -> p b t", b=DEC_B)
            step(pool.tensor_copy(tri8[:, :], tri[0:NS, 0:NS]))
            step(pool.affine_select(out=t8, in_=t8, compare_op=ALU.is_ge, fill=0.0, base=0,
                                    pattern=[[-DEC_S, DEC_B], [0, DEC_S]], channel_multiplier=1))
            step(pool.memset(bmask[:, :], 1.0))
            step(pool.affine_select(out=bmask[:, :], in_=bmask[:, :], compare_op=ALU.is_ge, fill=0.0, base=0,
                                    pattern=[[-DEC_S, DEC_B]], channel_multiplier=1))
            step(pool.affine_select(out=bmask[:, :], in_=bmask[:, :], compare_op=ALU.is_ge, fill=0.0, base=DEC_S - 1,
                                    pattern=[[DEC_S, DEC_B]], channel_multiplier=-1))
            step(pool.iota(iota16[:, :], pattern=[[1, 16]], base=0, channel_multiplier=0,
                           allow_small_or_imprecise_dtypes=True))
            pool.memset(zaT[:, :], 1.0).then_inc(consts_made, 1)
            pool.memset(ones[:, :], 1.0).then_inc(consts_made, 1)
            pool.dma_start(gln[:, :], a["conv_ln_g"].rearrange("o (k p) -> p (o k)", p=P),
                           allow_slow_non_contiguous=True).then_inc(const_loaded, 16)
            pool.dma_start(bln[:, :], a["conv_ln_b"].rearrange("o (k p) -> p (o k)", p=P),
                           allow_slow_non_contiguous=True).then_inc(const_loaded, 16)
            pool.dma_start(bdw[:, :], a["b_dw"].rearrange("o (k p) -> p (o k)", p=P),
                           allow_slow_non_contiguous=True).then_inc(const_loaded, 16)
            pool.dma_start(ggla[:, :], a["gla_norm_g"].rearrange("o (k p) -> p (o k)", p=P),
                           allow_slow_non_contiguous=True).then_inc(const_loaded, 16)
            for c in range(CT):
                pool.dma_start(wdw[:, c, :], a["w_dw"][0, :, c * P:(c + 1) * P].rearrange("j p -> p j"),
                               allow_slow_non_contiguous=True).then_inc(const_loaded, 16)
            pool.dma_start(wza[:, :, :], w_in[:, COL_Z:COL_Z + RANK].rearrange("(k p) c -> p k c", p=P)
                           ).then_inc(const_loaded, 16)
            for g in range(2):
                pool.dma_start(tails[0:4 * HIST, 1 + g, :],
                               a["state_conv"][0, 4 * g:4 * g + 4, :, :].rearrange("b t c -> (b t) c")
                               ).then_inc(hist_loaded, 16)
            wait(pool, normT_ready, 2 * TT)
            pool.memset(hist[:, :, 0:HIST], 0.0).then_inc(hist_zeroed, 1)
            wait(pool, hist_zeroed, 1)
            wait(pool, hist_ready, 2)
            with pool.Fori(0, CT // 2) as i:
                wait(pool, conv_done, 4 * i + 1)
                hv = hist[:, bass.ds(2 * i, 2), :]
                uv = uext[:, :, HIST + SEQ:].rearrange("p q (b t) -> p q b t", b=DEC_B)
                pool.tensor_copy(uext[:, :, 0:HIST], hv[:, :, 0:HIST]).then_inc(uext_hist, 1)
                for q in range(2):
                    pool.tensor_copy(uv[:, q, :, 0:HIST], hv[:, q, HIST:].rearrange("p (b t) -> p b t", b=DEC_B)
                                     ).then_inc(uext_hist, 1)
                wait(pool, uext_hist, 3 * i + 3)
                wait(pool, u_ready, 6 * i + 6)
                pool.tensor_copy(hv[:, :, 0:HIST], uext[:, :, SEQ:SEQ + HIST]).then_inc(tails_kept, 1)
                for q in range(2):
                    pool.tensor_copy(hv[:, q, HIST:].rearrange("p (b t) -> p b t", b=DEC_B), uv[:, q, :, DEC_S:]
                                     ).then_inc(tails_kept, 1)
                wait(pool, tails_kept, 3 * i + 3 + 1)

            wait(pool, spilled, 16)
            wait(pool, tail_stored, 48)
            wait(pool, za_ready, 1)
            base = step.base + step.n
            n = 0
            pool.memset(mask[:, :, :], 1.0).then_inc(pool_step, 1)
            pool.memset(qf[:, :, :, :], 0.0).then_inc(pool_step, 1)
            pool.memset(kf[:, :, :, :], 0.0).then_inc(pool_step, 1)
            pool.memset(qs[:, :, :], 0.0).then_inc(pool_step, 1)
            n = 4
            wait(pool, pool_step, base + n)
            for l, w in enumerate(LEVELS[1:], 1):
                for b, mul, st in ((0, 1, -2 * w), (2 * w - 1, -1, 2 * w)):
                    mv = mask[:, l, :].rearrange("p (g w) -> p g w", w=2 * w)
                    pool.affine_select(out=mv, in_=mv, compare_op=ALU.is_ge, fill=0.0, base=b,
                                       pattern=[[st, P // (2 * w)], [0, 2 * w]], channel_multiplier=mul
                                       ).then_inc(pool_step, 1)
                    n += 1
                    wait(pool, pool_step, base + n)
            pool.tensor_copy(mask[:, NL, :], ident[:, :]).then_inc(masks_made, 1)

            def state_load(h, b):
                pool.dma_start(sring[:, b % 4, :, :],
                               a["state_gla"][0, b, bass.ds(h, 1), :, :].rearrange("o (j p) e -> p (o j) e", p=P)
                               ).then_inc(st_loaded[b % 4], 16)

            with pool.Fori(0, HEADS) as h:
                for b in range(4):
                    state_load(h, b)
                wait(pool, state_ready, NT * h + NT)
                pool.dma_start(o[3][0, 0, bass.ds(h, 1), :, :].rearrange("o (j p) e -> p (o j) e", p=P),
                               state[:, :, :]).then_inc(state_stored, 16)
                for b in range(DEC_B):
                    wait(pool, st_updated, 2 * DEC_B * h + 2 * b + 2)
                    pool.dma_start(o[5][0, b, bass.ds(h, 1), :, :].rearrange("o (j p) e -> p (o j) e", p=P),
                                   sring[:, b % 4, :, :]).then_inc(st_stored[b % 4], 16)
                    if b < 4:
                        wait(pool, st_stored[b], 32 * h + 16)
                        state_load(h, b + 4)
                for b in range(4):
                    wait(pool, st_stored[b], 32 * h + 32)
                wait(pool, state_stored, 16 * h + 16)
                pool.sem_inc(stores_done, 1)
            wait(pool, gla_ready, 4 * HEADS)
            pool.dma_start(convg[:, :, :].rearrange("p c t -> p (c t)"), conv_dram).then_inc(conv_back, 16)
            wait(pool, ps_ready[0], USE_MIX - 2)
            wait(pool, ps_ready[1], USE_MIX - 2)
            pool.dma_start(resid[:, 0:NT, :], a["x_prompt"][0].rearrange("(t p) d -> p t d", p=P)
                           ).then_inc(resid_loaded, 16)
            pool.dma_start(resid[0:NS, NT, :], a["x_sample"].rearrange("b s d -> (b s) d")).then_inc(resid_loaded, 16)
            wait(pool, merged_ready, D // PAIR + 1)
            pool.dma_start(g2, a["norm2_g"].partition_broadcast(P)).then_inc(g2_loaded, 16)
            for half, key in enumerate(("peer_k1", "peer_k2")):
                pool.dma_start(ktab[:, half, :], a[key][0, :, :]).then_inc(ktab_loaded, 16)
            pool.iota(iota128, pattern=[[1, P]], base=0, channel_multiplier=0,
                      allow_small_or_imprecise_dtypes=True).then_inc(iota_ready, 1)
            wait(pool, selT_ready, DT)
            with pool.Fori(0, DN // (SET * SETS)) as r:
                for half in range(2 * SETS):
                    wait(pool, onehot_ready, 2 * SETS * r + half + 1)
                    pool.tensor_tensor(ohs[:, half % 4, 0, :, :], ohs[:, half % 4, 0, :, :],
                                       selT[:, 2, bass.ds(SET * SETS * r + SET // 2 * half, SET // 2)].unsqueeze(
                                           2).to_broadcast([P, SET // 2, P]), ALU.mult).then_inc(gated_ready, 1)

            def gathers(i):
                for m in range(ROWS):
                    t, k = m // (2 * TOPK), m % (2 * TOPK)
                    if k == 0:
                        wait(pool, rows_used, ROWS * i + m + 1)
                        pool.tensor_copy(idx[:, t, :], idxs[:, t, bass.ds(i * TOPK, TOPK)]).then_inc(idx_ready, 1)
                        wait(pool, idx_ready, GT * i + t + 1)
                    wait(pool, rows_used, ROWS * i + m + 1)
                    pool.indirect_dma_start(
                        ring[:, m % RING, :], None, (a["peer_u"] if k < TOPK else a["peer_v"])[0],
                        bass.IndirectOffsetOnAxis(ap=idx[:, t, k % TOPK:k % TOPK + 1], axis=0),
                        bounds_check=NEXP - 1, oob_is_err=True).then_inc(rows_loaded[m % RING], 16)

            with pool.Fori(0, PH) as i:
                gathers(i)
            wait(pool, tr_done, QUADS * NG)
            pool.dma_start(final_g, a["final_g"].rearrange("(o d) -> o d", o=1).partition_broadcast(P)
                           ).then_inc(fg_loaded, 16)

        @block.tensor
        def _(pe):
            pe.sem_inc(ps_free[0], 1)
            for first in (scores_ready, keyscores_ready):
                pe.sem_inc(first, 1)
            pe.sem_inc(ps_free[1], 1)

            def transposes(s, use, src, rows, n):
                wait(pe, ps_free[s], use + 1)
                for k in range(n):
                    last = pe.transpose(flat(s)[:, k * P:k * P + rows], src(k), ident[0:rows, 0:rows])
                last.then_inc(ps_ready[s], 1)

            def project(s, use, j, slot, srcT, kt=KT):
                pe.wait_ge(ps_free[s], use + 1)
                for h in range(2):
                    for k in range(kt):
                        last = pe.matmul(ps[:, s, h, 0:HALF], wring[:, slot, k, j * P:(j + 1) * P],
                                         srcT[:, k, h * HALF:(h + 1) * HALF], start=(k == 0), stop=(k == kt - 1))
                last.then_inc(ps_ready[s], 1)

            pe.wait_ge(consts_made, 2)
            pe.wait_ge(pool_step, 2)
            for t in range(TT):
                rows = P if t < NT else NS
                pe.wait_ge(x_normed, t + 1)
                for s in range(2):
                    transposes(s, USE_X + t, lambda k: x_in[0:rows, t, (8 * s + k) * P:(8 * s + k + 1) * P], rows, 8)
            pe.wait_ge(hist_loaded, 32)
            for g in range(2):
                transposes(g, USE_HIST, lambda k: tails[0:4 * HIST, 1 + g, k * P:(k + 1) * P], 4 * HIST, CT)
            pe.wait_ge(normT_ready, 2 * TT)
            with pe.Fori(0, CT // 2) as i:
                for half in range(2):
                    pe.wait_ge(w_loaded[half], 16 * i + 16)
                    for j in range(2):
                        project(j, USE_CONV + 2 * i + half, j, half, normT)
            pe.wait_ge(tails_kept, 3 * CT // 2 + 1)
            for k, (s, use, n) in enumerate([(0, USE_TAIL, HIST), (1, USE_TAIL, 4 * HIST), (0, USE_TAIL + 1, 4 * HIST)]):
                at = (0, HIST, 5 * HIST)[k]
                pe.wait_ge(ps_free[s], use + 1)
                for c in range(CT):
                    last = pe.transpose(flat(s)[0:n, c * P:(c + 1) * P], hist[:, c, at:at + n], ident[:, :])
                last.then_inc(ps_ready[s], 1)
            pe.wait_ge(const_loaded, 16 * 13)
            pe.wait_ge(ps_free[1], USE_ZA1 + 1)
            for h in range(2):
                for k in range(KT):
                    last = pe.matmul(ps[0:RANK, 1, h, 0:HALF], wza[:, k, :], normT[:, k, h * HALF:(h + 1) * HALF],
                                     start=(k == 0), stop=(k == KT - 1))
            last.then_inc(ps_ready[1], 1)
            pe.wait_ge(conv_kept, CT + 1)
            for s, use, src, ready in ((1, USE_MEAN1, conv, None), (0, USE_VAR0, sq_ln, sqln_ready)):
                pe.wait_ge(ps_free[s], use + 1)
                if ready is not None:
                    pe.wait_ge(ready, 1)
                for h in range(2):
                    for c in range(CT):
                        last = pe.matmul(ps[:, s, h, 0:HALF], ones[:, :], src[:, c, h * HALF:(h + 1) * HALF],
                                         start=(c == 0), stop=(c == CT - 1))
                last.then_inc(ps_ready[s], 1)
            def project_tok(use, slot, srcT, kt=KT):
                for s in range(2):
                    pe.wait_ge(ps_free[s], use + 1)
                    for t in (range(NT) if s == 0 else [NT]):
                        n = span(t).stop - span(t).start
                        c0 = t * PAIR if s == 0 else 0
                        for k in range(kt):
                            last = pe.matmul(flat(s)[0:n, c0:c0 + PAIR], srcT[:, k, span(t)], wring[:, slot, k, :],
                                             start=(k == 0), stop=(k == kt - 1))
                    last.then_inc(ps_ready[s], 1)

            pe.wait_ge(wa2_loaded, 32)
            pe.wait_ge(za_ready, 1)
            with pe.Fori(0, HEADS) as h:
                u = head(h)
                for t in range(TT):
                    last = pe.matmul(z_ps[:, t * DK:(t + 1) * DK], zaT[:, t * P:(t + 1) * P], wa2[:, bass.ds(h * DK, DK)],
                                     start=True, stop=True)
                    if t >= NT - 1:
                        last.then_inc(z_ready, 1)
                for slot in range(2):
                    pe.wait_ge(w_loaded[slot], 48 * h + 80)
                    for j in range(2):
                        project(j, u + 1 + slot, j, slot, normT)
                pe.wait_ge(lg_ready, 2 * h + 2)
                for j in range(2):
                    pe.wait_ge(ps_free[j], u + 4)
                    for t in range(TT):
                        n = span(t).stop - span(t).start
                        last = pe.matmul(flat(j)[:, span(t)], lg[0:n, t, j * P:(j + 1) * P],
                                         tri[:, :] if t < NT else tri8[:, :], start=True, stop=True)
                    last.then_inc(ps_ready[j], 1)
                for slot in range(2):
                    pe.wait_ge(w_loaded[slot], 48 * h + 96)
                    project_tok(u + 4 + slot, slot, normT)

                def kd_and_scores(c):
                    n = span(c).stop - span(c).start
                    pe.wait_ge(factors_ready, TT * h + c + 1 + 1)
                    pe.wait_ge(att_ready, TT * h + c + 1)
                    sc = pm[:, 0:2, :].rearrange("p b (l t) -> p (b l) t", t=P)
                    for l, _ in levels(c) + [(NL, 0)]:
                        for j in range(2):
                            kk = kf[:, l, j, 0:n] if l < NL else kT[:, j, span(c)]
                            qq = qf[:, l, j, 0:n] if l < NL else qT[:, j, span(c)]
                            last = pe.matmul(sc[0:n, l, 0:n], kk, qq, start=(j == 0), stop=(j == 1))
                    last.then_inc(scores_ready, 1)
                    pe.wait_ge(decay_ready, TT * h + c + 1)
                    wait(pe, kd_ready, TT * h + c + 1)
                    for j in range(2):
                        last = pe.transpose(pm[0:n, 3, j * P:(j + 1) * P], kdec[:, j, 0:n], ident[:, :])
                    last.then_inc(kdT_ready, 1)

                for c in range(NT):
                    kd_and_scores(c)
                    if c % 2 == 0:
                        pe.wait_ge(w_loaded[c // 2], 48 * h + 112)
                    project(0, u + 6 + c, c % 2, c // 2, normT)
                    pe.wait_ge(v_ready, 4 * h + 4)
                    pe.wait_ge(att_ready, TT * h + c + 1 + 1)
                    pe.wait_ge(o_kept, TT * h + c + 1)
                    if c:
                        pe.wait_ge(state_ready, NT * h + c)
                    for e in range(4):
                        for j in range(2 if c else 0):
                            pe.matmul(pm[:, 2, e * P:(e + 1) * P], state[:, j, e * P:(e + 1) * P], qe[:, j, :],
                                      start=(j == 0), stop=False)
                        last = pe.matmul(pm[:, 2, e * P:(e + 1) * P], vt[:, c, e * P:(e + 1) * P], att[:, :],
                                         start=(c == 0), stop=True)
                    last.then_inc(o_ready, 1)
                    pe.wait_ge(kd_ready, TT * h + c + 1 + 1)
                    pe.wait_ge(ps_free[1], u + 7 + c)
                    for j in range(2):
                        last = pe.matmul(ps[:, 1, j, :], kd[:, j * P:(j + 1) * P], vt[:, c, :], start=True, stop=True)
                    last.then_inc(ps_ready[1], 1)
                kd_and_scores(NT)
                wait(pe, att_ready, TT * h + TT + 1)
                wait(pe, o_kept, TT * h + NT + 1)
                pe.matmul(pm[0:NS, 2, :], att[0:NS, 0:NS], vt[0:NS, NT, :], start=True, stop=False)
                for b in range(DEC_B):
                    wait(pe, st_loaded[b % 4], 32 * h + 16 * (b // 4) + 16)
                    for j in range(2):
                        last = pe.matmul(pm[0:NS, 2, :], qs[:, j, b * NS:(b + 1) * NS], sring[:, b % 4, j, :],
                                         start=False, stop=(b == DEC_B - 1 and j == 1))
                    if b == DEC_B - 1:
                        last.then_inc(os_ready, 1)
                    pe.wait_ge(kdm_ready, DEC_B * h + b + 1)
                    pe.wait_ge(ps_free[b % 2], u + 11 + b // 2)
                    for j in range(2):
                        last = pe.matmul(ps[:, b % 2, j, :], kdm[0:NS, b % 2, j * P:(j + 1) * P], vt[0:NS, NT, :],
                                         start=True, stop=True)
                    last.then_inc(ps_ready[b % 2], 1)
                wait(pe, os_kept, h + 1)
                for e in range(4):
                    last = pe.transpose(pm[:, 2, e * P:e * P + NS], os_tok[:, e * P:(e + 1) * P], ident[0:NS, 0:NS])
                last.then_inc(o_ready, 1)
                pe.wait_ge(osq_ready, h + 1)
                for s in range(2):
                    pe.wait_ge(ps_free[s], u + 15)
                    for e in range(4):
                        last = pe.matmul(ps[:, s, 0, 0:HALF], ones[:, :], sq[:, e, s * HALF:(s + 1) * HALF],
                                         start=(e == 0), stop=(e == 3))
                    last.then_inc(ps_ready[s], 1)

            with pe.Fori(0, D // PAIR) as i:
                for n, (src, kt) in enumerate(((normT, KT), (glaT, KT), (normT, KT), (convg, CT))):
                    if n == 1:
                        pe.wait_ge(gla_ready, 4 * HEADS)
                    if n == 3:
                        pe.wait_ge(conv_back, 16)
                    pe.wait_ge(w_loaded[n % 2], 32 * i + 16 * (N_GATE // 2 + n // 2 + 1))
                    for j in range(2):
                        project(j, USE_GATE + 4 * i + n, j, n % 2, src, kt)
            pe.wait_ge(merged_ready, D // PAIR + 1)
            with pe.Fori(0, D // PAIR // 2) as i:
                for slot in range(2):
                    pe.wait_ge(w_loaded[slot], 16 * i + 16 * (N_MIX // 2 + 1))
                    project_tok(USE_MIX + 2 * i + slot, slot, merged)
            pe.wait_ge(ktab_loaded, 32)
            for half in range(2):
                last = pe.transpose(pm[:, 3, half * P:(half + 1) * P], ktab[:, half, :], ident[:, :])
            last.then_inc(kkT_ready, 1)
            for t in range(TT):
                rows = P if t < NT else NS
                pe.wait_ge(h2_ready, t + 1)
                for s in range(2):
                    transposes(s, USE_H2 + t, lambda k: h2[0:rows, t, (8 * s + k) * P:(8 * s + k + 1) * P], rows, 8)
            pe.wait_ge(h2T_ready, 2 * TT)
            pe.wait_ge(kk_ready, 1)
            for t in range(GT, TT):
                rows = P if t < NT else NS
                for s in range(2):
                    transposes(s, USE_RT + t - GT, lambda k: resid[0:rows, t, (8 * s + k) * P:(8 * s + k + 1) * P],
                               rows, 8)
            with pe.Fori(0, PH // 2) as i:
                for hh in range(2):
                    pe.wait_ge(w_loaded[hh], 16 * i + 16 * (N_WQ // 2 + 1))
                    for j in range(2):
                        project(j, USE_WQ + 2 * i + hh, j, hh, normT)
                pe.wait_ge(qp_ready, 4 * i + 4)
                for unit in range(UNITS):
                    hh, t = unit // TT, unit % TT
                    wait(pe, routed, UNITS * i + max(unit - 7, 0) + 1)
                    rows = P if t < NT else NS
                    for half in range(2):
                        last = pe.matmul(key_scores(unit, rows)[:, half, :], qp[:, hh, half, span(t)], kkT[:, half, :],
                                         start=True, stop=True)
                    last.then_inc(keyscores_ready, 1)

            def transpose_u(g, q):
                if q % 4 == 0:
                    wait(pe, u_loaded[q // 4], 16 * g + 16)
                wait(pe, ut_ready, QUADS * g + q - 1)
                for n in range(4):
                    kb = 4 * q + n
                    last = pe.transpose(pm[:, 2 + q % 2, n * P:(n + 1) * P],
                                        uraw[:, kb // KT, (kb % KT) * P:(kb % KT + 1) * P], ident[:, :])
                last.then_inc(tr_done, 1)

            def products_u(g):
                wait(pe, ut_ready, QUADS * g + QUADS)
                wait(pe, x1_ready, g)
                for b in range(2):
                    for k in range(KT):
                        last = pe.matmul(pm[:, b, 0:DN], UT[:, b * KT + k, :], h2T[:, k, :],
                                         start=(k == 0), stop=(k == KT - 1))
                last.then_inc(u_done, 1)

            wait(pe, routed, UNITS * PH // 2 - 2 + 1)
            for q in range(QUADS):
                transpose_u(0, q)
            wait(pe, routed, UNITS * PH // 2 + 1)
            products_u(0)
            for q in range(QUADS):
                transpose_u(1, q)
            pe.wait_ge(sel_ready, DT)
            for s, tiles in ((0, (0, 1)), (1, (2,))):
                pe.wait_ge(ps_free[s], USE_SEL + 1)
                for t in tiles:
                    rows = P if t < NT - GT else NS
                    for kind in range(3):
                        at = (3 * (t % 2) + kind) * P
                        last = pe.transpose(flat(s)[:, at:at + rows], seld[0:rows, t, kind, :], ident[0:rows, 0:rows])
                last.then_inc(ps_ready[s], 1)
            with pe.Fori(0, DN // (SET * SETS)) as r:
                for j in range(SETS):
                    wait(pe, ps_free[j % 2], USE_G + 4 * r + j // 2 + 1)
                    for n in range(SET):
                        half = 2 * j + n // (SET // 2)
                        if n % (SET // 2) == 0:
                            wait(pe, gated_ready, 2 * SETS * r + half + 1)
                        last = pe.matmul(flat(j % 2)[:, n * P:(n + 1) * P], ohs[:, half % 4, 1, n % (SET // 2), :],
                                         ohs[:, half % 4, 0, n % (SET // 2), :], start=True, stop=True)
                    last.then_inc(ps_ready[j % 2], 1)

            def products_v(g, par, q):
                if q == 0:
                    wait(pe, wt_ready, g + 1)
                    wait(pe, v_loaded[par], 16 * (g - par) + 32)
                wait(pe, ps_free[q % 2], USE_V + 4 * g + q // 2 + 1)
                for h in range(2):
                    for b in range(2):
                        last = pe.matmul(ps[:, q % 2, h, 0:DN], vblock(par, b)[:, q, h * P:(h + 1) * P],
                                         WT[:, par, b, :], start=(b == 0), stop=(b == 1))
                last.then_inc(ps_ready[q % 2], 1)

            def dense(i, j, final=False):
                g = STEPS * i + j
                products_u(g)
                for q in range(QUADS):
                    products_v(g - 1, (j + 1) % 2, q)
                    if not final:
                        transpose_u(g + 1, q)

            for j in range(1, STEPS):
                dense(0, j)
            with pe.Fori(1, PH - 1) as i:
                for j in range(STEPS):
                    dense(i, j)
            for j in range(STEPS):
                dense(PH - 1, j, final=j == STEPS - 1)
            for q in range(QUADS):
                products_v(NG - 1, 1, q)
            for s in range(2):
                pe.wait_ge(ps_free[s], USE_OUT + 1)
            for t in range(DT):
                rows = P if t < NT - GT else NS
                for s in range(2):
                    pe.wait_ge(ps_free[s], USE_OUT + t + 1)
                    for k in range(8):
                        last = pe.transpose(flat(s)[0:rows, k * P:(k + 1) * P], accT[:, 8 * s + k, t * P:t * P + rows],
                                            ident[:, :])
                    last.then_inc(ps_ready[s], 1)

        @block.scalar
        def _(act):
            step = Chain(act, act_step)
            for first in (conv_kept, kd_ready, o_kept, b_ready, softmax_ready):
                act.sem_inc(first, 1)
            for t in range(TT):
                rows = P if t < NT else NS
                wait(act, x_loaded[t], 16)
                step(nc.scalar.activation(regB[0:rows, 0:D], x_in[0:rows, t, :], ACT.Square,
                                          accum_out=small[0:rows, t:t + 1]))
            for t in range(TT):
                rows = P if t < NT else NS
                wait(act, ss_ready, t + 1)
                nc.scalar.activation(small[0:rows, TT + t:TT + t + 1], small[0:rows, TT + t:TT + t + 1], ACT.Sqrt
                                     ).then_inc(rms_ready, 1)
            for g in range(2):
                wait(act, ps_ready[g], USE_HIST + 1)
                nc.scalar.activation(hist[:, :, HIST + 4 * HIST * g:HIST + 4 * HIST * (g + 1)],
                                     flat(g).rearrange("p (c t) -> p c t", c=CT)[:, :, 0:4 * HIST], ACT.Copy
                                     ).then_inc(hist_ready, 1)
            wait(act, hist_ready, 2)
            act.sem_inc(ps_free[0], 1)
            act.sem_inc(ps_free[1], 1)
            wait(act, const_loaded, 16 * 13)
            def gates(i):
                if not isinstance(i, int):
                    wait(act, gate_used, 6 * i)
                for j in range(2):
                    wait(act, ps_ready[j], USE_CONV + 2 * i + 1)
                    nc.scalar.activation(th(gate_s[:, j, :]), halves(j), ACT.Tanh, scale=0.5).then_inc(ps_free[j], 1)
                    wait(act, ps_free[j], USE_CONV + 2 * i + 2)
                    nc.scalar.activation(gate_s[:, j, :], gate_s[:, j, :], ACT.Copy, scale=0.5, bias=0.5
                                         ).then_inc(gate_ready, 1)

            def keep_sums(i):
                wait(act, conv_done, 4 * i + 4 + 1)
                for j in range(2):
                    nc.scalar.activation(conv[:, bass.ds(2 * i + j, 1), :], acc[:, j:j + 1, :], ACT.Identity,
                                         bias=bdw[:, bass.ds(2 * i + j, 1)]).then_inc(conv_kept, 1)

            def taps_of(i):
                nc.scalar.activation(wcur[:, :, :], wdw[:, bass.ds(2 * i, 2), :], ACT.Copy).then_inc(wcur_ready, 1)

            taps_of(0)
            gates(0)
            with act.Fori(1, CT // 2) as i:
                gates(i)
                keep_sums(i - 1)
                taps_of(i)
            keep_sums(CT // 2 - 1)
            for k, (s, use, n) in enumerate([(0, USE_TAIL, HIST), (1, USE_TAIL, 4 * HIST), (0, USE_TAIL + 1, 4 * HIST)]):
                wait(act, ps_ready[s], use + 1)
                nc.scalar.activation(tails[0:n, k, :], flat(s)[0:n, :], ACT.Copy).then_inc(tail_ready, 1)
                wait(act, tail_ready, k + 1)
                act.sem_inc(ps_free[s], 1)
            wait(act, ps_ready[1], USE_ZA1 + 1)
            wait(act, consts_made, 2)
            nc.scalar.activation(th(zaT[0:RANK, 0:TOK]), ps[0:RANK, 1, :, 0:HALF], ACT.Copy).then_inc(za_ready, 1)
            wait(act, za_ready, 1)
            act.sem_inc(ps_free[1], 1)
            wait(act, ps_ready[1], USE_MEAN1 + 1)
            nc.scalar.activation(th(mean_s[:, :]), halves(1), ACT.Copy, scale=1.0 / CONV).then_inc(mean_ready, 1)
            wait(act, mean_ready, 1)
            act.sem_inc(ps_free[1], 1)
            wait(act, centered, 1)
            nc.scalar.activation(sq_ln[:, :, :], conv[:, :, :], ACT.Square).then_inc(sqln_ready, 1)
            wait(act, ps_ready[0], USE_VAR0 + 1)
            wait(act, sd_ready, 1)
            nc.scalar.activation(mean_s[:, :], mean_s[:, :], ACT.Sqrt).then_inc(sd_ready, 1)
            wait(act, lned, 1)
            for c in range(CT):
                nc.scalar.activation(conv[:, c, :], conv[:, c, :], ACT.Identity, scale=gln[:, c:c + 1],
                                     bias=bln[:, c:c + 1]).then_inc(affined, 1)
            wait(act, affined, CT)
            nc.scalar.activation(sq_ln[:, :, :], conv[:, :, :], ACT.Tanh, scale=0.5).then_inc(tanhed, 1)

            wait(act, spilled, 16)
            wait(act, tail_stored, 48)
            total = step.base + step.n
            step.base, step.n = total, 0
            with act.Fori(0, HEADS) as h:
                step.enter(h, 2 * 2)
                u = head(h)
                parts = ((0, lg[:, 0:NT, :].rearrange("p t d -> p (t d)"), z_ps[:, 0:NT * DK]),
                         (1, lg[0:NS, NT, :], z_ps[0:NS, NT * DK:TT * DK]))
                wait(act, b_ready, 2 * h + 1)
                for s, dst, src in parts:
                    wait(act, z_ready, 2 * h + s + 1)
                    step(nc.scalar.activation(dst, src, ACT.Abs))
                    step(nc.scalar.activation(dst, dst, ACT.Exp, scale=-1.0))
                    nc.scalar.activation(dst, dst, ACT.Ln, bias=1.0).then_inc(lgabs_ready, 1)
                wait(act, factors_ready, TT * h + 1)
                wait(act, scores_ready, TT * h + 1)
                for s in range(2):
                    wait(act, ps_ready[s], u + 2)
                    nc.scalar.activation(th(kT[:, s, :]), halves(s), ACT.Copy).then_inc(k_ready, 1)
                    wait(act, k_ready, 2 * h + s + 1)
                    act.sem_inc(ps_free[s], 1)
                for s in range(2):
                    wait(act, ps_ready[s], u + 3)
                    nc.scalar.activation(th(qT[:, s, :]), halves(s), ACT.Copy, scale=DK ** -0.5).then_inc(q_ready, 1)
                    wait(act, q_ready, 2 * h + s + 1)
                    act.sem_inc(ps_free[s], 1)
                for s in range(2):
                    wait(act, ps_ready[s], u + 4)
                    nc.scalar.activation(bT[:, s, :], flat(s)[:, 0:TOK], ACT.Copy).then_inc(b_ready, 1)
                    wait(act, b_ready, 2 * h + s + 1 + 1)
                    act.sem_inc(ps_free[s], 1)

                def level_decays(c):
                    wait(act, earg_ready, TT * h + c + 1)
                    nc.scalar.activation(earg[:, 0:2 * NL, :, :] if c < NT else earg[:, 8:14, :, 0:NS // 2],
                                         earg[:, 0:2 * NL, :, :] if c < NT else earg[:, 8:14, :, 0:NS // 2],
                                         ACT.Exp).then_inc(exp_ready, 1)

                def decays(c):
                    n = span(c).stop - span(c).start
                    if c:
                        wait(act, o_ready, TT * h + c)
                        wait(act, kdT_ready, TT * h + c)
                        wait(act, state_ready, NT * h + c)
                    nc.scalar.activation(qe[:, :, 0:n], bT[:, :, span(c)], ACT.Exp).then_inc(exp_ready, 1)
                    if c < NT:
                        for j in range(2):
                            e = span(c).stop
                            nc.scalar.activation(kdec[:, j, :], bT[:, j, span(c)], ACT.Exp, scale=-1.0,
                                                 bias=bT[:, j, e - 1:e]).then_inc(exp_ready, 1)
                        nc.scalar.activation(dec[:, :, 0:1], bT[:, :, span(c).stop - 1:span(c).stop], ACT.Exp
                                             ).then_inc(exp_ready, 1)
                    else:
                        wait(act, kdarg_ready, h + 1)
                        nc.scalar.activation(kdec[:, :, 0:NS], kdec[:, :, 0:NS], ACT.Exp).then_inc(exp_ready, 1)
                        nc.scalar.activation(dec[:, :, :],
                                             bT[:, :, SEQ:].rearrange("p j (b t) -> p j b t", b=DEC_B)[:, :, :, DEC_S - 1],
                                             ACT.Exp).then_inc(exp_ready, 1)

                def v_keep(p):
                    wait(act, ps_ready[0], u + 5 + p)
                    nc.scalar.activation(vt[:, 0:NT, p * PAIR:(p + 1) * PAIR],
                                         flat(0).rearrange("p (t c) -> p t c", t=NT), ACT.Copy).then_inc(v_ready, 1)
                    wait(act, v_ready, 4 * h + 2 * p + 1)
                    act.sem_inc(ps_free[0], 1)
                    wait(act, ps_ready[1], u + 5 + p)
                    nc.scalar.activation(vt[0:NS, NT, p * PAIR:(p + 1) * PAIR], flat(1)[0:NS, 0:PAIR], ACT.Copy
                                         ).then_inc(v_ready, 1)
                    wait(act, v_ready, 4 * h + 2 * p + 2)
                    act.sem_inc(ps_free[1], 1)

                def kd_keep(c):
                    n = span(c).stop - span(c).start
                    wait(act, kdT_ready, TT * h + c + 1)
                    nc.scalar.activation(kd[0:n, :], pm[0:n, 3, 0:DK], ACT.Copy).then_inc(kd_ready, 1)

                def o_keep(c):
                    n = span(c).stop - span(c).start
                    wait(act, o_ready, TT * h + c + 1)
                    nc.scalar.activation(glaT[:, bass.ds(4 * h, 4), span(c)],
                                         pm[:, 2, :].rearrange("p (e t) -> p e t", e=4)[:, :, 0:n], ACT.Copy
                                         ).then_inc(o_kept, 1)

                level_decays(0)
                decays(0)
                v_keep(0)
                v_keep(1)
                for c in range(NT):
                    kd_keep(c)
                    level_decays(c + 1)
                    wait(act, ps_ready[0], u + 7 + c)
                    nc.scalar.activation(th(rs[:, c, :]), halves(0), ACT.Tanh, scale=0.5).then_inc(rtanh_ready, 1)
                    o_keep(c)
                    decays(c + 1)
                kd_keep(NT)
                wait(act, os_ready, h + 1)
                nc.scalar.activation(os_tok, pm[0:NS, 2, :], ACT.Copy).then_inc(os_kept, 1)
                o_keep(NT)
                wait(act, o_kept, TT * h + TT + 1)
                wait(act, ps_ready[1], u + 14)
                nc.scalar.activation(sq[:, :, :], glaT[:, bass.ds(4 * h, 4), :], ACT.Square).then_inc(osq_ready, 1)
                for s in range(2):
                    wait(act, ps_ready[s], u + 15)
                    nc.scalar.activation(rms[:, s * HALF:(s + 1) * HALF], ps[:, s, 0, 0:HALF], ACT.Copy,
                                         scale=1.0 / DV, bias=EPS).then_inc(rms_done, 1)
                    wait(act, rms_done, 3 * h + s + 1)
                    act.sem_inc(ps_free[s], 1)
                nc.scalar.activation(rms[:, :], rms[:, :], ACT.Sqrt).then_inc(rms_done, 1)
            step.leave(HEADS)
            wait(act, gla_ready, 4 * HEADS)
            wait(act, stores_done, HEADS + 1)
            with act.Fori(0, D // PAIR) as i:
                for n, (dst, ready, used) in enumerate(((gsigB, gateB_ready, mergedB_ready),
                                                        (gsigA, gateA_ready, part_ready))):
                    wait(act, used, 2 * i + 1)
                    for j in range(2):
                        wait(act, ps_ready[j], USE_GATE + 4 * i + 2 * n + 1)
                        nc.scalar.activation(th(dst[:, j, :]), halves(j), ACT.Tanh, scale=0.5).then_inc(ready, 1)
                        wait(act, ready, 2 * i + j + 1)
                        act.sem_inc(ps_free[j], 1)
            wait(act, kkT_ready, 1)
            nc.scalar.activation(kkT[:, :, :].rearrange("p a b -> p (a b)"), pm[:, 3, 0:2 * P], ACT.Copy
                                 ).then_inc(kk_ready, 1)
            def root2(t):
                rows = P if t < NT else NS
                wait(act, ms2_ready, t + 1)
                nc.scalar.activation(small[0:rows, TT + t:TT + t + 1], small[0:rows, TT + t:TT + t + 1], ACT.Sqrt
                                     ).then_inc(rms2_ready, 1)

            wait(act, resid_ready, 16)
            for t in range(TT):
                rows = P if t < NT else NS
                if t:
                    wait(act, ss2_done, t)
                nc.scalar.activation(squares[0:rows, :], resid[0:rows, t, :], ACT.Square,
                                     accum_out=small[0:rows, t:t + 1]).then_inc(ss2_done, 1)
                if t:
                    root2(t - 1)
            root2(NT)
            for t in range(TT):
                rows = P if t < NT else NS
                for s in range(2):
                    wait(act, ps_ready[s], USE_H2 + t + 1)
                    nc.scalar.activation(normT[:, 8 * s:8 * s + 8, span(t)],
                                         flat(s).rearrange("p (k t) -> p k t", k=8)[:, :, 0:rows], ACT.Copy
                                         ).then_inc(h2T_ready, 1)
                    wait(act, h2T_ready, 2 * t + s + 1)
                    act.sem_inc(ps_free[s], 1)

            for t in range(DT):
                rows = P if t < NT - GT else NS
                for s in range(2):
                    wait(act, ps_ready[s], USE_RT + t + 1)
                    nc.scalar.activation(accT[:, 8 * s:8 * s + 8, t * P:t * P + rows],
                                         flat(s).rearrange("p (k t) -> p k t", k=8)[:, :, 0:rows], ACT.Copy
                                         ).then_inc(accT_ready, 1)
                    wait(act, accT_ready, 2 * t + s + 1)
                    act.sem_inc(ps_free[s], 1)

            def queries(i, hh):
                wait(act, keyscores_ready, UNITS * i + 1)
                for j in range(2):
                    wait(act, ps_ready[j], USE_WQ + 2 * i + hh + 1)
                    nc.scalar.activation(th(qp[:, hh, j, :]), halves(j), ACT.Copy).then_inc(qp_ready, 1)
                    wait(act, qp_ready, 4 * i + 2 * hh + j + 1)
                    act.sem_inc(ps_free[j], 1)

            def softmaxes(i, last=False):
                for unit in range(UNITS):
                    hh, t = unit // TT, unit % TT
                    rows = P if t < NT else NS
                    cols = bass.ds((2 * i + hh) * TOPK, TOPK)
                    wait(act, negmax_ready, UNITS * i + unit + 1)
                    nc.scalar.activation(gall[:, t, cols] if t < GT else seld[0:rows, t - GT, 2, cols],
                                         cs[unit % 2][0:rows, 0:TOPK], ACT.Exp,
                                         bias=cs[unit % 2][0:rows, TOPK:TOPK + 1]).then_inc(softmax_ready, 1)
                    if unit in (5, 9) and not last:
                        queries(i + 1, unit // 9)

            queries(0, 0)
            queries(0, 1)
            with act.Fori(0, PH // 2 - 1) as i:
                softmaxes(i)
            softmaxes(PH // 2 - 1, last=True)

            def keep_u(g, q):
                wait(act, tr_done, QUADS * g + q + 1)
                nc.scalar.activation(UT[:, 4 * q:4 * q + 4, :].rearrange("p n e -> p (n e)"), pm[:, 2 + q % 2, :],
                                     ACT.Copy).then_inc(ut_ready, 1)

            def square_u(g):
                wait(act, u_done, g + 1)
                wait(act, wt_ready, g)
                nc.scalar.activation(x2[:, :, :], pm[:, 0:2, 0:DN], ACT.Square, scale=float(np.sqrt(0.044715))
                                     ).then_inc(sq_ready, 1)

            def tanh_u(g):
                wait(act, arg_ready, g + 1)
                nc.scalar.activation(x2[:, :, :], x2[:, :, :], ACT.Tanh, scale=float(np.sqrt(2.0 / np.pi))
                                     ).then_inc(tanh_ready, 1)

            for q in range(QUADS):
                keep_u(0, q)
            square_u(0)
            for q in range(QUADS):
                keep_u(1, q)
            tanh_u(0)
            for t in range(DT):
                rows = P if t < NT - GT else NS
                wait(act, ps_ready[t // 2], USE_SEL + 1)
                at = 3 * (t % 2) * P
                nc.scalar.activation(selT[:, :, t * P:t * P + rows],
                                     flat(t // 2)[:, at:at + 3 * P].rearrange("p (k n) -> p k n", k=3)[:, :, 0:rows],
                                     ACT.Copy).then_inc(selT_ready, 1)
            wait(act, selT_ready, DT)
            for s in range(2):
                act.sem_inc(ps_free[s], 1)
            with act.Fori(0, DN // (SET * SETS)) as r:
                for j in range(SETS):
                    st = j // 4
                    if j % 4 == 0:
                        wait(act, stage_free, 2 * r + st + 1)
                    wait(act, ps_ready[j % 2], USE_G + 4 * r + j // 2 + 1)
                    nc.scalar.activation(stage[st][:, :, SET * (j % 4):SET * (j % 4) + SET],
                                         flat(j % 2).rearrange("p (n i) -> p i n", n=SET), ACT.Copy
                                         ).then_inc(g_staged, 1)
                    wait(act, g_staged, SETS * r + j + 1)
                    act.sem_inc(ps_free[j % 2], 1)

            def gelu(i, j, final=False):
                g = STEPS * i + j
                square_u(g)
                for q in range(QUADS):
                    if not final:
                        keep_u(g + 1, q)
                    if q == 1:
                        tanh_u(g)
                if j % 4 == 1:
                    wait(act, gelu_arg, GT * i + j // 4 + 1)
                    nc.scalar.activation(gelu_t, gelu_t, ACT.Tanh, scale=float(np.sqrt(2.0 / np.pi))
                                         ).then_inc(gelu_tanh, 1)

            for j in range(1, STEPS):
                gelu(0, j)
            with act.Fori(1, PH - 1) as i:
                for j in range(STEPS):
                    gelu(i, j)
            for j in range(STEPS):
                gelu(PH - 1, j, final=j == STEPS - 1)
            def root3(t):
                rows = P if t < NT else NS
                wait(act, ms3_ready, t + 1)
                nc.scalar.activation(small[0:rows, TT + t:TT + t + 1], small[0:rows, TT + t:TT + t + 1], ACT.Sqrt
                                     ).then_inc(rms3_ready, 1)

            wait(act, peer_done, 1)
            for t in range(TT):
                rows = P if t < NT else NS
                if t >= GT:
                    for s in range(2):
                        wait(act, ps_ready[s], USE_OUT + t - GT + 1)
                        nc.scalar.activation(resid[0:rows, t, s * D // 2:(s + 1) * D // 2], flat(s)[0:rows, :],
                                             ACT.Copy).then_inc(back_ready, 1)
                        wait(act, back_ready, 2 * (t - GT) + s + 1)
                        act.sem_inc(ps_free[s], 1)
                if t:
                    wait(act, ss3_done, t)
                nc.scalar.activation(ring[0:rows, 0, :], resid[0:rows, t, :], ACT.Square,
                                     accum_out=small[0:rows, t:t + 1]).then_inc(ss3_done, 1)
                if t:
                    root3(t - 1)
            root3(NT)

        @block.vector
        def _(dve):
            step = Chain(dve, dve_step)
            for first in (conv_done, att_ready, factors_ready, mergedB_ready, part_ready, merged_ready, routed):
                dve.sem_inc(first, 1)
            for t in range(TT):
                rows = P if t < NT else NS
                dve.wait_ge(act_step, t + 1)
                dve.tensor_scalar(small[0:rows, TT + t:TT + t + 1], small[0:rows, t:t + 1], 1.0 / D, EPS,
                                  ALU.mult, ALU.add).then_inc(ss_ready, 1)
                dve.wait_ge(rms_ready, t + 1)
                step(dve.reciprocal(small[0:rows, 2 * TT + t:2 * TT + t + 1], small[0:rows, TT + t:TT + t + 1]))
                dve.tensor_scalar(x_in[0:rows, t, :], x_in[0:rows, t, :], small[0:rows, 2 * TT + t:2 * TT + t + 1],
                                  None, ALU.mult).then_inc(x_normed, 1)
            dve.wait_ge(g1_loaded, 16)
            for t in range(TT):
                rows = P if t < NT else NS
                for s in range(2):
                    dve.wait_ge(ps_ready[s], USE_X + t + 1)
                    dve.tensor_tensor(normT[:, 8 * s:8 * s + 8, t * P:t * P + rows],
                                      flat(s).rearrange("p (k t) -> p k t", k=8)[:, :, 0:rows],
                                      g1[:, 8 * s:8 * s + 8].unsqueeze(2).to_broadcast([P, 8, rows]), ALU.mult
                                      ).then_inc(normT_ready, 1)
                    dve.wait_ge(normT_ready, 2 * t + s + 1)
                    dve.sem_inc(ps_free[s], 1)
            per = 6 + 4 * TAPS
            with dve.Fori(0, CT // 2) as i:
                uv = uext[:, :, HIST + SEQ:].rearrange("p q (b t) -> p q b t", b=DEC_B)
                b0 = SEQ - HALF
                for j in range(2):
                    dve.wait_ge(gate_ready, 2 * i + j + 1)
                    dve.wait_ge(ps_ready[j], USE_CONV + 2 * i + 2)
                    if j == 0:
                        dve.wait_ge(tails_kept, 3 * i + 1)
                        dve.wait_ge(conv_done, 4 * i + 1)
                    dve.tensor_tensor(uext[:, j, HIST:HIST + HALF], gate_s[:, j, 0:HALF], ps[:, j, 0, 0:HALF],
                                      ALU.mult).then_inc(u_ready, 1)
                    dve.tensor_tensor(uext[:, j, HIST + HALF:HIST + SEQ], gate_s[:, j, HALF:SEQ], ps[:, j, 1, 0:b0],
                                      ALU.mult).then_inc(u_ready, 1)
                    dve.tensor_tensor(uv[:, j, :, HIST:], gate_s[:, j, SEQ:].rearrange("p (b t) -> p b t", b=DEC_B),
                                      ps[:, j, 1, b0:HALF].rearrange("p (b t) -> p b t", b=DEC_B), ALU.mult
                                      ).then_inc(u_ready, 1)
                    dve.wait_ge(u_ready, 6 * i + 3 * j + 3)
                    dve.sem_inc(ps_free[j], 1)
                dve.sem_inc(gate_used, 6)
                dve.wait_ge(uext_hist, 3 * i + 3)
                dve.wait_ge(wcur_ready, i + 1)
                dve.wait_ge(conv_kept, 2 * i + 1)
                for tap in range(TAPS):
                    for q in range(4):
                        j, sample = q % 2, q // 2
                        out = acc[:, j, SEQ:].rearrange("p (b t) -> p b t", b=DEC_B) if sample else acc[:, j, 0:SEQ]
                        src = uv[:, j, :, tap:tap + DEC_S] if sample else uext[:, j, tap:tap + SEQ]
                        n = 4 * tap + q
                        if tap:
                            dve.wait_ge(dve_step, TT + i * 4 * (TAPS - 1) + n - 3)
                            ins = dve.scalar_tensor_tensor(out=out, in0=src, scalar=wcur[:, j, tap:tap + 1], in1=out,
                                                           op0=ALU.mult, op1=ALU.add)
                        else:
                            ins = dve.tensor_scalar(out, src, wcur[:, j, tap:tap + 1], None, ALU.mult)
                        ins.then_inc(conv_done if tap == TAPS - 1 else dve_step, 1)
            dve.wait_ge(mean_ready, 1)
            dve.wait_ge(conv_kept, CT + 1)
            dve.tensor_tensor(conv[:, :, :], conv[:, :, :], mean_s[:, :].unsqueeze(1).to_broadcast([P, CT, TOK]),
                              ALU.subtract).then_inc(centered, 1)
            dve.wait_ge(ps_ready[0], USE_VAR0 + 1)
            dve.wait_ge(centered, 1)
            dve.tensor_scalar(th(mean_s[:, :]), halves(0), 1.0 / CONV, EPS, ALU.mult, ALU.add).then_inc(sd_ready, 1)
            dve.wait_ge(sd_ready, 2)
            dve.sem_inc(ps_free[0], 1)
            base = TT + CT // 2 * 4 * (TAPS - 1)
            dve.reciprocal(mean_s[:, :], mean_s[:, :]).then_inc(dve_step, 1)
            dve.wait_ge(dve_step, base + 1)
            dve.tensor_tensor(conv[:, :, :], conv[:, :, :], mean_s[:, :].unsqueeze(1).to_broadcast([P, CT, TOK]),
                              ALU.mult).then_inc(lned, 1)
            dve.wait_ge(tanhed, 1)
            dve.scalar_tensor_tensor(out=conv[:, :, :], in0=sq_ln[:, :, :], scalar=1.0, in1=conv[:, :, :],
                                     op0=ALU.add, op1=ALU.mult).then_inc(silu_ready, 1)

            dve.wait_ge(spilled, 16)
            dve.wait_ge(tail_stored, 48)
            dve.wait_ge(za_ready, 1)
            dve.wait_ge(masks_made, 1)
            step.base, step.n = base + 1, 0
            with dve.Fori(0, HEADS) as h:
                step.enter(h, TT + 3 + 2)
                u = head(h)
                for s, dst, src in ((0, lg[:, 0:NT, :].rearrange("p t d -> p (t d)"), z_ps[:, 0:NT * DK]),
                                    (1, lg[0:NS, NT, :], z_ps[0:NS, NT * DK:TT * DK])):
                    dve.wait_ge(lgabs_ready, 2 * h + s + 1)
                    dve.scalar_tensor_tensor(out=dst, in0=src, scalar=0.0, in1=dst, op0=ALU.min, op1=ALU.subtract
                                             ).then_inc(lg_ready, 1)
                dve.wait_ge(b_ready, 2 * h + 2 + 1)

                def views(x, c, w):
                    g = (P if c < NT else NS) // (2 * w)
                    return x.rearrange("p j (g u w) -> p j g u w", g=g, u=2)

                def arguments(c):
                    n = span(c).stop - span(c).start
                    for l, w in levels(c):
                        bv = views(bT[:, :, span(c)], c, w)
                        piv = bv[:, :, :, 0, w - 1:w].to_broadcast([P, 2, n // (2 * w), w])
                        eq = earg[:, 2 * l, :, 0:n // 2].rearrange("p j (g w) -> p j g w", w=w)
                        ek = earg[:, 2 * l + 1, :, 0:n // 2].rearrange("p j (g w) -> p j g w", w=w)
                        dve.tensor_tensor(eq, bv[:, :, :, 1, :], piv, ALU.subtract)
                        last = dve.tensor_tensor(ek, piv, bv[:, :, :, 0, :], ALU.subtract)
                    last.then_inc(earg_ready, 1)
                    if c == NT:
                        dve.wait_ge(kdT_ready, TT * h + c)
                        bb = bT[:, :, SEQ:].rearrange("p j (b t) -> p j b t", b=DEC_B)
                        dve.tensor_tensor(kdec[:, :, 0:NS].rearrange("p j (b t) -> p j b t", b=DEC_B),
                                          bb[:, :, :, DEC_S - 1:DEC_S].to_broadcast([P, 2, DEC_B, DEC_S]), bb,
                                          ALU.subtract).then_inc(kdarg_ready, 1)

                def factors(c):
                    n = span(c).stop - span(c).start
                    e = 5 * NT * h + 4 * h + 5 * c
                    dve.wait_ge(scores_ready, TT * h + c + 1)
                    dve.wait_ge(exp_ready, e + 1)
                    for l, w in levels(c):
                        eq = earg[:, 2 * l, :, 0:n // 2].rearrange("p j (g w) -> p j g w", w=w)
                        ek = earg[:, 2 * l + 1, :, 0:n // 2].rearrange("p j (g w) -> p j g w", w=w)
                        dve.tensor_tensor(views(qf[:, l, :, 0:n], c, w)[:, :, :, 1, :], eq,
                                          views(qT[:, :, span(c)], c, w)[:, :, :, 1, :], ALU.mult)
                        last = dve.tensor_tensor(views(kf[:, l, :, 0:n], c, w)[:, :, :, 0, :], ek,
                                                 views(kT[:, :, span(c)], c, w)[:, :, :, 0, :], ALU.mult)
                    last.then_inc(factors_ready, 1)

                def scaled(c):
                    n = span(c).stop - span(c).start
                    e = 5 * NT * h + 4 * h + 5 * c
                    dve.wait_ge(exp_ready, e + (5 if c < NT else 4))
                    if c < NT:
                        dve.tensor_tensor(qe[:, :, 0:n], qe[:, :, 0:n], qT[:, :, span(c)], ALU.mult)
                    else:
                        far = (DEC_B - 1) * DEC_S
                        dve.tensor_tensor(
                            qs[:, :, 0:(DEC_B - 1) * (NS + DEC_S)].rearrange(
                                "p j (b t) -> p j b t", b=DEC_B - 1)[:, :, :, 0:DEC_S],
                            qe[:, :, 0:far].rearrange("p j (b t) -> p j b t", t=DEC_S),
                            qT[:, :, SEQ:SEQ + far].rearrange("p j (b t) -> p j b t", t=DEC_S), ALU.mult)
                        dve.tensor_tensor(qs[:, :, DEC_B * NS - DEC_S:], qe[:, :, far:NS], qT[:, :, SEQ + far:],
                                          ALU.mult)
                    dve.tensor_tensor(kdec[:, :, 0:n], kdec[:, :, 0:n], kT[:, :, span(c)], ALU.mult
                                      ).then_inc(decay_ready, 1)

                def attention(c):
                    n = span(c).stop - span(c).start
                    lo = levels(c)[0][0]
                    sc = pm[:, 0:2, :].rearrange("p b (l t) -> p (b l) t", t=P)
                    dve.wait_ge(scores_ready, TT * h + c + 1 + 1)
                    dve.wait_ge(factors_ready, TT * h + c + 1 + 1)
                    step(dve.tensor_tensor(masked[0:n, lo:NL + 1, 0:n], sc[0:n, lo:NL + 1, 0:n],
                                           mask[0:n, lo:NL + 1, 0:n], ALU.mult))
                    if c:
                        dve.wait_ge(o_ready, TT * h + c)
                    dve.tensor_reduce(att[0:n, 0:n], masked[0:n, lo:NL + 1, 0:n].rearrange("p l t -> p t l"), AX.X,
                                      ALU.add).then_inc(att_ready, 1)
                    dve.wait_ge(att_ready, TT * h + c + 1 + 1)

                dve.wait_ge(q_ready, 2 * h + 2)
                dve.wait_ge(k_ready, 2 * h + 2)
                arguments(0)
                factors(0)
                scaled(0)
                for c in range(NT):
                    attention(c)
                    arguments(c + 1)
                    factors(c + 1)
                    dve.wait_ge(rtanh_ready, 4 * h + c + 1)
                    dve.scalar_tensor_tensor(out=th(rs[:, c, :]), in0=th(rs[:, c, :]), scalar=1.0, in1=halves(0),
                                             op0=ALU.add, op1=ALU.mult).then_inc(rsilu_ready, 1)
                    dve.wait_ge(rsilu_ready, 4 * h + c + 1)
                    dve.sem_inc(ps_free[0], 1)
                    dve.wait_ge(ps_ready[1], u + 7 + c)
                    if c == 0:
                        dve.wait_ge(stores_done, h + 1)
                        dve.tensor_copy(state[:, :, :], ps[:, 1, :, :]).then_inc(state_ready, 1)
                    else:
                        step(dve.scalar_tensor_tensor(out=state[:, 0, :], in0=state[:, 0, :], scalar=dec[:, 0, 0:1],
                                                      in1=ps[:, 1, 0, :], op0=ALU.mult, op1=ALU.add))
                        dve.scalar_tensor_tensor(out=state[:, 1, :], in0=state[:, 1, :], scalar=dec[:, 1, 0:1],
                                                 in1=ps[:, 1, 1, :], op0=ALU.mult, op1=ALU.add
                                                 ).then_inc(state_ready, 1)
                    dve.wait_ge(state_ready, NT * h + c + 1)
                    dve.sem_inc(ps_free[1], 1)
                    scaled(c + 1)
                attention(NT)
                dve.wait_ge(kd_ready, TT * h + TT + 1)
                for b in range(DEC_B):
                    if b >= 2:
                        dve.wait_ge(ps_ready[b % 2], u + 10 + b // 2)
                    dve.tensor_scalar(kdm[0:NS, b % 2, :], kd[0:NS, :], bmask[:, b:b + 1], None, ALU.mult
                                      ).then_inc(kdm_ready, 1)
                    dve.wait_ge(ps_ready[b % 2], u + 11 + b // 2)
                    for j in range(2):
                        dve.scalar_tensor_tensor(out=sring[:, b % 4, j, :], in0=sring[:, b % 4, j, :],
                                                 scalar=dec[:, j, b:b + 1], in1=ps[:, b % 2, j, :], op0=ALU.mult,
                                                 op1=ALU.add).then_inc(st_updated, 1)
                    dve.wait_ge(st_updated, 2 * DEC_B * h + 2 * b + 2)
                    dve.sem_inc(ps_free[b % 2], 1)
                dve.wait_ge(rms_done, 3 * h + 3)
                step(dve.reciprocal(rms[:, :], rms[:, :]))
                step(dve.tensor_tensor(rs[:, :, :], rs[:, :, :], rms[:, :].unsqueeze(1).to_broadcast([P, 4, TOK]),
                                       ALU.mult))
                for e in range(4):
                    dve.scalar_tensor_tensor(out=glaT[:, bass.ds(4 * h + e, 1), :].rearrange("p a t -> p (a t)"),
                                             in0=glaT[:, bass.ds(4 * h + e, 1), :].rearrange("p a t -> p (a t)"),
                                             scalar=ggla[:, bass.ds(4 * h + e, 1)], in1=rs[:, e, :],
                                             op0=ALU.mult, op1=ALU.mult).then_inc(gla_ready, 1)
                dve.wait_ge(gla_ready, 4 * h + 4)
            step.leave(HEADS)
            dve.wait_ge(stores_done, HEADS + 1)
            with dve.Fori(0, D // PAIR) as i:
                for n, (gate, ready, done) in enumerate(((gsigB, gateB_ready, mergedB_ready),
                                                         (gsigA, gateA_ready, part_ready))):
                    if n:
                        dve.wait_ge(merged_ready, i + 1)
                    for j in range(2):
                        dve.wait_ge(ready, 2 * i + j + 1)
                        dve.wait_ge(ps_ready[j], USE_GATE + 4 * i + 2 * n + 2)
                        dst = th(part[:, j, :]) if n else merged[:, bass.ds(2 * i + j, 1), :].rearrange(
                            "p a (b n) -> p (a b) n", b=2)
                        dve.scalar_tensor_tensor(out=dst, in0=th(gate[:, j, :]), scalar=1.0, in1=halves(j),
                                                 op0=ALU.add, op1=ALU.mult).then_inc(done, 1)
                        dve.wait_ge(done, 2 * i + j + 1 + 1)
                        dve.sem_inc(ps_free[j], 1)
                dve.tensor_tensor(merged[:, bass.ds(2 * i, 2), :], merged[:, bass.ds(2 * i, 2), :], part[:, :, :],
                                  ALU.add).then_inc(merged_ready, 1)
            dve.wait_ge(resid_loaded, 32)
            with dve.Fori(0, D // PAIR) as i:
                for s, rows, dst, src in ((0, P, resid[:, 0:NT, bass.ds(i * PAIR, PAIR)],
                                           flat(0).rearrange("p (t c) -> p t c", t=NT)),
                                          (1, NS, resid[0:NS, NT, bass.ds(i * PAIR, PAIR)], flat(1)[0:NS, 0:PAIR])):
                    dve.wait_ge(ps_ready[s], USE_MIX + i + 1)
                    dve.scalar_tensor_tensor(out=dst, in0=src, scalar=0.25, in1=dst, op0=ALU.mult, op1=ALU.add
                                             ).then_inc(resid_ready, 1)
                    dve.wait_ge(resid_ready, 2 * i + s + 1)
                    dve.sem_inc(ps_free[s], 1)
            dve.wait_ge(g2_loaded, 16)
            def norm2(t):
                rows = P if t < NT else NS
                dve.wait_ge(rms2_ready, t + 1)
                step(dve.reciprocal(small[0:rows, 2 * TT + t:2 * TT + t + 1], small[0:rows, TT + t:TT + t + 1]))
                dve.scalar_tensor_tensor(out=h2[0:rows, t, :], in0=resid[0:rows, t, :],
                                         scalar=small[0:rows, 2 * TT + t:2 * TT + t + 1], in1=g2[0:rows, :],
                                         op0=ALU.mult, op1=ALU.mult).then_inc(h2_ready, 1)

            for t in range(TT):
                rows = P if t < NT else NS
                dve.wait_ge(ss2_done, t + 1)
                dve.tensor_scalar(small[0:rows, TT + t:TT + t + 1], small[0:rows, t:t + 1], 1.0 / D, EPS,
                                  ALU.mult, ALU.add).then_inc(ms2_ready, 1)
                if t:
                    norm2(t - 1)
            norm2(NT)
            dve.wait_ge(h2_ready, TT)
            dve.wait_ge(kk_ready, 1)

            def route(i, pair):
                units = [(b, 2 * pair + b, P if (2 * pair + b) % TT < NT else NS) for b in range(2)]
                scores = [key_scores(u, n) for _, u, n in units]

                def each(op, before=1):
                    for b, u, n in units:
                        step.wait(1 if b else before)
                        step.mark(op(b, n))

                def each_half(op, first=False):
                    for b, u, n in units:
                        if not first:
                            step.wait(2)
                        for a_ in range(2):
                            step.mark(op(b, n, a_))

                def cands(b, n):
                    return cand[b][0:n, :, :].rearrange("p a b -> p (a b)")

                wait(dve, keyscores_ready, UNITS * i + 2 * pair + 2 + 1)
                each_half(lambda b, n, a_: dve.max(v12[b][0:n, a_, 0:8], scores[b][:, a_, :]), first=True)
                each_half(lambda b, n, a_: dve.max_index(i12[0:n, b, a_, 0:8], v12[b][0:n, a_, 0:8],
                                                         scores[b][:, a_, :]))
                each_half(lambda b, n, a_: dve.match_replace(sc2[b][0:n, a_, :], v12[b][0:n, a_, 0:8],
                                                             scores[b][:, a_, :], NEG))
                each_half(lambda b, n, a_: dve.max(v12[b][0:n, a_, 8:16], sc2[b][0:n, a_, :]))
                each_half(lambda b, n, a_: dve.max_index(i12[0:n, b, a_, 8:16], v12[b][0:n, a_, 8:16],
                                                         sc2[b][0:n, a_, :]))
                each(lambda b, n: dve.tensor_tensor(
                    cand[b][0:n, :, :], v12[b][0:n, 0, :].unsqueeze(2).to_broadcast([n, TOPK, TOPK]),
                    v12[b][0:n, 1, :].unsqueeze(1).to_broadcast([n, TOPK, TOPK]), ALU.add), before=2)
                wait(dve, softmax_ready, UNITS * i + 2 * pair + 1)
                each(lambda b, n: dve.max(cs[b][0:n, 0:8], cands(b, n)))
                each(lambda b, n: dve.max_index(ci[0:n, b, 0:8], cs[b][0:n, 0:8], cands(b, n)))
                each(lambda b, n: dve.match_replace(cand2[b][0:n, :], cs[b][0:n, 0:8], cands(b, n), NEG))
                each(lambda b, n: dve.max(cs[b][0:n, 8:16], cand2[b][0:n, :]))
                for b, _, n in units:
                    dve.tensor_scalar(cs[b][0:n, TOPK:TOPK + 1], cs[b][0:n, 0:1], -1.0, None, ALU.mult
                                      ).then_inc(negmax_ready, 1)
                each(lambda b, n: dve.max_index(ci[0:n, b, 8:16], cs[b][0:n, 8:16], cand2[b][0:n, :]))
                for b, _, n in units:
                    step.wait(3 if b else 1)
                    step.mark(dve.tensor_copy(i12f[b][0:n, :, :], i12[0:n, b, :, :]))
                    step.mark(dve.tensor_scalar(abi[0:n, b, 0, :], ci[0:n, b, :], 4, None, ALU.logical_shift_right))
                    step.mark(dve.tensor_scalar(abi[0:n, b, 1, :], ci[0:n, b, :], TOPK - 1, None, ALU.bitwise_and))
                each(lambda b, n: dve.tensor_copy(ab[b][0:n, :, :], abi[0:n, b, :, :]), before=3)
                each(lambda b, n: dve.tensor_tensor(
                    oh[b][0:n, :, :, :], ab[b][0:n, :, :].unsqueeze(3).to_broadcast([n, 2, TOPK, TOPK]),
                    iota16[0:n, :].unsqueeze(1).unsqueeze(1).to_broadcast([n, 2, TOPK, TOPK]), ALU.is_equal))
                each(lambda b, n: dve.tensor_tensor(
                    oh[b][0:n, :, :, :], oh[b][0:n, :, :, :],
                    i12f[b][0:n, :, :].unsqueeze(2).to_broadcast([n, 2, TOPK, TOPK]), ALU.mult))
                each(lambda b, n: dve.tensor_reduce(esel[b][0:n, :, :], oh[b][0:n, :, :, :], AX.X, ALU.add))
                for b, u, n in units:
                    step.wait(1 - b)
                    t = u % TT
                    cols = bass.ds((2 * i + u // TT) * TOPK, TOPK)
                    if t < GT:
                        dve.scalar_tensor_tensor(out=idxs[:, t, cols], in0=esel[b][:, 0, :], scalar=float(NKEY),
                                                 in1=esel[b][:, 1, :], op0=ALU.mult, op1=ALU.add).then_inc(routed, 1)
                    else:
                        dve.tensor_tensor(seld[0:n, t - GT, 0:2, cols], esel[b][0:n, :, :],
                                          ones[0:n, 0:2 * TOPK].rearrange("p (a k) -> p a k", a=2), ALU.mult
                                          ).then_inc(routed, 1)
                wait(dve, routed, UNITS * i + 2 * pair + 2 + 1)

            with dve.Fori(0, PH // 2) as i:
                step.enter(i, (5 * 4 + 6 * 2 + 6 + 4 * 2) * (UNITS // 2))
                for pair in range(UNITS // 2):
                    route(i, pair)
            step.leave(PH // 2)
            wait(dve, softmax_ready, UNITS * PH // 2 + 1)
            for t in range(TT):
                n = P if t < NT else NS
                gates = (gall[:, t, :] if t < GT else seld[0:n, t - GT, 2, :]).rearrange("p (h k) -> p h k", h=PH)
                step(dve.tensor_reduce(gsum[0:n, :], gates, AX.X, ALU.add))
                step(dve.reciprocal(gsum[0:n, :], gsum[0:n, :]))
                step(dve.tensor_scalar(gsum[0:n, :], gsum[0:n, :], 0.5, None, ALU.mult))
                last = dve.tensor_tensor(gates, gates, gsum[0:n, :].unsqueeze(2).to_broadcast([n, PH, TOPK]), ALU.mult)
                if t < GT:
                    step(last)
                else:
                    last.then_inc(sel_ready, 1)
                    wait(dve, sel_ready, t - GT + 1)
            def argument(g):
                dve.wait_ge(sq_ready, g + 1)
                dve.scalar_tensor_tensor(out=x2[:, :, :], in0=x2[:, :, :], scalar=1.0, in1=pm[:, 0:2, 0:DN],
                                         op0=ALU.add, op1=ALU.mult).then_inc(arg_ready, 1)

            def one_tanh_x(g):
                dve.wait_ge(tanh_ready, g + 1)
                dve.scalar_tensor_tensor(out=x2[:, :, :], in0=x2[:, :, :], scalar=1.0, in1=pm[:, 0:2, 0:DN],
                                         op0=ALU.add, op1=ALU.mult).then_inc(x1_ready, 1)

            argument(0)
            one_tanh_x(0)
            wait(dve, iota_ready, 1)
            wait(dve, selT_ready, DT)
            with dve.Fori(0, DN // (SET * SETS)) as r:
                for half in range(2 * SETS):
                    j = half // 2
                    if half % 2 == 0:
                        wait(dve, ps_ready[j % 2], USE_G + 4 * r + j // 2)
                    dve.tensor_tensor(ohs[:, half % 4, :, :, :],
                                      iota128.unsqueeze(1).unsqueeze(1).to_broadcast([P, 2, SET // 2, P]),
                                      selT[:, 0:2, bass.ds(SET * SETS * r + SET // 2 * half, SET // 2)].unsqueeze(
                                          3).to_broadcast([P, 2, SET // 2, P]), ALU.is_equal).then_inc(onehot_ready, 1)
            wait(dve, onehot_ready, 2 * DN // SET)
            wait(dve, stage_free, NST + 2)
            dve.sem_inc(rows_used, RING)

            def gathered(i, j, r):
                m = PER * j + r
                t, k = m // (2 * TOPK), m % (2 * TOPK)
                tile = ring[:, m % RING, :]
                if k < TOPK:
                    dve.wait_ge(rows_loaded[m % RING], 16 * (ROWS // RING) * i + 16 * (m // RING) + 16)
                    dve.tensor_tensor_reduce(out=tile, in0=tile, in1=h2[:, t, :], scale=1.0, scalar=0.0,
                                             op0=ALU.mult, op1=ALU.add, accum_out=hidden[:, k:k + 1]
                                             ).then_inc(rows_used, 1)
                else:
                    wait(dve, rows_used, ROWS * i + m + RING)
                    dve.wait_ge(rows_loaded[m % RING], 16 * (ROWS // RING) * i + 16 * (m // RING) + 16)
                    dve.scalar_tensor_tensor(out=resid[:, t, :], in0=tile, scalar=wexp[:, k - TOPK:k - TOPK + 1],
                                             in1=resid[:, t, :], op0=ALU.mult, op1=ALU.add).then_inc(rows_used, 1)

            def add_v(g, q):
                dve.wait_ge(ps_ready[q % 2], USE_V + 4 * g + q // 2 + 1)
                dve.tensor_tensor(accT[:, 2 * q:2 * q + 2, :], ps[:, q % 2, :, 0:DN], accT[:, 2 * q:2 * q + 2, :],
                                  ALU.add).then_inc(ps_free[q % 2], 1)

            def weights(i, j, first=False):
                g = STEPS * i + j

                def add(*qs):
                    for q in qs:
                        if not first:
                            add_v(g - 1, q)

                def gather_most():
                    for r in range(PER - 1):
                        gathered(i, j, r)

                if not first:
                    gather_most()
                add(0)
                if not first:
                    argument(g)
                add(1, 2)
                if not first:
                    one_tanh_x(g)
                add(3)
                wait(dve, x1_ready, g + 1)
                dve.wait_ge(gt_loaded[j % 2], 16 * (STEPS // 2) * i + 16 * (j // 2) + 16)
                dve.tensor_tensor(WT[:, j % 2, :, :].rearrange("p b (t n) -> p b t n", t=NST),
                                  x2[:, :, :].rearrange("p b (t n) -> p b t n", t=NST),
                                  gT[:, j % 2, :, :].rearrange("p t (b n) -> p b t n", b=2), ALU.mult
                                  ).then_inc(wt_ready, 1)
                if first:
                    gather_most()
                gathered(i, j, PER - 1)
                tile = GT * i + j // 4
                if j % 4 == 1:
                    dve.wait_ge(rows_used, ROWS * i + PER * (j + 1) + RING)
                    step(dve.tensor_tensor(gelu_t, hidden, hidden, ALU.mult))
                    step(dve.tensor_scalar(gelu_t, gelu_t, 0.044715, 1.0, ALU.mult, ALU.add))
                    dve.tensor_tensor(gelu_t, gelu_t, hidden, ALU.mult).then_inc(gelu_arg, 1)
                add(4, 5, 6, 7)
                if j % 4 == 1:
                    dve.wait_ge(gelu_tanh, tile + 1)
                    step(dve.scalar_tensor_tensor(out=wexp, in0=gelu_t, scalar=1.0, in1=hidden,
                                                  op0=ALU.add, op1=ALU.mult))
                    step(dve.tensor_tensor(wexp, wexp, gall[:, j // 4, bass.ds(i * TOPK, TOPK)], ALU.mult))

            for j in range(STEPS):
                weights(0, j, first=j == 0)
            with dve.Fori(1, PH - 1) as i:
                step.enter(i, 4 * GT, 1)
                for j in range(STEPS):
                    weights(i, j)
            step.leave(PH - 2)
            for j in range(STEPS):
                weights(PH - 1, j)
            for q in range(QUADS):
                add_v(NG - 1, q)
            dve.wait_ge(rows_used, ROWS * PH + RING)
            dve.sem_inc(peer_done, 1)
            dve.wait_ge(fg_loaded, 16)

            def norm3(t):
                rows = P if t < NT else NS
                dve.wait_ge(rms3_ready, t + 1)
                step(dve.reciprocal(small[0:rows, 2 * TT + t:2 * TT + t + 1], small[0:rows, TT + t:TT + t + 1]))
                dve.scalar_tensor_tensor(out=resid[0:rows, t, :], in0=resid[0:rows, t, :],
                                         scalar=small[0:rows, 2 * TT + t:2 * TT + t + 1], in1=final_g[0:rows, :],
                                         op0=ALU.mult, op1=ALU.mult).then_inc(y_ready, 1)

            for t in range(TT):
                rows = P if t < NT else NS
                dve.wait_ge(ss3_done, t + 1)
                dve.tensor_scalar(small[0:rows, TT + t:TT + t + 1], small[0:rows, t:t + 1], 1.0 / D, EPS,
                                  ALU.mult, ALU.add).then_inc(ms3_ready, 1)
                if t:
                    norm3(t - 1)
            norm3(NT)


_INS = ['x_prompt', 'x_sample', 'state_conv', 'state_gla', 'norm1_g', 'w_in', 'w_a2', 'b_a', 'w_dw', 'b_dw',
        'conv_ln_g', 'conv_ln_b', 'w_conv_out', 'gla_norm_g', 'w_gla_o', 'w_mix_out', 'norm2_g', 'peer_wq',
        'peer_k1', 'peer_k2', 'peer_u', 'peer_v', 'final_g']
_OUTS = [(1, 512, 2048), (8, 8, 2048), (1, 1, 30, 1024), (1, 1, 4, 256, 512), (1, 8, 30, 1024), (1, 8, 4, 256, 512)]


def kernel(**inputs):
    import numpy as _np
    import concourse.bacc as _bacc
    from concourse import mybir as _mybir
    from concourse.bass_utils import run_bass_kernel_spmd as _run

    nc = _bacc.Bacc("TRN2", target_bir_lowering=False, num_devices=1)
    arrays, ins = {}, {}
    for name in _INS:
        x = _np.ascontiguousarray(inputs[name])
        arrays[f"in_{name}"] = x
        ins[name] = nc.dram_tensor(f"in_{name}", x.shape, _mybir.dt.from_np(x.dtype), kind="ExternalInput").ap()
    outs = [nc.dram_tensor(f"out_{i}", s, _mybir.dt.float32, kind="ExternalOutput").ap() for i, s in enumerate(_OUTS)]
    trunk(nc, ins, outs)
    r = _run(nc, [arrays], core_ids=[0])
    return tuple(r.results[0][f"out_{i}"] for i in range(len(_OUTS)))
```
